# Optimizing a Trainium2 kernel written in Bass

```python
import math
import jax, jax.numpy as jnp
from jax import lax
import numpy as np

D_MODEL = 1024
BATCH = 1
SEQ = 256
DEPTH = 2
DEC_BATCH = 8
DEC_SEQ = 4
PAST_LEN = 2048
PAGE_SIZE = 128

N_A_LAYERS = (DEPTH + 1) // 2
N_C_LAYERS = DEPTH // 2

HA_HEADS = 4
HA_DK = 128
HA_DV = 128
HA_FDIM = HA_HEADS * HA_DK
HA_WIDTH = HA_HEADS * HA_DV
SC_WIDTH = D_MODEL - HA_WIDTH
SC_KERNEL = 3
EVEN_IN = 2 * HA_FDIM + 2 * HA_WIDTH + 3 * SC_WIDTH
EVEN_SPLITS = (HA_FDIM, 2 * HA_FDIM, 2 * HA_FDIM + HA_WIDTH, 2 * HA_FDIM + 2 * HA_WIDTH,
               2 * HA_FDIM + 2 * HA_WIDTH + SC_WIDTH, 2 * HA_FDIM + 2 * HA_WIDTH + 2 * SC_WIDTH)
GLA_HEADS = 4
GLA_KEY = D_MODEL // 2
GLA_VAL = D_MODEL
GLA_DK = GLA_KEY // GLA_HEADS
GLA_DV = GLA_VAL // GLA_HEADS
GLA_RANK = 16
GLA_NORMALIZER = 16.0
ODD_IN = 2 * GLA_KEY + 2 * GLA_VAL + GLA_RANK
ODD_SPLITS = (GLA_KEY, 2 * GLA_KEY, 2 * GLA_KEY + GLA_VAL, 2 * GLA_KEY + 2 * GLA_VAL)
MEM_LEN = 256
MEM_HEADS = 4
MEM_HD = D_MODEL // MEM_HEADS
N_GROUPS = 4
EXP_PER_GROUP = 8
TOP_K = 2
D_EXPERT = 512
CHUNK = 64
LN_EPS = 1e-5
RMS_EPS = 1e-6
DN_ALPHA = (2.0 * DEPTH) ** 0.25
DN_BETA = (8.0 * DEPTH) ** -0.25

kernel_name = "hgrn2_conv_gla_memxattn_hmoe_step"

def layer_norm(x, g, b):
    xf = x.astype(jnp.float32)
    mu = jnp.mean(xf, axis=-1, keepdims=True)
    var = jnp.mean(jnp.square(xf - mu), axis=-1, keepdims=True)
    y = (xf - mu) * lax.rsqrt(var + LN_EPS)
    return (y * g.astype(jnp.float32) + b.astype(jnp.float32)).astype(x.dtype)

def rms_norm_swish_gate(o, w, gate):
    of = o.astype(jnp.float32)
    y = of * lax.rsqrt(jnp.mean(of * of, axis=-1, keepdims=True) + RMS_EPS) * w.astype(jnp.float32)
    return (y * jax.nn.silu(gate.astype(jnp.float32))).astype(gate.dtype)

def gated_linear_recurrence(q, k, v, log_a, s0):
    f32 = jnp.float32
    bsz, T, H, _ = q.shape
    dv = v.shape[-1]
    c = min(CHUNK, T)
    n = -(-T // c)
    pad = n * c - T

    def to_chunks(t):
        t = jnp.pad(t.astype(f32), ((0, 0), (0, pad), (0, 0), (0, 0)))
        return t.reshape(bsz, n, c, H, t.shape[-1]).transpose(1, 0, 3, 2, 4)

    causal = jnp.tril(jnp.ones((c, c), dtype=bool))[:, :, None]

    def step(S, blk):
        qb, kb, vb, ab = blk
        b = jnp.cumsum(ab, axis=2)
        diff = b[:, :, :, None, :] - b[:, :, None, :, :]
        decay = jnp.exp(jnp.where(causal, diff, -jnp.inf))
        scores = jnp.einsum('bhtd,bhsd,bhtsd->bhts', qb, kb, decay)
        o = (jnp.einsum('bhts,bhsv->bhtv', scores, vb)
             + jnp.einsum('bhtd,bhdv->bhtv', qb * jnp.exp(b), S))
        b_last = b[:, :, -1:, :]
        S = (jnp.exp(b_last[:, :, 0, :])[..., None] * S
             + jnp.einsum('bhsd,bhsv->bhdv', kb * jnp.exp(b_last - b), vb))
        return S, o

    S, o = lax.scan(step, s0.astype(f32), (to_chunks(q), to_chunks(k), to_chunks(v), to_chunks(log_a)))
    o = o.transpose(1, 0, 3, 2, 4).reshape(bsz, n * c, H, dv)[:, :T]
    return o, S

def hgrn2_mix(q, f, i, g, lb, norm_w, s0):
    bsz, T, _ = q.shape
    z = f.astype(jnp.float32)
    log_f = jnp.logaddexp(jnp.log(lb), jnp.log1p(-lb) + jax.nn.log_sigmoid(z))
    k = (1.0 - lb) * jax.nn.sigmoid(-z)
    qa = jax.nn.silu(q.astype(jnp.float32))
    o, s = gated_linear_recurrence(qa.reshape(bsz, T, HA_HEADS, HA_DK),
                                   k.reshape(bsz, T, HA_HEADS, HA_DK),
                                   i.reshape(bsz, T, HA_HEADS, HA_DV),
                                   log_f.reshape(bsz, T, HA_HEADS, HA_DK), s0)
    o = rms_norm_swish_gate(o, norm_w, g.reshape(bsz, T, HA_HEADS, HA_DV))
    return o.reshape(bsz, T, HA_WIDTH), s

def short_conv_mix(b_gate, c_gate, h, w, buf):
    u = c_gate * h
    ext = jnp.concatenate([buf.astype(u.dtype), u], axis=1)
    T = u.shape[1]
    y = ext[:, 0:T] * w[:, 0]
    for j in range(1, SC_KERNEL):
        y = y + ext[:, j:j + T] * w[:, j]
    return b_gate * y, ext[:, T:]

def gla_mix(q, k, v, g, gz, w_gk2, b_gk2, norm_w, s0):
    bsz, T, _ = q.shape
    log_a = jax.nn.log_sigmoid((gz @ w_gk2 + b_gk2).astype(jnp.float32)) / GLA_NORMALIZER
    qs = q.astype(jnp.float32) * (GLA_DK ** -0.5)
    o, s = gated_linear_recurrence(qs.reshape(bsz, T, GLA_HEADS, GLA_DK),
                                   k.reshape(bsz, T, GLA_HEADS, GLA_DK),
                                   v.reshape(bsz, T, GLA_HEADS, GLA_DV),
                                   log_a.reshape(bsz, T, GLA_HEADS, GLA_DK), s0)
    o = rms_norm_swish_gate(o, norm_w, g.reshape(bsz, T, GLA_HEADS, GLA_DV))
    return o.reshape(bsz, T, GLA_VAL), s

def memory_attention(x, mem_k, mem_v, w_mq, w_mo):
    bsz, T, _ = x.shape
    q = (x @ w_mq).reshape(bsz, T, MEM_HEADS, MEM_HD)
    s = jnp.einsum('bthd,bmhd->bhtm', q, mem_k).astype(jnp.float32) * (MEM_HD ** -0.5)
    p = jax.nn.softmax(s, axis=-1).astype(mem_v.dtype)
    o = jnp.einsum('bhtm,bmhd->bthd', p, mem_v).reshape(bsz, T, MEM_HEADS * MEM_HD)
    return o @ w_mo

def hier_moe(x, w_grp, b_grp, w_er, b_er, w_gate, w_up, w_down):
    bsz, T, D = x.shape
    xt = x.reshape(bsz * T, D)
    grp_logits = (xt @ w_grp + b_grp).astype(jnp.float32)
    grp_prob = jax.nn.softmax(grp_logits, axis=-1)
    g_sel = jnp.argmax(grp_logits, axis=-1)
    g_w = jnp.take_along_axis(grp_prob, g_sel[:, None], axis=-1)
    e_logits = (jnp.einsum('nd,gde->nge', xt, w_er) + b_er).astype(jnp.float32)
    e_logits = jnp.take_along_axis(e_logits, g_sel[:, None, None], axis=1)[:, 0]
    top_v, top_i = lax.top_k(e_logits, TOP_K)
    top_w = jax.nn.softmax(top_v, axis=-1) * g_w
    e_w = jnp.sum(jax.nn.one_hot(top_i, EXP_PER_GROUP, dtype=jnp.float32) * top_w[..., None], axis=1)
    combine = (jax.nn.one_hot(g_sel, N_GROUPS, dtype=jnp.float32)[:, :, None]
               * e_w[:, None, :]).astype(x.dtype)
    out = jnp.zeros_like(xt)
    for gi in range(N_GROUPS):
        hid = (jax.nn.silu(jnp.einsum('nd,edf->nef', xt, w_gate[gi]))
               * jnp.einsum('nd,edf->nef', xt, w_up[gi]))
        out = out + jnp.einsum('nef,efd->nd', hid * combine[:, gi, :, None], w_down[gi])
    return out.reshape(bsz, T, D)

def trunk(x, s_hgrn, s_conv, s_gla, mem_k, mem_v,
          w_in_a, lb_a, conv_w, gnorm_a, w_out_a, w_in_c, w_gk2, b_gk2, gnorm_c, w_out_c,
          w_mq, w_mo, ln_g, ln_b, w_grp, b_grp, w_er, b_er, w_gate, w_up, w_down):
    lb = jnp.cumsum(jax.nn.softmax(lb_a.astype(jnp.float32), axis=0), axis=0)
    lb = lb - lb[0]
    new_hgrn, new_conv, new_gla = [], [], []
    for l in range(DEPTH):
        j = l // 2
        if l % 2 == 0:
            q, f, i, g, bg, cg, h = jnp.split(x @ w_in_a[j], EVEN_SPLITS, axis=-1)
            o_a, s_a = hgrn2_mix(q, f, i, g, lb[j], gnorm_a[j], s_hgrn[j])
            o_b, buf = short_conv_mix(bg, cg, h, conv_w[j], s_conv[j])
            mix = jnp.concatenate([o_a, o_b], axis=-1) @ w_out_a[j]
            new_hgrn.append(s_a)
            new_conv.append(buf)
        else:
            q, k, v, g, gz = jnp.split(x @ w_in_c[j], ODD_SPLITS, axis=-1)
            o_c, s_c = gla_mix(q, k, v, g, gz, w_gk2[j], b_gk2[j], gnorm_c[j], s_gla[j])
            mix = o_c @ w_out_c[j]
            new_gla.append(s_c)
        x = layer_norm(DN_ALPHA * x + mix, ln_g[l, 0], ln_b[l, 0])
        x = layer_norm(DN_ALPHA * x + memory_attention(x, mem_k[l], mem_v[l], w_mq[l], w_mo[l]),
                       ln_g[l, 1], ln_b[l, 1])
        x = layer_norm(DN_ALPHA * x + hier_moe(x, w_grp[l], b_grp[l], w_er[l], b_er[l],
                                               w_gate[l], w_up[l], w_down[l]),
                       ln_g[l, 2], ln_b[l, 2])
    return x, jnp.stack(new_hgrn), jnp.stack(new_conv), jnp.stack(new_gla)

def setup_inputs(seed: int = 0) -> dict:
    key = jax.random.key(seed)
    ks = iter(jax.random.split(key, 40))

    def nrm(shape, scale):
        return jax.random.normal(next(ks), shape, jnp.float32) * scale

    d_in = D_MODEL ** -0.5
    return {
        "x_prompt": nrm((BATCH, SEQ, D_MODEL), 1.0),
        "x_sample": nrm((DEC_BATCH, DEC_SEQ, D_MODEL), 1.0),
        "state_hgrn": nrm((N_A_LAYERS, DEC_BATCH, HA_HEADS, HA_DK, HA_DV), 0.5),
        "state_conv": nrm((N_A_LAYERS, DEC_BATCH, SC_KERNEL - 1, SC_WIDTH), 0.5),
        "state_gla": nrm((N_C_LAYERS, DEC_BATCH, GLA_HEADS, GLA_DK, GLA_DV), 0.3),
        "cache_mem_k": nrm((DEPTH, DEC_BATCH, MEM_LEN, MEM_HEADS, MEM_HD), 1.0),
        "cache_mem_v": nrm((DEPTH, DEC_BATCH, MEM_LEN, MEM_HEADS, MEM_HD), 1.0),
        "mem_prompt": nrm((BATCH, MEM_LEN, D_MODEL), 1.0),
        "w_in_a": nrm((N_A_LAYERS, D_MODEL, EVEN_IN), d_in),
        "lb_a": nrm((N_A_LAYERS, HA_FDIM), 0.5),
        "conv_w": nrm((N_A_LAYERS, SC_WIDTH, SC_KERNEL), SC_KERNEL ** -0.5),
        "gnorm_a": 1.0 + nrm((N_A_LAYERS, HA_DV), 0.02),
        "w_out_a": nrm((N_A_LAYERS, HA_WIDTH + SC_WIDTH, D_MODEL), (HA_WIDTH + SC_WIDTH) ** -0.5 * DN_BETA),
        "w_in_c": nrm((N_C_LAYERS, D_MODEL, ODD_IN), d_in),
        "w_gk2": nrm((N_C_LAYERS, GLA_RANK, GLA_KEY), GLA_RANK ** -0.5),
        "b_gk2": nrm((N_C_LAYERS, GLA_KEY), 0.1),
        "gnorm_c": 1.0 + nrm((N_C_LAYERS, GLA_DV), 0.02),
        "w_out_c": nrm((N_C_LAYERS, GLA_VAL, D_MODEL), GLA_VAL ** -0.5 * DN_BETA),
        "w_mq": nrm((DEPTH, D_MODEL, MEM_HEADS * MEM_HD), d_in),
        "w_mk": nrm((DEPTH, D_MODEL, MEM_HEADS * MEM_HD), d_in),
        "w_mv": nrm((DEPTH, D_MODEL, MEM_HEADS * MEM_HD), d_in),
        "w_mo": nrm((DEPTH, MEM_HEADS * MEM_HD, D_MODEL), (MEM_HEADS * MEM_HD) ** -0.5 * DN_BETA),
        "ln_g": 1.0 + nrm((DEPTH, 3, D_MODEL), 0.02),
        "ln_b": nrm((DEPTH, 3, D_MODEL), 0.02),
        "w_grp": nrm((DEPTH, D_MODEL, N_GROUPS), d_in),
        "b_grp": nrm((DEPTH, N_GROUPS), 0.01),
        "w_er": nrm((DEPTH, N_GROUPS, D_MODEL, EXP_PER_GROUP), d_in),
        "b_er": nrm((DEPTH, N_GROUPS, EXP_PER_GROUP), 0.01),
        "w_gate": nrm((DEPTH, N_GROUPS, EXP_PER_GROUP, D_MODEL, D_EXPERT), d_in),
        "w_up": nrm((DEPTH, N_GROUPS, EXP_PER_GROUP, D_MODEL, D_EXPERT), d_in),
        "w_down": nrm((DEPTH, N_GROUPS, EXP_PER_GROUP, D_EXPERT, D_MODEL), D_EXPERT ** -0.5 * DN_BETA),
    }

def reference(x_prompt, x_sample, state_hgrn, state_conv, state_gla, cache_mem_k, cache_mem_v, mem_prompt,
              w_in_a, lb_a, conv_w, gnorm_a, w_out_a, w_in_c, w_gk2, b_gk2, gnorm_c, w_out_c,
              w_mq, w_mk, w_mv, w_mo, ln_g, ln_b, w_grp, b_grp, w_er, b_er, w_gate, w_up, w_down):
    bsz = x_prompt.shape[0]
    mlen = mem_prompt.shape[1]
    mk_p = jnp.einsum('bmd,ldk->lbmk', mem_prompt, w_mk).reshape(DEPTH, bsz, mlen, MEM_HEADS, MEM_HD)
    mv_p = jnp.einsum('bmd,ldk->lbmk', mem_prompt, w_mv).reshape(DEPTH, bsz, mlen, MEM_HEADS, MEM_HD)
    z_hgrn = jnp.zeros((N_A_LAYERS, bsz, HA_HEADS, HA_DK, HA_DV), jnp.float32)
    z_conv = jnp.zeros((N_A_LAYERS, bsz, SC_KERNEL - 1, SC_WIDTH), x_prompt.dtype)
    z_gla = jnp.zeros((N_C_LAYERS, bsz, GLA_HEADS, GLA_DK, GLA_DV), jnp.float32)
    y_prompt, hgrn_p, conv_p, gla_p = trunk(
        x_prompt, z_hgrn, z_conv, z_gla, mk_p, mv_p,
        w_in_a, lb_a, conv_w, gnorm_a, w_out_a, w_in_c, w_gk2, b_gk2, gnorm_c, w_out_c,
        w_mq, w_mo, ln_g, ln_b, w_grp, b_grp, w_er, b_er, w_gate, w_up, w_down)
    y_sample, hgrn_s, conv_s, gla_s = trunk(
        x_sample, state_hgrn, state_conv, state_gla, cache_mem_k, cache_mem_v,
        w_in_a, lb_a, conv_w, gnorm_a, w_out_a, w_in_c, w_gk2, b_gk2, gnorm_c, w_out_c,
        w_mq, w_mo, ln_g, ln_b, w_grp, b_grp, w_er, b_er, w_gate, w_up, w_down)
    return (y_prompt, y_sample, hgrn_p, conv_p, gla_p, mk_p, mv_p, hgrn_s, conv_s, gla_s)


_drawn_inputs = setup_inputs


def setup_inputs(seed=0):
    import zlib

    import numpy as np

    out = dict(_drawn_inputs(seed))
    spreads = {}
    factors = {'gnorm_a': 4.667, 'gnorm_c': 21.471, 'b_grp': 8.0, 'b_er': 4.056}
    for name, (base, spread) in spreads.items():
        noise = np.random.default_rng([zlib.crc32(name.encode()), seed]).standard_normal(out[name].shape)
        drawn = base * np.exp(spread * noise) if base else spread * noise
        out[name] = __import__('jax').numpy.asarray(drawn.astype(out[name].dtype))
    for name, factor in factors.items():
        out[name] = (out[name] * factor).astype(out[name].dtype)
    return out
```

```python
from contextlib import ExitStack

import concourse.bass as bass
from concourse import mybir

ALU = mybir.AluOpType
ACT = mybir.ActivationFunctionType
AX = mybir.AxisListType
F32 = mybir.dt.float32
I32 = mybir.dt.int32
P = 128


class Steps:

    def __init__(self, eng, own, base=0):
        self.eng, self.own, self.base, self.n, self.told = eng, own, base, 0, {}

    def step(self, ins):
        self.n += 1
        ins.then_inc(self.own, 1)
        self.eng.wait_ge(self.own, self.base + self.n)

    def tell(self, ins, sem, base=0):
        self.told[sem.name] = self.told.get(sem.name, 0) + 1
        ins.then_inc(sem, 1)
        self.eng.wait_ge(sem, base + self.told[sem.name])


def build(nc, I, O):
    _, SEQ, D = I["x_prompt"].shape
    DB, DS, _ = I["x_sample"].shape
    NA, _, HEADS, DK, HDV = I["state_hgrn"].shape
    NC_, GDV = I["state_gla"].shape[0], I["state_gla"].shape[4]
    DEPTH, _, MEM, MH, MHD = I["cache_mem_k"].shape
    GROUPS, EPG, _, DE = I["w_gate"].shape[1:]
    CW = I["conv_w"].shape[1]
    NE = GROUPS * EPG
    KC = D // P
    NS = DB * DS
    NT = SEQ + NS
    PT_ = SEQ // P
    ROWS = [P] * PT_ + [NS]
    TT = len(ROWS)
    HALF = 512
    SLOTS = 6
    CAP = 64
    PAIRS = NE // 2
    LEVELS = 8
    SL = 3
    MT_ = MEM // P
    RANK = I["w_gk2"].shape[1]
    ALPHA = (2.0 * DEPTH) ** 0.25
    LN_EPS, RMS_EPS = 1e-5, 1e-6
    assert NA == 1 and NC_ == 1 and DEPTH == 2 and PT_ == 2 and DK == P and DS == 4 and D == 1024
    DVC = [HDV // P, GDV // P]

    def cols(t):
        return slice(t * P, t * P + ROWS[t])

    ctx = ExitStack()
    with ctx:
        sems = {}

        def S(name):
            if name not in sems:
                sems[name] = ctx.enter_context(nc.semaphore(name))
            return sems[name]

        def sb(name, shape, dt=F32):
            return ctx.enter_context(nc.sbuf_tensor(name, shape, dt))

        ident = sb("ident", [P, P])
        ones = sb("ones", [P, P])
        masks = sb("masks", [P, LEVELS, P])
        upper = sb("upper", [P, P])
        iota = sb("iota", [P, P])
        bmask = sb("bmask", [NS, DB])
        carry = sb("carry", [P, NT])
        valid = sb("valid", [P, TT])
        W = sb("W", [P, SLOTS, KC * HALF])
        X = sb("X", [P, TT, D])
        XT = sb("XT", [P, KC, NT])
        GB = sb("GB", [P, 2, D])
        convw = sb("convw", [P, CW // P, 3])
        gnorm = [sb(f"gnorm{l}", [P, DVC[l]]) for l in range(2)]
        wgz = sb("wgz", [P, KC, RANK])
        wgk2 = sb("wgk2", [RANK, HEADS * DK])
        bgk2 = sb("bgk2", [P, HEADS])
        gz = sb("gz", [RANK, NT])
        router_w = sb("router_w", [P, KC, GROUPS + NE])
        router_b = sb("router_b", [P, GROUPS + NE])
        stat = sb("stat", [P, 2, 6])
        mv = sb("mv", [P, 4])
        small = sb("small", [P, 16, 4])
        rev = sb("rev", [P, EPG])
        rounds = sb("rounds", [1, 1], I32)
        SCR_WORDS = nc.sbuf_bytes_remaining // 4 - 8
        scr = sb("scr", [P, SCR_WORDS])
        ps = ctx.enter_context(nc.psum_tensor("ps", [P, 8, HALF], F32))

        class Region:

            def __init__(self):
                self.at = 0

            def take(self, *shape, rows=P):
                n = 1
                for x in shape:
                    n *= x
                assert self.at + n <= SCR_WORDS, (self.at + n, SCR_WORDS)
                v = scr[0:rows, self.at:self.at + n]
                self.at += n
                if len(shape) == 2:
                    v = v.rearrange("p (a b) -> p a b", a=shape[0])
                if len(shape) == 3:
                    v = v.rearrange("p (a b c) -> p a b c", a=shape[0], b=shape[1])
                return v

        MIX = []
        for l in range(2):
            r, nv = Region(), DVC[l] * P
            m = dict(q=r.take(HEADS, NT), k=r.take(HEADS, NT), b=r.take(HEADS, NT),
                     g=r.take(HEADS * DVC[l], NT), v=r.take(TT, HEADS * nv),
                     qkd=r.take(2 * NT), kexp_all=r.take(DB * P),
                     o=r.take(KC, NT), ktok=r.take(TT, P), sq=r.take(DVC[l], NT), rs=r.take(NT),
                     s1=r.take(nv), sf=r.take(nv), dec=r.take(DB + PT_),
                     s0=[r.take(DB, nv) for _ in range(1)])
            m["qd"], m["kd"] = m["qkd"][:, 0:NT], m["qkd"][:, NT:2 * NT]
            m["conv_rows"] = m["qkd"][:, 0:CW]
            m["kexp"] = m["kexp_all"][0:NS, :].rearrange("p (b d) -> p b d", b=DB)
            mark = r.at
            m["ms"], m["st"] = r.take(LEVELS, P), r.take(TT, P)
            m["qk"] = XT[:, 0:7, :]
            m["tmp"] = m["o"][:, 0:HEADS, :]
            if l == 0:
                m["conv"] = [r.take(CW // P, NT) for _ in range(3)]
                r.at = mark
                m["up"], m["us"] = r.take(CW // P, SEQ + 2), r.take(CW // P, DB, 6)
            MIX.append(m)
        conv_in = MIX[0]["conv_rows"][0:2 * DB, :]
        conv_tok = MIX[0]["kexp_all"][0:2 + 2 * DB, 0:CW]
        conv_tail = MIX[0]["s1"][:, 0:(CW // P) * (2 + 2 * DB)].rearrange("p (c n) -> p c n", c=CW // P)
        r = Region()
        QT, KTP, VP = r.take(KC, NT), r.take(KC, MEM), r.take(MT_, D)
        KV = [r.take(MT_, D) for _ in range(3)]
        KT0 = r.take(KC, MEM)
        at = r.at
        PR = r.take(MH, MEM)
        PRT = r.take(MT_, MH * P)
        r.at = at
        KT = [KT0, r.take(KC, MEM)]
        SS, SST = r.take(MEM), r.take(MT_, P)
        OA = XT
        r = Region()
        LG, OHG, GE = r.take(TT, GROUPS + NE), r.take(TT, GROUPS), r.take(TT, GROUPS)
        SEL, OH1, OH2, WE8, AS8 = (r.take(TT, EPG) for _ in range(5))
        EM, THR = r.take(TT, GROUPS, EPG), r.take((NT - 1) // CAP)
        ASG, CMB, KEY = r.take(TT, NE), r.take(TT, NE), r.take(TT, NE + 2)
        PG, PW, PWT = r.take(TT, 2, CAP), r.take(TT, 2, CAP), r.take(NT)
        XG, SG, HS, HT = r.take(KC, P), r.take(DE), r.take(DE), r.take(DE // P, P)
        Y, ACC = r.take(D), r.take(TT, D)

        def unit_cols(w, a):
            return w[:, a:a + HALF].rearrange("(k p) n -> p k n", p=P)

        wia, woa, wic, woc = I["w_in_a"][0], I["w_out_a"][0], I["w_in_c"][0], I["w_out_c"][0]
        F = HEADS * DK
        in_cols = [
            [("bg", 4 * F), ("cg", 5 * F), ("h", 6 * F), ("f", F), ("q", 0), ("g", 3 * F), ("v", 2 * F)],
            [("q", 0), ("k", F), ("g", 4 * F), ("g1", 5 * F), ("v", 2 * F), ("v1", 3 * F)],
        ]
        units = []
        for l in range(DEPTH):
            while len(units) % SLOTS:
                units.append(None)
            for name, a in in_cols[l]:
                units.append((l, name, unit_cols([wia, wic][l], a)))
            for j in range(2):
                units.append((l, f"out{j}", unit_cols([woa, woc][l], j * HALF)))
            for name in ("mk", "mv", "mq", "mo"):
                for j in range(2):
                    units.append((l, f"{name}{j}", unit_cols(I[f"w_{name}"][l], j * HALF)))
        UNIT = {u[:2]: n for n, u in enumerate(units) if u}

        def wslot(l, name):
            return W[:, UNIT[l, name] % SLOTS, :].rearrange("p (k n) -> p k n", k=KC)

        def loads_in(n):
            return sum(1 for m in range(n % SLOTS, n + 1, SLOTS) if units[m])

        def unit_landed(eng, l, name):
            n = UNIT[l, name]
            eng.wait_ge(S(f"w_in{n % SLOTS}"), 16 * loads_in(n))

        jobs = {}
        order = []

        def plan(stage, *names):
            jobs.setdefault(stage, [])
            for name in names:
                jobs[stage].append((len(order), name))
                order.append((stage, name))

        def plan_xt(inst):
            plan(("xt", inst), *[("xt", t, h) for t in range(TT) for h in range(2)])

        plan_xt(0)
        for l in range(DEPTH):
            for name, _ in in_cols[l]:
                if name[0] != "v":
                    plan(("in", l), *[("feat", name, c) for c in range(4)])
            if l == 1:
                plan(("in", l), ("gz", "gz", 0), *[("gk", "gk", c) for c in range(4)])
            for name, _ in in_cols[l]:
                if name[0] == "v":
                    plan(("in", l), *[("tok", name, t) for t in range(TT)])
            plan(("mem", l), *[("mt", i, h) for i in range(MT_) for h in range(2)])
            plan(("mem", l), *[("memtok", f"{w}{j}", i) for w in ("mk", "mv") for j in range(2) for i in range(MT_)])
            plan_xt(1 + 3 * l)
            plan(("mq", l), *[("feat", f"mq{j}", c) for j in range(2) for c in range(4)])
            plan_xt(2 + 3 * l)
            if l + 1 < DEPTH:
                plan_xt(3 + 3 * l)

        def number(stage, name=None):
            return max(n for n, j in jobs[stage] if name is None or j[1] == name) + 1

        def kv_loads(l, i):
            return l * len(range(i % 3, 2 * DB, 3)) + i // 3 + 1

        per_layer = dict(
            softplus=1, e_ready=HEADS, ex_ready=HEADS, ktok_ps=HEADS, ktok=HEADS, s_ps=HEADS,
            s1_ready=HEADS, o_ps=HEADS, sq_ready=HEADS, ms_ready=HEADS, root=HEADS, score_ps=TT * HEADS,
            kd_ready=HEADS, qk_ready=HEADS, st_ready=TT * HEADS, kexp=HEADS, ns_ps=HEADS, ss_ps=HEADS,
            rms=HEADS, state_new=HEADS, state_out=32 * HEADS, kt_full=4 * (DB + 1), kt_a=2 * (DB + 1), kt_d=2
            * (DB + 1), ssc=DB, ss_sb=1, ss_rows=1, smax=1, sexp=1, sp_ready=1, spt_ps=1, spt_sb=1, psc=PT_,
            pmax=PT_, pexp=PT_, pr_ready=PT_, prt_ps=PT_, prt_sb=PT_, po_ps=PT_, oa_ready=TT, pv_done=DB,
            memk_out=16, logits=1, assigned=1, ranks=1, rounds_known=1, gdiff=1, gexp=1)

        def count_at(name, l, n):
            return l * per_layer[name] + n

        LNS = 3 * DEPTH
        mem_src = I["mem_prompt"][0].rearrange("(i p) d -> p i d", p=P)
        EXPERT_UNITS = ("gate", "up", "down")
        gate_rows = I["w_gate"].rearrange("l g e (k p) f -> (l g e) p k f", p=P)
        up_rows = I["w_up"].rearrange("l g e (k p) f -> (l g e) p k f", p=P)
        down_rows = I["w_down"].rearrange("l g e (k p) d -> (l g e) p k d", p=P)

        block = ctx.enter_context(nc.Block())

        @block.sync
        def _(sp):
            for t in range(PT_):
                sp.dma_start(X[:, t, :], I["x_prompt"][0, t * P:(t + 1) * P, :]).then_inc(S("x_in"), 16)
            sp.dma_start(X[0:NS, PT_, :], I["x_sample"].rearrange("b t d -> (b t) d")).then_inc(S("x_in"), 16)

            def used(n):
                l, name = units[n][:2]
                if name.startswith("out") or name.startswith("mo"):
                    i = 2 * l + (name[:2] == "mo")
                    sp.wait_ge(S("mix_unit"), 2 * i + int(name[-1]) + 1)
                else:
                    stage = ("in", l) if name[:2] not in ("mk", "mv", "mq") else ("mq", l) if name[:2] == "mq" else ("mem", l)
                    sp.wait_ge(S("pipe_full"), number(stage, name))

            n = 0
            rm1 = None
            for l in range(DEPTH):
                end = max(UNIT[k] for k in UNIT if k[0] == l) + 1
                start = min(UNIT[k] for k in UNIT if k[0] == l)
                for n in range(start, end):
                    if n - SLOTS >= start:
                        used(n - SLOTS)
                    elif l:
                        sp.wait_ge(S(f"{EXPERT_UNITS[n % SLOTS // 2]}_done{l - 1}"), rm1 * PAIRS + PAIRS)
                    sp.dma_start(W[:, n % SLOTS, :].rearrange("p (k n) -> p k n", k=KC), units[n][2]).then_inc(S(f"w_in{n % SLOTS}"), 16)

                def load_expert_unit(s, e):
                    base = (gate_rows, up_rows, down_rows)[s // 2]
                    sp.dma_start(W[:, s, :].rearrange("p (k n) -> p k n", k=(KC if s < 4 else DE // P)), base[e]).then_inc(S(f"e_in{l}_{s}"), 16)

                for s in range(SLOTS):
                    last = max(n for n in range(start, end) if n % SLOTS == s)
                    used(last)
                    load_expert_unit(s, l * NE + s % 2)
                sp.wait_ge(S("rounds_known"), count_at("rounds_known", l, 1))
                rm1 = sp.value_load(rounds[0:1, 0:1], min_val=0, max_val=4)
                with sp.Fori(0, rm1 * PAIRS + (PAIRS - 1)) as i:
                    nxt = (i + 1) % PAIRS
                    for s in range(SLOTS):
                        if s % 2 == 0:
                            sp.wait_ge(S(f"{EXPERT_UNITS[s // 2]}_done{l}"), i + 1)
                        load_expert_unit(s, nxt * 2 + (l * NE + s % 2))

        @block.gpsimd
        def _(pool):
            st = Steps(pool, S("pool_step"))
            st.step(pool.memset(ones[:], 1.0))
            st.step(pool.affine_select(out=ident[:], in_=ones[:], compare_op=ALU.is_equal, fill=0.0, base=0,
                                       pattern=[[1, P]], channel_multiplier=-1))
            st.step(pool.affine_select(out=upper[:], in_=ones[:], compare_op=ALU.is_gt, fill=0.0, base=0,
                                       pattern=[[1, P]], channel_multiplier=-1))
            st.step(pool.memset(masks[:], 0.0))
            st.step(pool.tensor_copy(masks[:, 0, :], ident[:]))
            for lv in range(1, LEVELS):
                B = 1 << lv
                right = masks[:, lv, :].rearrange("p (n two h) -> p n two h", two=2, h=B // 2)[:, :, 1, :]
                one = ones[:].rearrange("p (n two h) -> p n two h", two=2, h=B // 2)[:, :, 1, :]
                st.step(pool.affine_select(out=right, in_=one, compare_op=ALU.is_ge, fill=0.0, base=0,
                                           pattern=[[-B, P // B], [0, B // 2]], channel_multiplier=1))
                st.step(pool.affine_select(out=right, in_=right, compare_op=ALU.is_ge, fill=0.0, base=B // 2 - 1,
                                           pattern=[[B, P // B], [0, B // 2]], channel_multiplier=-1))
            st.step(pool.affine_select(out=bmask[:], in_=ones[0:NS, 0:DB], compare_op=ALU.is_ge, fill=0.0, base=0,
                                       pattern=[[-DS, DB]], channel_multiplier=1))
            st.step(pool.affine_select(out=bmask[:], in_=bmask[:], compare_op=ALU.is_ge, fill=0.0, base=DS - 1,
                                       pattern=[[DS, DB]], channel_multiplier=-1))
            st.step(pool.memset(carry[:], 1.0))
            st.step(pool.memset(carry[:, 0:SEQ].rearrange("p (t c) -> p t c", c=P)[:, :, 0], 0.0))
            st.step(pool.memset(carry[:, SEQ:NT].rearrange("p (b t) -> p b t", t=DS)[:, :, 0], 0.0))
            st.step(pool.memset(valid[:], 1.0))
            st.step(pool.memset(valid[:, TT - 1:TT], 0.0))
            pool.memset(valid[0:NS, TT - 1:TT], 1.0).then_inc(S("consts"), 1)

            def load(dst, src, sem):
                pool.dma_start(dst, src, allow_slow_non_contiguous=True).then_inc(S(sem), 16)

            load(convw[:], I["conv_w"][0].rearrange("(c p) j -> p c j", p=P), "small_in")
            for l in range(2):
                load(gnorm[l][:], I[("gnorm_a", "gnorm_c")[l]][0].rearrange("(c p) -> p c", p=P), "small_in")
            load(wgz[:], wic[:, 6 * F:6 * F + RANK].rearrange("(k p) n -> p k n", p=P), "small_in")
            load(wgk2[:], I["w_gk2"][0], "small_in")
            load(bgk2[:], I["b_gk2"][0].rearrange("(c p) -> p c", p=P), "small_in")

            for l in range(DEPTH):
                m, nv = MIX[l], DVC[l] * P
                s_in = (I["state_hgrn"], I["state_gla"])[l][0].rearrange("b h k v -> h k b v")
                s_out = O[("hgrn_s", "gla_s")[l]][0].rearrange("b h k v -> h k b v")
                p_out = O[("hgrn_p", "gla_p")[l]][0, 0]
                nb = len(m["s0"])
                if l == 0:
                    load(conv_in, I["state_conv"][0].rearrange("b j w -> (b j) w"), "conv_in")
                else:
                    pool.wait_ge(S("ln_done"), 9 * l)
                for h in range(nb):
                    load(m["s0"][h], s_in[h], f"s0_in{l}_{h % nb}")
                if l == 0:
                    pool.wait_ge(S("conv_out"), 1)
                    pool.dma_start(O["conv_p"][0, 0], conv_tok[0:2, :]).then_inc(S("stores"), 16)
                    pool.dma_start(O["conv_s"][0].rearrange("b j w -> (b j) w"), conv_tok[2:2 + 2 * DB, :]).then_inc(S("stores"), 16)
                for h in range(HEADS):
                    pool.wait_ge(S("state_new"), count_at("state_new", l, h + 1))
                    pool.dma_start(s_out[h], m["s0"][h % nb]).then_inc(S("state_out"), 16)
                    pool.dma_start(p_out[h], m["sf"]).then_inc(S("state_out"), 16)
                    if h + nb < HEADS:
                        pool.wait_ge(S("state_out"), count_at("state_out", l, 32 * (h + 1)))
                        load(m["s0"][h % nb], s_in[h + nb], f"s0_in{l}_{h % nb}")
                pool.wait_ge(S("state_out"), count_at("state_out", l, 32 * HEADS))

                pool.wait_ge(S("mix_unit"), 4 * l + 2)
                load(KV[0], mem_src, "mem_in")
                load(router_w[:, :, 0:GROUPS], I["w_grp"][l].rearrange("(k p) g -> p k g", p=P), "router_in")
                for g in range(GROUPS):
                    load(router_w[:, :, GROUPS + g * EPG:GROUPS + (g + 1) * EPG],
                         I["w_er"][l, g].rearrange("(k p) e -> p k e", p=P), "router_in")
                load(router_b[:, 0:GROUPS], I["b_grp"][l].partition_broadcast(P), "router_in")
                load(router_b[:, GROUPS:], I["b_er"][l].rearrange("g e -> (g e)").partition_broadcast(P), "router_in")
                kc = [I["cache_mem_k"][l, b].rearrange("(i p) h d -> p i (h d)", p=P) for b in range(DB)]
                vc = [I["cache_mem_v"][l, b].rearrange("(i p) h d -> p i (h d)", p=P) for b in range(DB)]
                pool.wait_ge(S("pipe_full"), jobs[("mem", l)][2 * MT_ - 1][0] + 1)
                load(KV[0], kc[0], f"kv_in0")
                pool.wait_ge(S("pipe_free"), number(("mem", l)))
                pool.dma_start(O["mem_k"][l, 0].rearrange("(i p) h d -> p i (h d)", p=P), KV[2]).then_inc(S("memk_out"), 16)
                pool.dma_start(O["mem_v"][l, 0].rearrange("(i p) h d -> p i (h d)", p=P), VP).then_inc(S("memv_out"), 16)
                load(KV[1], kc[1], f"kv_in1")
                pool.wait_ge(S("memk_out"), count_at("memk_out", l, 16))
                for i in range(2, 2 * DB):
                    if i < DB:
                        pool.wait_ge(S("kt_full"), count_at("kt_full", l, 4 * (1 if i == 2 else i - 1)))
                    elif i < DB + 3:
                        pool.wait_ge(S("kt_full"), count_at("kt_full", l, 4 * (i - 3 + 2)))
                    else:
                        pool.wait_ge(S("pv_done"), count_at("pv_done", l, i - 3 - DB + 1))
                    load(KV[i % 3], kc[i] if i < DB else vc[i - DB], f"kv_in{i % 3}")

            for t in range(TT):
                pool.wait_ge(S("ln_done"), 3 * (LNS - 1) + t + 1)
                dst = O["y_prompt"][0, t * P:(t + 1) * P, :] if t < PT_ else O["y_sample"].rearrange("b t d -> (b t) d")
                pool.dma_start(dst, X[0:ROWS[t], t, :]).then_inc(S("stores"), 16)
            pool.wait_ge(S("memv_out"), 16 * DEPTH)
            pool.wait_ge(S("stores"), 16 * (2 + TT))

        @block.tensor
        def _(pe):
            mm, tr = pe.matmul, pe.transpose

            def run_jobs(stage):
                for n, (kind, name, c) in jobs[stage]:
                    if n >= 2:
                        pe.wait_ge(S("pipe_free"), n - 1)
                    bank = ps[:, 6 + n % 2, :]
                    l = stage[1]
                    if kind == "xt":
                        t, h = name, c
                        if h == 0 and stage[1] == 0:
                            pe.wait_ge(S("x_in"), 16 * TT)
                            pe.wait_ge(S("consts"), 1)
                        elif h == 0:
                            pe.wait_ge(S("ln_done"), 3 * (stage[1] - 1) + t + 1)
                        for k in range(4):
                            last = tr(bank[:, k * P:k * P + ROWS[t]], X[0:ROWS[t], t, (4 * h + k) * P:(4 * h + k + 1) * P],
                                      ident[0:ROWS[t], 0:ROWS[t]])
                    elif kind == "feat":
                        if c == 0:
                            unit_landed(pe, l, name)
                        w = wslot(l, name)
                        for k in range(KC):
                            last = mm(bank[:, 0:NT], w[:, k, c * P:(c + 1) * P], XT[:, k, :], start=(k == 0), stop=(k == KC - 1))
                    elif kind == "gz":
                        pe.wait_ge(S("small_in"), 16 * 6)
                        for k in range(KC):
                            last = mm(bank[0:RANK, 0:NT], wgz[:, k, :], XT[:, k, :], start=(k == 0), stop=(k == KC - 1))
                    elif kind == "gk":
                        if c == 0:
                            pe.wait_ge(S("pipe_free"), number(("in", 1), "gz"))
                        last = mm(bank[:, 0:NT], wgk2[:, c * P:(c + 1) * P], gz[:], start=True, stop=True)
                    elif kind == "tok":
                        if c == 0:
                            unit_landed(pe, l, name)
                        w = wslot(l, name)
                        for k in range(KC):
                            last = mm(bank[0:ROWS[c], :], XT[:, k, cols(c)], w[:, k, :], start=(k == 0), stop=(k == KC - 1))
                    elif kind == "mt":
                        i, h = name, c
                        if i == 0 and h == 0:
                            pe.wait_ge(S("mem_in"), 16 * (l + 1))
                        for k in range(4):
                            last = tr(bank[:, k * P:(k + 1) * P], KV[0][:, i, (4 * h + k) * P:(4 * h + k + 1) * P], ident[:])
                    elif kind == "memtok":
                        if c == 0:
                            unit_landed(pe, l, name)
                        if name == "mk0" and c == 0:
                            pe.wait_ge(S("pipe_free"), n)
                        w = wslot(l, name)
                        memT = KV[1].rearrange("p i d -> p (i d)").rearrange("p (k m) -> p k m", k=KC)
                        for k in range(KC):
                            last = mm(bank, memT[:, k, c * P:(c + 1) * P], w[:, k, :], start=(k == 0), stop=(k == KC - 1))
                    last.then_inc(S("pipe_full"), 1)
                pe.wait_ge(S("pipe_free"), number(stage))

            def project_out(l, src, which, inst):
                for j in range(2):
                    unit_landed(pe, l, f"{which}{j}")
                    w = wslot(l, f"{which}{j}")
                    for t in range(TT):
                        for k in range(KC):
                            last = mm(ps[0:ROWS[t], 2 * t + j, :], src[:, k, cols(t)], w[:, k, :], start=(k == 0), stop=(k == KC - 1))
                        if t < TT - 1:
                            last.then_inc(S("mix_done"), 1)
                    last.then_inc(S("mix_unit"), 1)

            def mixer(l):
                m, dvc = MIX[l], DVC[l]
                nv = dvc * P
                o_bank = [5, 6]
                if l == 0:
                    pe.wait_ge(S("iota_ready"), 1)
                    pe.wait_ge(S("conv_in"), 16)
                    for c in range(CW // P):
                        last = tr(ps[:, 0, c * 16:(c + 1) * 16], conv_in[:, c * P:(c + 1) * P], ident[0:2 * DB, 0:2 * DB])
                    last.then_inc(S("conv_ps"), 1)
                    pe.wait_ge(S("conv_u"), 1)
                    for c in range(CW // P):
                        last = tr(ps[0:2 + 2 * DB, 1, c * P:(c + 1) * P], conv_tail[:, c, :], ident[:])
                    last.then_inc(S("conv_ps"), 1)
                    pe.wait_ge(S("conv_out"), 1)
                for h in range(HEADS):
                    pe.wait_ge(S("qk_ready"), count_at("qk_ready", l, h + 1))
                    if h:
                        pe.wait_ge(S("state_new"), count_at("state_new", l, h))
                    for t in range(PT_):
                        for lv in range(LEVELS):
                            a = m["k"][:, h, cols(t)] if lv == 0 else m["qk"][:, lv - 1, cols(t)]
                            b = m["q"][:, h, cols(t)] if lv == 0 else m["qk"][:, lv - 1, cols(t)]
                            last = mm(ps[:, 2 * t + lv // 4, (lv % 4) * P:(lv % 4 + 1) * P], a, b, start=True, stop=True)
                        last.then_inc(S("score_ps"), 1)
                    t = PT_
                    if h:
                        pe.wait_ge(S("rms"), count_at("rms", l, h))
                    for lv in range(SL):
                        a = m["k"][:, h, cols(t)] if lv == 0 else m["qk"][:, lv - 1, cols(t)]
                        b = m["q"][:, h, cols(t)] if lv == 0 else m["qk"][:, lv - 1, cols(t)]
                        last = mm(ps[0:NS, 4, lv * NS:(lv + 1) * NS], a, b, start=True, stop=True)
                    last.then_inc(S("score_ps"), 1)
                    pe.wait_ge(S("kd_ready"), count_at("kd_ready", l, h + 1))
                    for t in range(TT):
                        last = tr(ps[0:ROWS[t], 5, t * P:(t + 1) * P], m["kd"][:, cols(t)], ident[:])
                    last.then_inc(S("ktok_ps"), 1)
                    pe.wait_ge(S("ktok"), count_at("ktok", l, h + 1))
                    if h:
                        pe.wait_ge(S("state_new"), count_at("state_new", l, h))
                    for t in range(PT_):
                        last = mm(ps[:, 7, t * nv:(t + 1) * nv], m["ktok"][:, t, :], m["v"][:, t, h * nv:(h + 1) * nv], start=True, stop=True)
                    last.then_inc(S("s_ps"), 1)
                    pe.wait_ge(S("st_ready"), count_at("st_ready", l, TT * (h + 1)))
                    pe.wait_ge(S("s1_ready"), count_at("s1_ready", l, h + 1))
                    pe.wait_ge(S(f"s0_in{l}_{h % len(m['s0'])}"), 16 * (h // len(m["s0"]) + 1))
                    s0 = m["s0"][h % len(m["s0"])]
                    for c in range(dvc):
                        o = ps[:, o_bank[c], :]
                        vc = slice(h * nv + c * P, h * nv + (c + 1) * P)
                        mm(o[:, cols(0)], m["v"][:, 0, vc], m["st"][:, 0, :], start=True, stop=True)
                        mm(o[:, cols(1)], m["v"][:, 1, vc], m["st"][:, 1, :], start=True, stop=False)
                        mm(o[:, cols(1)], m["s1"][:, c * P:(c + 1) * P], m["qd"][:, cols(1)], start=False, stop=True)
                        mm(o[:, cols(2)], m["v"][0:NS, 2, vc], m["st"][0:NS, 2, 0:NS], start=True, stop=False)
                        for b in range(DB):
                            sc = slice(SEQ + b * DS, SEQ + (b + 1) * DS)
                            last = mm(o[:, sc], s0[:, b, c * P:(c + 1) * P], m["qd"][:, sc], start=False, stop=(b == DB - 1))
                    last.then_inc(S("o_ps"), 1)
                    pe.wait_ge(S("kexp"), count_at("kexp", l, h + 1))
                    per = HALF // nv
                    for b in range(DB):
                        last = mm(ps[:, b // per, (b % per) * nv:(b % per + 1) * nv], m["kexp"][:, b, :],
                                  m["v"][0:NS, 2, h * nv:(h + 1) * nv], start=True, stop=True)
                    last.then_inc(S("ns_ps"), 1)
                    pe.wait_ge(S("sq_ready"), count_at("sq_ready", l, h + 1))
                    for c in range(dvc):
                        last = mm(ps[:, 4, 0:NT], ones[:], m["sq"][:, c, :], start=(c == 0), stop=(c == dvc - 1))
                    last.then_inc(S("ss_ps"), 1)
                pe.wait_ge(S("rms"), count_at("rms", l, HEADS))

            def attention(l):
                def turn_keys(n, src):
                    for j in range(4):
                        if n:
                            pe.wait_ge(S(("kt_a", "kt_d")[j // 2]), count_at("kt_a", l, 2 * (n - 1) + j % 2 + 1))
                        for c in range(2):
                            for i in range(MT_):
                                last = tr(ps[:, j, (2 * c + i) * P:(2 * c + i + 1) * P], src[:, i, (2 * j + c) * P:(2 * j + c + 1) * P], ident[:])
                        last.then_inc(S("kt_full"), 1)

                pe.wait_ge(S("ln_done"), 3 * (3 * l) + TT)
                turn_keys(0, KV[2])
                run_jobs(("xt", 1 + 3 * l))
                run_jobs(("mq", l))

                def sample_scores(b):
                    pe.wait_ge(S("kt_a"), count_at("kt_a", l, 2 * (b + 2)))
                    pe.wait_ge(S("kt_d"), count_at("kt_d", l, 2 * (b + 2)))
                    for h in range(MH):
                        for i in range(MT_):
                            for c in range(2):
                                at = i * P + (b * MH + h) * DS
                                last = mm(ps[:, 4, at:at + DS], KT[b % 2][:, 2 * h + c, i * P:(i + 1) * P],
                                          QT[:, 2 * h + c, SEQ + b * DS:SEQ + (b + 1) * DS], start=(c == 0), stop=(c == 1))
                    last.then_inc(S("ssc"), 1)

                for b in range(DB):
                    pe.wait_ge(S(f"kv_in{b % 3}"), 16 * (kv_loads(l, b)))
                    turn_keys(b + 1, KV[b % 3])
                    if b:
                        sample_scores(b - 1)
                sample_scores(DB - 1)
                pe.wait_ge(S("ss_sb"), count_at("ss_sb", l, 1))
                for i in range(MT_):
                    last = tr(ps[:, 5, i * P:(i + 1) * P], SST[:, i, :], ident[:])
                last.then_inc(S("ss_rows"), 1)
                pe.wait_ge(S("kt_a"), count_at("kt_a", l, 2 * (DB + 1)))
                pe.wait_ge(S("kt_d"), count_at("kt_d", l, 2 * (DB + 1)))

                def prompt_scores(t):
                    for h in range(MH):
                        for c in range(2):
                            last = mm(ps[:, 2 * t + h // 2, (h % 2) * MEM:(h % 2 + 1) * MEM], QT[:, 2 * h + c, cols(t)],
                                      KTP[:, 2 * h + c, :], start=(c == 0), stop=(c == 1))
                    last.then_inc(S("psc"), 1)

                prompt_scores(0)
                prompt_scores(1)
                pe.wait_ge(S("sp_ready"), count_at("sp_ready", l, 1))
                for i in range(MT_):
                    last = tr(ps[:, 4, i * P:(i + 1) * P], SS[:, i * P:(i + 1) * P], ident[:])
                last.then_inc(S("spt_ps"), 1)
                pe.wait_ge(S("spt_sb"), count_at("spt_sb", l, 1))
                for b in range(DB):
                    i = DB + b
                    pe.wait_ge(S(f"kv_in{i % 3}"), 16 * kv_loads(l, i))
                    for h in range(MH):
                        for c in range(2):
                            at = (2 * h + c) * NS + b * DS
                            for i2 in range(MT_):
                                last = mm(ps[:, 5, at:at + DS], KV[i % 3][:, i2, (2 * h + c) * P:(2 * h + c + 1) * P],
                                          SST[:, i2, (b * MH + h) * DS:(b * MH + h + 1) * DS], start=(i2 == 0), stop=(i2 == MT_ - 1))
                    last.then_inc(S("pv_done"), 1)
                for t in range(PT_):
                    pe.wait_ge(S("pr_ready"), count_at("pr_ready", l, t + 1))
                    for i in range(MT_):
                        for h in range(MH):
                            last = tr(ps[:, 6 + i, h * P:(h + 1) * P], PR[:, h, i * P:(i + 1) * P], ident[:])
                    last.then_inc(S("prt_ps"), 1)
                    pe.wait_ge(S("prt_sb"), count_at("prt_sb", l, t + 1))
                    for k in range(KC):
                        for i in range(MT_):
                            last = mm(ps[:, 2 * t + k // 4, (k % 4) * P:(k % 4 + 1) * P], VP[:, i, k * P:(k + 1) * P],
                                      PRT[:, i, (k // 2) * P:(k // 2 + 1) * P], start=(i == 0), stop=(i == MT_ - 1))
                    last.then_inc(S("po_ps"), 1)
                pe.wait_ge(S("oa_ready"), count_at("oa_ready", l, 3))

            def moe(l):
                pe.wait_ge(S("router_in"), 16 * (GROUPS + 3) * (l + 1))
                for t in range(TT):
                    for k in range(KC):
                        last = mm(ps[0:ROWS[t], 0, t * 64:t * 64 + GROUPS + NE], XT[:, k, cols(t)], router_w[:, k, :],
                                  start=(k == 0), stop=(k == KC - 1))
                last.then_inc(S("logits"), 1)
                pe.wait_ge(S("assigned"), count_at("assigned", l, 1))
                for t in range(TT):
                    for u in range(t + 1):
                        last = mm(ps[:, 1, t * NE:(t + 1) * NE], upper[:] if u == t else ones[:], ASG[:, u, :],
                                  start=(u == 0), stop=(u == t))
                for u in range(TT):
                    last = mm(ps[:, 1, TT * NE:(TT + 1) * NE], ones[:], ASG[:, u, :], start=(u == 0), stop=(u == TT - 1))
                last.then_inc(S("ranks"), 1)
                pe.wait_ge(S("rounds_known"), count_at("rounds_known", l, 1))
                rm1 = pe.value_load(rounds[0:1, 0:1], min_val=0, max_val=4)

                def scatter(it, part):
                    for n in part:
                        t, j = n // 2, n % 2
                        if n >= 2:
                            pe.wait_ge(S(f"acc{l}"), it * (2 * TT) + (n - 1))
                        last = mm(ps[0:ROWS[t], 7 - n % 2, :], PWT[:, cols(t)], Y[:, j * HALF:(j + 1) * HALF], start=True, stop=True)
                        last.then_inc(S(f"scat{l}"), 1)

                def gather(it):
                    pe.wait_ge(S(f"pg_part{l}"), it * TT + TT)
                    for k in range(KC):
                        for t in range(TT):
                            last = mm(ps[:, k // 4, (k % 4) * P:(k % 4 + 1) * P], X[0:ROWS[t], t, k * P:(k + 1) * P],
                                      PG[0:ROWS[t], t, :, :].rearrange("p j c -> p (j c)"), start=(t == 0), stop=(t == TT - 1))
                        if k == 3:
                            last.then_inc(S(f"xg_ps0{l}"), 1)
                    last.then_inc(S(f"xg_ps1{l}"), 1)

                gather(0)
                def both_experts(bank, s, x, n):
                    w = [W[:, s + j, :].rearrange("p (k n) -> p k n", k=x.shape[1]) for j in range(2)]
                    for k in range(x.shape[1]):
                        for j in range(2):
                            last = mm(ps[j * CAP:(j + 1) * CAP, bank, :], x[:, k, j * CAP:(j + 1) * CAP],
                                      w[j][:, k, n * HALF:(n + 1) * HALF], start=(k == 0), stop=(k == x.shape[1] - 1))
                    return last

                def landed(it, s):
                    pe.wait_ge(S(f"e_in{l}_{s}"), 16 * (it + 1))
                    pe.wait_ge(S(f"e_in{l}_{s + 1}"), 16 * (it + 1))

                with pe.Fori(0, rm1 + 1) as rd:
                    with pe.Fori(0, PAIRS) as p:
                        it = rd * PAIRS + p
                        pe.wait_ge(S(f"xg_a{l}"), it + 1)
                        pe.wait_ge(S(f"xg_d{l}"), it + 1)
                        pe.wait_ge(S(f"ht{l}"), it + 1)
                        landed(it, 0)
                        both_experts(2, 0, XG, 0).then_inc(S(f"gate_done{l}"), 1)
                        gather(it + 1)
                        pe.wait_ge(S(f"h_ready{l}"), it + 1)
                        landed(it, 2)
                        both_experts(3, 2, XG, 0).then_inc(S(f"up_done{l}"), 1)
                        pe.wait_ge(S(f"y_sb{l}"), it + 1)
                        pe.wait_ge(S(f"pwt_sb{l}"), it + 1)
                        scatter(it, range(0, 3))
                        pe.wait_ge(S(f"h_ready{l}"), it + 2)
                        for f in range(DE // P):
                            last = tr(ps[:, 2, f * P:(f + 1) * P], HS[:, f * P:(f + 1) * P], ident[:])
                        last.then_inc(S(f"ht_ps{l}"), 1)
                        scatter(it, range(3, 2 * TT))
                        pe.wait_ge(S(f"acc{l}"), it * (2 * TT) + 2 * TT)
                        pe.wait_ge(S(f"pw_part{l}"), it * TT + TT)
                        for t in range(TT):
                            last = tr(ps[:, 6, cols(t)], PW[0:ROWS[t], t, :, :].rearrange("p j c -> p (j c)"), ident[0:ROWS[t], 0:ROWS[t]])
                        last.then_inc(S(f"pwt_ps{l}"), 1)
                        pe.wait_ge(S(f"ht{l}"), it + 2)
                        landed(it, 4)
                        both_experts(4, 4, HT, 0)
                        both_experts(5, 4, HT, 1).then_inc(S(f"down_done{l}"), 1)
                pe.wait_ge(S(f"y_sb{l}"), rm1 * PAIRS + (PAIRS + 1))
                pe.wait_ge(S(f"pwt_sb{l}"), rm1 * PAIRS + (PAIRS + 1))
                scatter(rm1 * PAIRS + PAIRS, range(2 * TT))
                pe.wait_ge(S(f"acc{l}"), rm1 * (PAIRS * 2 * TT) + (PAIRS + 1) * 2 * TT)

            pe.wait_ge(S("consts"), 1)
            mm(ps[:, 0, 0:P], ones[:], upper[:], start=True, stop=True).then_inc(S("iota_ps"), 1)
            run_jobs(("xt", 0))
            for l in range(DEPTH):
                run_jobs(("in", l))
                mixer(l)
                project_out(l, MIX[l]["o"], "out", 1 + 3 * l)
                run_jobs(("mem", l))
                attention(l)
                project_out(l, OA, "mo", 2 + 3 * l)
                run_jobs(("xt", 2 + 3 * l))
                moe(l)
                if l + 1 < DEPTH:
                    run_jobs(("xt", 3 + 3 * l))

        @block.scalar
        def _(act):
            st = Steps(act, S("act_step"))
            fn = act.activation

            def load_gb(inst):
                l, n = (inst - 1) // 3, (inst - 1) % 3
                if inst > 1:
                    act.wait_ge(S("ln_done"), 3 * (inst - 1))
                act.dma_start(GB[:, 0, :], I["ln_g"][l, n].partition_broadcast(P)).then_inc(S("gb_in"), 16)
                act.dma_start(GB[:, 1, :], I["ln_b"][l, n].partition_broadcast(P)).then_inc(S("gb_in"), 16)

            def empty_jobs(stage, before=None):
                for n, (kind, name, c) in jobs[stage]:
                    act.wait_ge(S("pipe_full"), n + 1)
                    bank = ps[:, 6 + n % 2, :]
                    l = stage[1]
                    m = MIX[l] if l < 2 else None
                    full = bank[:, 0:NT]
                    if kind == "xt":
                        src = bank.rearrange("p (k t) -> p k t", k=4)[:, :, 0:ROWS[name]]
                        ins = fn(XT[:, 4 * c:4 * c + 4, cols(name)], src, ACT.Copy)
                    elif kind == "feat" and name[:2] == "mq":
                        ins = fn(QT[:, 4 * int(name[2]) + c, :], full, ACT.Copy, scale=float(MHD) ** -0.5)
                    elif kind == "feat" and name in ("bg", "cg", "h"):
                        ins = fn(m["conv"][("bg", "cg", "h").index(name)][:, c, :], full, ACT.Copy)
                    elif kind == "feat" and name == "f":
                        ins = fn(m["b"][:, c, :], full, ACT.Copy)
                    elif kind == "feat" and name == "q" and l == 0:
                        ins = fn(m["q"][:, c, :], full, ACT.Silu)
                    elif kind == "feat" and name == "q":
                        ins = fn(m["q"][:, c, :], full, ACT.Copy, scale=float(DK) ** -0.5)
                    elif kind == "feat" and name == "k":
                        ins = fn(m["k"][:, c, :], full, ACT.Copy)
                    elif kind == "feat":
                        ins = fn(m["g"][:, 4 * (name == "g1") + c, :], full, ACT.Silu)
                    elif kind == "gz":
                        ins = fn(gz[:], bank[0:RANK, 0:NT], ACT.Copy)
                    elif kind == "gk":
                        ins = fn(m["b"][:, c, :], full, ACT.Identity, bias=bgk2[:, c:c + 1])
                    elif kind == "tok":
                        at = HALF * (name == "v1")
                        ins = fn(m["v"][0:ROWS[c], c, at:at + HALF], bank[0:ROWS[c], :], ACT.Copy)
                    elif kind == "mt":
                        memT = KV[1].rearrange("p i d -> p (i d)").rearrange("p (k m) -> p k m", k=KC)
                        ins = fn(memT[:, 4 * c:4 * c + 4, name * P:(name + 1) * P], bank.rearrange("p (k t) -> p k t", k=4), ACT.Copy)
                    elif kind == "memtok":
                        at = HALF * int(name[2])
                        dst = KV[2] if name[:2] == "mk" else VP
                        ins = fn(dst[:, c, at:at + HALF], bank, ACT.Copy)
                    ins.then_inc(S("pipe_free"), 1)

            def mixer(l):
                m, dvc = MIX[l], DVC[l]
                z, tmp = m["b"], m["tmp"]
                act.wait_ge(S("pipe_free"), number(("in", l), "f" if l == 0 else "gk"))
                st.step(fn(tmp, z, ACT.Abs))
                st.step(fn(tmp, tmp, ACT.Exp, scale=-1.0))
                st.tell(fn(tmp, tmp, ACT.Ln, bias=1.0), S("softplus"))
                if l == 0:
                    act.wait_ge(S("amz_ready"), 1)
                    st.tell(fn(m["k"], m["k"], ACT.Exp), S("k_ready"))
                for h in range(HEADS):
                    act.wait_ge(S("e_ready"), count_at("e_ready", l, h + 1))
                    st.step(fn(m["qk"][:, 0:SL - 1, :], m["qk"][:, 0:SL - 1, :], ACT.Exp))
                    st.step(fn(m["qk"][:, SL - 1:, 0:SEQ], m["qk"][:, SL - 1:, 0:SEQ], ACT.Exp))
                    st.step(fn(m["qd"], m["b"][:, h, :], ACT.Exp))
                    st.step(fn(m["dec"], m["dec"], ACT.Exp))
                    st.tell(fn(m["kd"], m["kd"], ACT.Exp), S("ex_ready"))
                    act.wait_ge(S("ktok_ps"), count_at("ktok_ps", l, h + 1))
                    st.step(fn(m["ktok"][:, 0:PT_, :], ps[:, 5, 0:PT_ * P].rearrange("p (t c) -> p t c", t=PT_), ACT.Copy))
                    st.tell(fn(m["ktok"][0:NS, PT_, :], ps[0:NS, 5, PT_ * P:(PT_ + 1) * P], ACT.Copy), S("ktok"))
                    act.wait_ge(S("s_ps"), count_at("s_ps", l, h + 1))
                    st.tell(fn(m["s1"], ps[:, 7, 0:dvc * P], ACT.Copy), S("s1_ready"))
                    act.wait_ge(S("o_ps"), count_at("o_ps", l, h + 1))
                    for c in range(dvc):
                        ins = fn(m["sq"][:, c, :], ps[:, 5 + c, 0:NT], ACT.Square)
                        if c < dvc - 1:
                            st.step(ins)
                    st.tell(ins, S("sq_ready"))
                    act.wait_ge(S("ms_ready"), count_at("ms_ready", l, h + 1))
                    st.tell(fn(m["rs"], m["rs"], ACT.Sqrt), S("root"))

            def norm(inst):
                for t in range(TT):
                    act.wait_ge(S("var_ready"), 3 * (inst - 1) + t + 1)
                    st.tell(fn(mv[0:ROWS[t], 2:3], mv[0:ROWS[t], 2:3], ACT.Sqrt), S("std_ready"))

            def attention(l):
                def keys(n, dst):
                    for j in range(2):
                        act.wait_ge(S("kt_full"), count_at("kt_full", l, 4 * n + j + 1))
                        st.tell(fn(dst[:, 2 * j:2 * j + 2, :].rearrange("p c m -> p (c m)"), ps[:, j, :], ACT.Copy), S("kt_a"))

                keys(0, KTP)
                empty_jobs(("xt", 1 + 3 * l))
                load_gb(2 + 3 * l)
                empty_jobs(("mq", l))
                for b in range(DB):
                    if b >= 2:
                        act.wait_ge(S("ssc"), count_at("ssc", l, b - 1))
                    keys(b + 1, KT[b % 2])
                act.wait_ge(S("ssc"), count_at("ssc", l, DB))
                st.tell(fn(SST.rearrange("p i c -> p (i c)"), ps[:, 4, 0:MEM], ACT.Copy), S("ss_sb"))
                act.wait_ge(S("smax"), count_at("smax", l, 1))
                st.tell(fn(SS, ps[:, 5, 0:MEM], ACT.Exp, bias=small[:, 0, 0:1], accum_out=small[:, 1, 0:1]), S("sexp"))
                act.wait_ge(S("spt_ps"), count_at("spt_ps", l, 1))
                st.tell(fn(SST.rearrange("p i c -> p (i c)"), ps[:, 4, 0:MEM], ACT.Copy), S("spt_sb"))
                for t in range(PT_):
                    act.wait_ge(S("pmax"), count_at("pmax", l, t + 1))
                    for h in range(MH):
                        ins = fn(PR[:, h, :], ps[:, 2 * t + h // 2, (h % 2) * MEM:(h % 2 + 1) * MEM], ACT.Exp,
                                 bias=small[:, 2, h:h + 1], accum_out=small[:, 3, h:h + 1])
                        if h < MH - 1:
                            st.step(ins)
                    st.tell(ins, S("pexp"))
                    act.wait_ge(S("prt_ps"), count_at("prt_ps", l, t + 1))
                    st.step(fn(PRT[:, 0, :], ps[:, 6, :], ACT.Copy))
                    st.tell(fn(PRT[:, 1, :], ps[:, 7, :], ACT.Copy), S("prt_sb"))
                    if t == 0:
                        act.wait_ge(S("pv_done"), count_at("pv_done", l, DB))
                        st.tell(fn(OA[:, :, SEQ:NT], ps[:, 5, 0:KC * NS].rearrange("p (k t) -> p k t", k=KC), ACT.Copy), S("oa_ready"))
                    act.wait_ge(S("po_ps"), count_at("po_ps", l, t + 1))
                    st.step(fn(OA[:, 0:4, cols(t)], ps[:, 2 * t, :].rearrange("p (k t) -> p k t", k=4), ACT.Copy))
                    st.tell(fn(OA[:, 4:8, cols(t)], ps[:, 2 * t + 1, :].rearrange("p (k t) -> p k t", k=4), ACT.Copy), S("oa_ready"))

            def moe(l):
                act.wait_ge(S("gdiff"), count_at("gdiff", l, 1))
                st.step(fn(GE, GE, ACT.Exp))
                st.tell(fn(small[:, 6, 0:TT], small[:, 6, 0:TT], ACT.Exp), S("gexp"))
                act.wait_ge(S("rounds_known"), count_at("rounds_known", l, 1))
                rm1 = act.value_load(rounds[0:1, 0:1], min_val=0, max_val=4)
                def move_gathered(it):
                    act.wait_ge(S(f"xg_ps0{l}"), it + 1)
                    fn(XG[:, 0:4, :].rearrange("p k c -> p (k c)"), ps[:, 0, :], ACT.Copy).then_inc(S(f"xg_a{l}"), 1)

                move_gathered(0)
                with act.Fori(0, rm1 + 1) as rd:
                    with act.Fori(0, PAIRS) as p:
                        it = rd * PAIRS + p
                        act.wait_ge(S(f"gate_done{l}"), it + 1)
                        act.wait_ge(S(f"h_ready{l}"), it + 1)
                        fn(SG, ps[:, 2, :], ACT.Silu).then_inc(S(f"sg{l}"), 1)
                        act.wait_ge(S(f"up_done{l}"), it + 1)
                        move_gathered(it + 1)
                        act.wait_ge(S(f"ht_ps{l}"), it + 1)
                        fn(HT.rearrange("p f c -> p (f c)"), ps[:, 2, :], ACT.Copy).then_inc(S(f"ht{l}"), 1)
                        act.wait_ge(S(f"pwt_ps{l}"), it + 2)
                        fn(PWT, ps[:, 6, 0:NT], ACT.Copy).then_inc(S(f"pwt_sb{l}"), 1)
                        act.wait_ge(S(f"down_done{l}"), it + 1)
                        fn(Y, ps[:, 4:6, :].rearrange("p j n -> p (j n)"), ACT.Copy).then_inc(S(f"y_sb{l}"), 1)

            load_gb(1)
            empty_jobs(("xt", 0))
            for l in range(DEPTH):
                empty_jobs(("in", l))
                mixer(l)
                norm(1 + 3 * l)
                empty_jobs(("mem", l))
                attention(l)
                norm(2 + 3 * l)
                empty_jobs(("xt", 2 + 3 * l))
                load_gb(3 + 3 * l)
                moe(l)
                norm(3 + 3 * l)
                if l + 1 < DEPTH:
                    empty_jobs(("xt", 3 + 3 * l))
                    load_gb(4 + 3 * l)

        @block.vector
        def _(dve):
            st = Steps(dve, S("dve_step"))
            step, tell = st.step, st.tell
            tt, ts, stt, cp, red = (dve.tensor_tensor, dve.tensor_scalar, dve.scalar_tensor_tensor,
                                    dve.tensor_copy, dve.tensor_reduce)

            def bc(ap, *shape):
                return ap.to_broadcast(list(shape))

            def conv(m):
                bg, cg, hh = m["conv"]
                up, us, C = m["up"], m["us"], CW // P
                dve.wait_ge(S("pipe_free"), number(("in", 0), "h"))
                step(dve.memset(up[:, :, 0:2], 0.0))
                dve.wait_ge(S("conv_ps"), 1)
                for c in range(C):
                    step(tt(up[:, c, 2:], cg[:, c, 0:SEQ], hh[:, c, 0:SEQ], ALU.mult))
                    step(tt(us[:, c, :, 2:], cg[:, c, SEQ:].rearrange("p (b t) -> p b t", b=DB),
                            hh[:, c, SEQ:].rearrange("p (b t) -> p b t", b=DB), ALU.mult))
                    step(cp(us[:, c, :, 0:2], ps[:, 0, c * 16:(c + 1) * 16].rearrange("p (b j) -> p b j", b=DB)))
                step(cp(conv_tail[:, :, 0:2], up[:, :, SEQ:SEQ + 2]))
                for c in range(C - 1):
                    step(cp(conv_tail[:, c, 2:].rearrange("p (b j) -> p b j", b=DB), us[:, c, :, DS:DS + 2]))
                tell(cp(conv_tail[:, C - 1, 2:].rearrange("p (b j) -> p b j", b=DB), us[:, C - 1, :, DS:DS + 2]), S("conv_u"))
                dve.wait_ge(S("small_in"), 16 * 6)
                for c in range(C):
                    for y, u, gate in ((m["o"][:, HEADS + c, 0:SEQ], lambda j: up[:, c, j:j + SEQ], bg[:, c, 0:SEQ]),
                                       (m["o"][:, HEADS + c, SEQ:].rearrange("p (b t) -> p b t", b=DB), lambda j: us[:, c, :, j:j + DS],
                                        bg[:, c, SEQ:].rearrange("p (b t) -> p b t", b=DB))):
                        step(ts(y, u(0), convw[:, c, 0:1], None, ALU.mult))
                        step(stt(y, u(1), convw[:, c, 1:2], y, ALU.mult, ALU.add))
                        step(stt(y, u(2), convw[:, c, 2:3], y, ALU.mult, ALU.add))
                        step(tt(y, y, gate, ALU.mult))
                dve.wait_ge(S("conv_ps"), 2)
                tell(cp(conv_tok, ps[0:2 + 2 * DB, 1, :]), S("conv_out"))

            def halves(x, lv, upto):
                v = x[:, 0:upto].rearrange("p (n two h) -> p n two h", two=2, h=(1 << lv) // 2)
                return v[:, :, 0, :], v[:, :, 1, :]

            def mixer(l):
                m, dvc = MIX[l], DVC[l]
                nv = dvc * P
                dv = nv
                if l == 0:
                    conv(m)
                z = m["b"]
                dve.wait_ge(S("pipe_free"), number(("in", l)))
                dve.wait_ge(S("softplus"), count_at("softplus", l, 1))
                zf, tf = (x.rearrange("p h t -> p (h t)") for x in (z, m["tmp"]))
                if l == 0:
                    step(stt(tf, zf, 0.0, tf, ALU.min, ALU.subtract))
                    tell(tt(m["k"].rearrange("p h t -> p (h t)"), tf, zf, ALU.subtract), S("amz_ready"))
                    a = m["tmp"]
                    dve.wait_ge(S("k_ready"), 1)
                else:
                    step(stt(tf, zf, 0.0, tf, ALU.min, ALU.subtract))
                    step(ts(tf, tf, 1.0 / 16.0, None, ALU.mult))
                    a = m["tmp"]
                for h in range(HEADS):
                    step(dve.tensor_tensor_scan(m["b"][:, h, :], carry[:], a[:, h, :], 0.0, ALU.mult, ALU.add))
                for h in range(HEADS):
                    b, q, k, qk = m["b"][:, h, :], m["q"][:, h, :], m["k"][:, h, :], m["qk"]
                    s0 = m["s0"][h % len(m["s0"])]
                    if h:
                        dve.wait_ge(S("score_ps"), count_at("score_ps", l, TT * h))
                        dve.wait_ge(S("o_ps"), count_at("o_ps", l, h))
                    for lv in range(1, LEVELS):
                        upto, half = (NT if lv < SL else SEQ), (1 << lv) // 2
                        (bl, br), (el, er) = halves(b, lv, upto), halves(qk[:, lv - 1, :], lv, upto)
                        mid = bc(bl[:, :, half - 1:half], P, upto // (2 * half), half)
                        step(tt(el, mid, bl, ALU.subtract))
                        step(tt(er, br, mid, ALU.subtract))
                    bp = b[:, 0:SEQ].rearrange("p (t c) -> p t c", t=PT_)
                    bs = b[:, SEQ:].rearrange("p (b t) -> p b t", b=DB)
                    step(tt(m["kd"][:, 0:SEQ].rearrange("p (t c) -> p t c", t=PT_), bc(bp[:, :, P - 1:P], P, PT_, P), bp, ALU.subtract))
                    step(tt(m["kd"][:, SEQ:].rearrange("p (b t) -> p b t", b=DB), bc(bs[:, :, DS - 1:DS], P, DB, DS), bs, ALU.subtract))
                    step(cp(m["dec"][:, 0:PT_], bp[:, :, P - 1]))
                    tell(cp(m["dec"][:, PT_:], bs[:, :, DS - 1]), S("e_ready"))
                    dve.wait_ge(S("ex_ready"), count_at("ex_ready", l, h + 1))
                    step(tt(m["kd"], m["kd"], k, ALU.mult))
                    tell(tt(m["qd"], m["qd"], q, ALU.mult), S("kd_ready"))
                    for lv in range(1, LEVELS):
                        upto = NT if lv < SL else SEQ
                        (el, er), (kl, _), (_, qr) = halves(qk[:, lv - 1, :], lv, upto), halves(k, lv, upto), halves(q, lv, upto)
                        step(tt(el, el, kl, ALU.mult))
                        ins = tt(er, er, qr, ALU.mult)
                        if lv < LEVELS - 1:
                            step(ins)
                    tell(ins, S("qk_ready"))
                    for t in range(TT):
                        R, L, C = ROWS[t], (LEVELS if t < PT_ else SL), ROWS[t]
                        dve.wait_ge(S("score_ps"), count_at("score_ps", l, TT * h + t + 1))
                        if t < PT_:
                            src = ps[:, 2 * t:2 * t + 2, :].rearrange("p a (b c) -> p (a b) c", c=P)
                        else:
                            src = ps[0:NS, 4, 0:SL * NS].rearrange("p (a c) -> p a c", a=SL)
                        ms = m["ms"][0:R, 0:L, 0:C]
                        step(tt(ms, src, masks[0:R, 0:L, 0:C], ALU.mult))
                        tell(red(m["st"][0:R, t, 0:C], ms.rearrange("p l t -> p t l"), AX.X, ALU.add), S("st_ready"))
                    dve.wait_ge(S("ktok"), count_at("ktok", l, h + 1))
                    if h:
                        dve.wait_ge(S("ns_ps"), count_at("ns_ps", l, h))
                    elif l == 0:
                        dve.wait_ge(S("stores"), 32)
                    tell(tt(m["kexp"], bc(m["ktok"][0:NS, PT_:PT_ + 1, :], NS, DB, P), bc(bmask[:].unsqueeze(2), NS, DB, P), ALU.mult),
                         S("kexp"))
                    if h:
                        dve.wait_ge(S("state_out"), count_at("state_out", l, 32 * h))
                    dve.wait_ge(S("s_ps"), count_at("s_ps", l, h + 1))
                    dve.wait_ge(S("s1_ready"), count_at("s1_ready", l, h + 1))
                    step(stt(m["sf"], m["s1"], m["dec"][:, 1:2], ps[:, 7, nv:2 * nv], ALU.mult, ALU.add))
                    dve.wait_ge(S("ns_ps"), count_at("ns_ps", l, h + 1))
                    step(tt(s0, s0, bc(m["dec"][:, PT_:].unsqueeze(2), P, DB, nv), ALU.mult))
                    nb = DB * nv // HALF
                    tell(tt(s0.rearrange("p b v -> p (b v)"), s0.rearrange("p b v -> p (b v)"),
                            ps[:, 0:nb, :].rearrange("p a n -> p (a n)"), ALU.add), S("state_new"))
                    dve.wait_ge(S("ss_ps"), count_at("ss_ps", l, h + 1))
                    tell(ts(m["rs"], ps[:, 4, 0:NT], 1.0 / dv, RMS_EPS, ALU.mult, ALU.add), S("ms_ready"))
                    dve.wait_ge(S("root"), count_at("root", l, h + 1))
                    step(dve.reciprocal(m["rs"], m["rs"]))
                    for c in range(dvc):
                        o = m["o"][:, h * dvc + c, :]
                        step(stt(o, ps[:, 5 + c, 0:NT], gnorm[l][:, c:c + 1], m["rs"], ALU.mult, ALU.mult))
                        ins = tt(o, o, m["g"][:, h * dvc + c, :], ALU.mult)
                        if c < dvc - 1:
                            step(ins)
                    tell(ins, S("rms"))

            def norm(inst, src=None):
                dve.wait_ge(S("gb_in"), 32 * inst)
                i = 2 * ((inst - 1) // 3) + ((inst - 1) % 3)
                for t in range(TT):
                    R = ROWS[t]
                    x = X[0:R, t, :]
                    if src is None:
                        if t < TT - 1:
                            dve.wait_ge(S("mix_done"), 2 * (TT - 1) * i + (TT - 1) + t + 1)
                        else:
                            dve.wait_ge(S("mix_unit"), 2 * i + 2)
                        y = ps[0:R, 2 * t:2 * t + 2, :].rearrange("p a n -> p (a n)")
                    else:
                        y = src[0:R, t, :]
                    step(stt(x, x, ALPHA, y, ALU.mult, ALU.add))
                    for j in range(2):
                        step(dve.bn_stats(stat[0:R, j, :], x[:, j * HALF:(j + 1) * HALF]))
                    step(dve.bn_aggr(mv[0:R, 0:2], stat[0:R].rearrange("p a b -> p (a b)")))
                    tell(ts(mv[0:R, 2:3], mv[0:R, 1:2], LN_EPS, None, ALU.add), S("var_ready"))
                    dve.wait_ge(S("std_ready"), 3 * (inst - 1) + t + 1)
                    step(dve.reciprocal(mv[0:R, 3:4], mv[0:R, 2:3]))
                    step(ts(x, x, mv[0:R, 0:1], mv[0:R, 3:4], ALU.subtract, ALU.mult))
                    step(tt(x, x, GB[0:R, 0, :], ALU.mult))
                    tell(tt(x, x, GB[0:R, 1, :], ALU.add), S("ln_done"))

            def attention(l):
                def keys(n, dst):
                    for j in (2, 3):
                        dve.wait_ge(S("kt_full"), count_at("kt_full", l, 4 * n + j + 1))
                        tell(cp(dst[:, 2 * j:2 * j + 2, :].rearrange("p c m -> p (c m)"), ps[:, j, :]), S("kt_d"))

                keys(0, KTP)
                for b in range(DB):
                    if b >= 2:
                        dve.wait_ge(S("ssc"), count_at("ssc", l, b - 1))
                    keys(b + 1, KT[b % 2])
                dve.wait_ge(S("ss_rows"), count_at("ss_rows", l, 1))
                step(red(small[:, 0, 1:2], ps[:, 5, 0:MEM], AX.X, ALU.max))
                tell(ts(small[:, 0, 0:1], small[:, 0, 1:2], -1.0, None, ALU.mult), S("smax"))
                dve.wait_ge(S("sexp"), count_at("sexp", l, 1))
                step(dve.reciprocal(small[:, 1, 1:2], small[:, 1, 0:1]))
                tell(ts(SS, SS, small[:, 1, 1:2], None, ALU.mult), S("sp_ready"))
                for t in range(PT_):
                    dve.wait_ge(S("psc"), count_at("psc", l, t + 1))
                    step(red(small[:, 4, 0:MH], ps[:, 2 * t:2 * t + 2, :].rearrange("p a (b m) -> p (a b) m", m=MEM), AX.X, ALU.max))
                    tell(ts(small[:, 2, 0:MH], small[:, 4, 0:MH], -1.0, None, ALU.mult), S("pmax"))
                    dve.wait_ge(S("pexp"), count_at("pexp", l, t + 1))
                    step(dve.reciprocal(small[:, 5, 0:MH], small[:, 3, 0:MH]))
                    tell(tt(PR, PR, bc(small[:, 5, 0:MH].unsqueeze(2), P, MH, MEM), ALU.mult), S("pr_ready"))

            def one_hot(dst, src, mx, n):
                step(red(mx, src, AX.X, ALU.max))
                step(tt(dst, src, bc(mx.unsqueeze(2), P, TT, n), ALU.is_equal))
                step(tt(dst, dst, bc(rev[:, 0:n].unsqueeze(1), P, TT, n), ALU.mult))
                step(red(small[:, 15, 0:TT], dst, AX.X, ALU.max))
                step(tt(dst, dst, bc(small[:, 15, 0:TT].unsqueeze(2), P, TT, n), ALU.is_equal))

            def moe(l):
                gm, m1, m2, dif, gw, w1, w2 = (small[:, n, 0:TT] for n in (4, 5, 7, 6, 8, 9, 10))
                dve.wait_ge(S("memv_out"), 16 * (l + 1))
                dve.wait_ge(S("router_in"), 16 * (GROUPS + 3) * (l + 1))
                step(dve.memset(LG, 0.0))
                dve.wait_ge(S("logits"), count_at("logits", l, 1))
                for t in range(TT):
                    R = ROWS[t]
                    step(tt(LG[0:R, t, :], ps[0:R, 0, t * 64:t * 64 + GROUPS + NE], router_b[0:R, :], ALU.add))
                one_hot(OHG, LG[:, :, 0:GROUPS], gm, GROUPS)
                step(tt(GE, LG[:, :, 0:GROUPS], bc(gm.unsqueeze(2), P, TT, GROUPS), ALU.subtract))
                for t in range(TT):
                    step(tt(EM[:, t, :, :], LG[:, t, GROUPS:].rearrange("p (g e) -> p g e", g=GROUPS),
                            bc(OHG[:, t, :].unsqueeze(2), P, GROUPS, EPG), ALU.mult))
                    step(red(SEL[:, t, :], EM[:, t, :, :].rearrange("p g e -> p e g"), AX.X, ALU.add))
                one_hot(OH1, SEL, m1, EPG)
                flat = [x.rearrange("p t e -> p (t e)") for x in (SEL, OH1)]
                step(stt(flat[0], flat[1], -3.0e38, flat[0], ALU.mult, ALU.add))
                one_hot(OH2, SEL, m2, EPG)
                tell(tt(dif, m2, m1, ALU.subtract), S("gdiff"))
                dve.wait_ge(S("gexp"), count_at("gexp", l, 1))
                step(red(gw, GE, AX.X, ALU.add))
                step(ts(w1, dif, 1.0, None, ALU.add))
                step(tt(w1, w1, gw, ALU.mult))
                step(dve.reciprocal(w1, w1))
                step(tt(w2, w1, dif, ALU.mult))
                step(tt(AS8, OH1, OH2, ALU.add))
                step(tt(OH1, OH1, bc(w1.unsqueeze(2), P, TT, EPG), ALU.mult))
                step(tt(OH2, OH2, bc(w2.unsqueeze(2), P, TT, EPG), ALU.mult))
                step(tt(WE8, OH1, OH2, ALU.add))
                step(tt(OHG, OHG, bc(valid[:].unsqueeze(2), P, TT, GROUPS), ALU.mult))
                for t in range(TT):
                    og = bc(OHG[:, t, :].unsqueeze(2), P, GROUPS, EPG)
                    for dst, src in ((ASG, AS8), (CMB, WE8)):
                        step(tt(dst[:, t, :].rearrange("p (g e) -> p g e", g=GROUPS), og, bc(src[:, t:t + 1, :], P, GROUPS, EPG), ALU.mult))
                step(dve.memset(ACC, 0.0))
                tell(dve.memset(small[:, 15, :], 0.0), S("assigned"))
                dve.wait_ge(S("ranks"), count_at("ranks", l, 1))
                step(red(small[:, 11, 0:1], ps[:, 1, TT * NE:(TT + 1) * NE], AX.X, ALU.max))
                step(ts(THR, iota[:, 1:1 + (NT - 1) // CAP], float(CAP), small[:, 11, 0:1], ALU.mult, ALU.is_lt))
                step(red(small[:, 12, 0:1], THR, AX.X, ALU.add))
                key = KEY.rearrange("p t e -> p (t e)")
                for t in range(TT):
                    step(stt(KEY[:, t, 0:NE], ps[:, 1, t * NE:(t + 1) * NE], 1.0, ASG[:, t, :], ALU.add, ALU.mult))
                step(ts(KEY[:, :, 0:NE], KEY[:, :, 0:NE], -1.0, None, ALU.add))
                step(ts(KEY[:, :, NE:], KEY[:, :, 0:2], -float(CAP), None, ALU.add))
                for n, free in enumerate(("xg_ps1", "pwt_ps", "ht", "h_ready")):
                    tell(dve.memset(small[:, 13, n:n + 1], 0.0), S(f"{free}{l}"))
                tell(dve.memset(PWT, 0.0), S(f"pwt_sb{l}"))
                tell(dve.memset(Y, 0.0), S(f"y_sb{l}"))
                tell(cp(rounds[:], small[0:1, 12, 0:1]), S("rounds_known"))
                rm1 = dve.value_load(rounds[0:1, 0:1], min_val=0, max_val=4)
                io = bc(iota[:, 0:CAP].unsqueeze(1), P, 2, CAP)

                def one_hots(e):
                    for t in range(TT):
                        k2 = KEY[:, t, e].unsqueeze(2)
                        tt(PG[:, t, :, :], io, bc(k2, P, 2, CAP), ALU.is_equal).then_inc(S(f"pg_part{l}"), 1)

                def move_gathered(it):
                    dve.wait_ge(S(f"xg_ps1{l}"), it + 2)
                    cp(XG[:, 4:8, :].rearrange("p k c -> p (k c)"), ps[:, 1, :]).then_inc(S(f"xg_d{l}"), 1)

                one_hots(slice(0, 2))
                move_gathered(0)
                with dve.Fori(0, rm1 + 1) as rd:
                    with dve.Fori(0, PAIRS) as p:
                        it = rd * PAIRS + p
                        dve.wait_ge(S(f"pg_part{l}"), it * TT + TT)
                        dve.wait_ge(S(f"pwt_ps{l}"), it + 1)
                        for t in range(TT):
                            w2e = CMB[:, t, bass.ds(p * 2, 2)].unsqueeze(2)
                            tt(PW[:, t, :, :], PG[:, t, :, :], bc(w2e, P, 2, CAP), ALU.mult).then_inc(S(f"pw_part{l}"), 1)
                        dve.wait_ge(S(f"pw_part{l}"), it * TT + TT)
                        dve.wait_ge(S(f"xg_ps1{l}"), it + 2)
                        one_hots(bass.ds(p * 2 + 2, 2))
                        dve.wait_ge(S(f"sg{l}"), it + 1)
                        dve.wait_ge(S(f"up_done{l}"), it + 1)
                        tt(HS, SG, ps[:, 3, :], ALU.mult).then_inc(S(f"h_ready{l}"), 1)
                        move_gathered(it + 1)
                        for n in range(2 * TT):
                            t, j = n // 2, n % 2
                            dve.wait_ge(S(f"scat{l}"), it * (2 * TT) + (n + 1))
                            a = ACC[0:ROWS[t], t, j * HALF:(j + 1) * HALF]
                            tt(a, a, ps[0:ROWS[t], 7 - n % 2, :], ALU.add).then_inc(S(f"acc{l}"), 1)
                    dve.wait_ge(S(f"pg_part{l}"), rd * (PAIRS * TT) + (PAIRS + 1) * TT)
                    ts(key, key, -float(CAP), None, ALU.add).then_inc(S(f"round_end{l}"), 1)
                    dve.wait_ge(S(f"round_end{l}"), rd + 1)
                for n in range(2 * TT):
                    t, j = n // 2, n % 2
                    dve.wait_ge(S(f"scat{l}"), rm1 * (PAIRS * 2 * TT) + (PAIRS * 2 * TT + n + 1))
                    a = ACC[0:ROWS[t], t, j * HALF:(j + 1) * HALF]
                    tt(a, a, ps[0:ROWS[t], 7 - n % 2, :], ALU.add).then_inc(S(f"acc{l}"), 1)
                dve.wait_ge(S(f"acc{l}"), rm1 * (PAIRS * 2 * TT) + (PAIRS + 1) * 2 * TT)

            dve.wait_ge(S("iota_ps"), 1)
            step(cp(iota[:], ps[:, 0, 0:P]))
            tell(ts(rev[:], iota[:, 0:EPG], -1.0, float(EPG), ALU.mult, ALU.add), S("iota_ready"))
            for l in range(DEPTH):
                mixer(l)
                norm(1 + 3 * l)
                attention(l)
                norm(2 + 3 * l)
                moe(l)
                norm(3 + 3 * l, ACC)


_INS = ["x_prompt", "x_sample", "state_hgrn", "state_conv", "state_gla", "cache_mem_k", "cache_mem_v", "mem_prompt",
        "w_in_a", "lb_a", "conv_w", "gnorm_a", "w_out_a", "w_in_c", "w_gk2", "b_gk2", "gnorm_c", "w_out_c",
        "w_mq", "w_mk", "w_mv", "w_mo", "ln_g", "ln_b", "w_grp", "b_grp", "w_er", "b_er", "w_gate", "w_up", "w_down"]


def kernel(**inputs):
    import numpy as _np
    import concourse.bacc as _bacc
    from concourse.bass_utils import run_bass_kernel_spmd as _run

    nc = _bacc.Bacc("TRN2", target_bir_lowering=False, num_devices=1)
    arrays, I, O = {}, {}, {}
    for name in _INS:
        a = _np.ascontiguousarray(inputs[name])
        arrays[f"in_{name}"] = a
        I[name] = nc.dram_tensor(f"in_{name}", a.shape, mybir.dt.from_np(a.dtype), kind="ExternalInput").ap()
    like = {k: inputs[k].shape for k in _INS}
    depth, _, mem, mh, mhd = like["cache_mem_k"]
    outs = [
        ("y_prompt", like["x_prompt"]), ("y_sample", like["x_sample"]),
        ("hgrn_p", (like["state_hgrn"][0], 1) + tuple(like["state_hgrn"][2:])),
        ("conv_p", (like["state_conv"][0], 1) + tuple(like["state_conv"][2:])),
        ("gla_p", (like["state_gla"][0], 1) + tuple(like["state_gla"][2:])),
        ("mem_k", (depth, 1, mem, mh, mhd)), ("mem_v", (depth, 1, mem, mh, mhd)),
        ("hgrn_s", like["state_hgrn"]), ("conv_s", like["state_conv"]), ("gla_s", like["state_gla"]),
    ]
    for name, shape in outs:
        O[name] = nc.dram_tensor(f"out_{name}", tuple(shape), F32, kind="ExternalOutput").ap()
    build(nc, I, O)
    r = _run(nc, [arrays], core_ids=[0])
    return tuple(r.results[0][f"out_{name}"] for name, _ in outs)
```

```python
from contextlib import ExitStack

import concourse.bass as bass
from concourse import mybir

ALU = mybir.AluOpType
ACT = mybir.ActivationFunctionType
AX = mybir.AxisListType
F32 = mybir.dt.float32
I32 = mybir.dt.int32
P = 128


class Steps:

    def __init__(self, eng, own, base=0):
        self.eng, self.own, self.base, self.n, self.told = eng, own, base, 0, {}

    def step(self, ins):
        self.n += 1
        ins.then_inc(self.own, 1)
        self.eng.wait_ge(self.own, self.base + self.n)

    def tell(self, ins, sem, base=0):
        self.told[sem.name] = self.told.get(sem.name, 0) + 1
        ins.then_inc(sem, 1)
        self.eng.wait_ge(sem, base + self.told[sem.name])


def build(nc, I, O):
    _, SEQ, D = I["x_prompt"].shape
    DB, DS, _ = I["x_sample"].shape
    NA, _, HEADS, DK, HDV = I["state_hgrn"].shape
    NC_, GDV = I["state_gla"].shape[0], I["state_gla"].shape[4]
    DEPTH, _, MEM, MH, MHD = I["cache_mem_k"].shape
    GROUPS, EPG, _, DE = I["w_gate"].shape[1:]
    CW = I["conv_w"].shape[1]
    NE = GROUPS * EPG
    KC = D // P
    NS = DB * DS
    NT = SEQ + NS
    PT_ = SEQ // P
    ROWS = [P] * PT_ + [NS]
    TT = len(ROWS)
    HALF = 512
    SLOTS = 6
    CAP = 64
    PAIRS = NE // 2
    LEVELS = 8
    SL = 3
    MT_ = MEM // P
    RANK = I["w_gk2"].shape[1]
    ALPHA = (2.0 * DEPTH) ** 0.25
    LN_EPS, RMS_EPS = 1e-5, 1e-6
    assert NA == 1 and NC_ == 1 and DEPTH == 2 and PT_ == 2 and DK == P and DS == 4 and D == 1024
    DVC = [HDV // P, GDV // P]

    def cols(t):
        return slice(t * P, t * P + ROWS[t])

    ctx = ExitStack()
    with ctx:
        sems = {}

        def S(name):
            if name not in sems:
                sems[name] = ctx.enter_context(nc.semaphore(name))
            return sems[name]

        def sb(name, shape, dt=F32):
            return ctx.enter_context(nc.sbuf_tensor(name, shape, dt))

        ident = sb("ident", [P, P])
        ones = sb("ones", [P, P])
        masks = sb("masks", [P, LEVELS, P])
        upper = sb("upper", [P, P])
        iota = sb("iota", [P, P])
        bmask = sb("bmask", [P, DB])
        carry = sb("carry", [P, NT])
        valid = sb("valid", [P, TT])
        W = sb("W", [P, SLOTS, KC * HALF])
        X = sb("X", [P, TT, D])
        XT = sb("XT", [P, KC, NT])
        GB = sb("GB", [P, 2, D])
        convw = sb("convw", [P, CW // P, 3])
        gnorm = [sb(f"gnorm{l}", [P, DVC[l]]) for l in range(2)]
        wgz = sb("wgz", [P, KC, RANK])
        wgk2 = sb("wgk2", [RANK, HEADS * DK])
        bgk2 = sb("bgk2", [P, HEADS])
        gz = sb("gz", [RANK, NT])
        router_w = sb("router_w", [P, KC, GROUPS + NE])
        router_b = sb("router_b", [P, GROUPS + NE])
        stat = sb("stat", [P, 2, 6])
        mv = sb("mv", [P, 4])
        small = sb("small", [P, 16, 4])
        rev = sb("rev", [P, EPG])
        rounds = sb("rounds", [1, 1], I32)
        SCR_WORDS = nc.sbuf_bytes_remaining // 4 - 8
        scr = sb("scr", [P, SCR_WORDS])
        ps = ctx.enter_context(nc.psum_tensor("ps", [P, 8, HALF], F32))

        class Region:

            def __init__(self):
                self.at = 0

            def take(self, *shape, rows=P):
                n = 1
                for x in shape:
                    n *= x
                assert self.at + n <= SCR_WORDS, (self.at + n, SCR_WORDS)
                v = scr[0:rows, self.at:self.at + n]
                self.at += n
                if len(shape) == 2:
                    v = v.rearrange("p (a b) -> p a b", a=shape[0])
                if len(shape) == 3:
                    v = v.rearrange("p (a b c) -> p a b c", a=shape[0], b=shape[1])
                return v

        MIX = []
        for l in range(2):
            r, nv = Region(), DVC[l] * P
            m = dict(q=r.take(HEADS, NT), k=r.take(HEADS, NT), b=r.take(HEADS, NT),
                     g=r.take(HEADS * DVC[l], NT), v=r.take(TT, HEADS * nv),
                     qkd=r.take(2 * NT), kexp_all=r.take(DB * P),
                     o=r.take(KC, NT), ktok=r.take(TT, P), sq=r.take(DVC[l], NT), rs=r.take(NT),
                     s1=r.take(nv), sf=r.take(nv), dec=r.take(DB + PT_),
                     s0=r.take(DB, nv))
            m["qd"] = m["qkd"][:, 0:NT]
            m["conv_rows"] = m["qkd"][:, 0:CW]
            m["kexp"] = m["kexp_all"][0:NS, :].rearrange("p (b d) -> p b d", b=DB)
            mark = r.at
            m["ms"], m["st"] = r.take(LEVELS, P), r.take(TT, P)
            spare = GB[:, :, :].rearrange("p a d -> p (a d)")
            m["qk"] = [XT[:, 0:LEVELS - 1, :], spare[:, 0:(LEVELS - 1) * NT].rearrange("p (v t) -> p v t", v=LEVELS - 1)]
            m["kd"] = [m["qkd"][:, NT:2 * NT], XT[:, LEVELS - 1, :]]
            m["dec"] = [m["dec"], spare[:, (LEVELS - 1) * NT:(LEVELS - 1) * NT + DB + PT_]]
            m["tmp"] = m["o"][:, 0:HEADS, :]
            if l == 0:
                m["conv"] = [r.take(CW // P, NT) for _ in range(3)]
                r.at = mark
                m["up"], m["us"] = r.take(CW // P, SEQ + 2), r.take(CW // P, DB, 6)
            MIX.append(m)
        def halves(x, lv, upto):
            v = x[:, 0:upto].rearrange("p (n two h) -> p n two h", two=2, h=(1 << lv) // 2)
            return v[:, :, 0, :], v[:, :, 1, :]

        conv_in = MIX[0]["conv_rows"][0:2 * DB, :]
        conv_tok = MIX[0]["kexp_all"][0:2 + 2 * DB, 0:CW]
        conv_tail = MIX[0]["s1"][:, 0:(CW // P) * (2 + 2 * DB)].rearrange("p (c n) -> p c n", c=CW // P)
        r = Region()
        QT, KTP, VP = r.take(KC, NT), r.take(KC, MEM), r.take(MT_, D)
        KV = [r.take(MT_, D) for _ in range(3)]
        KT0 = r.take(KC, MEM)
        at = r.at
        PR = r.take(MH, MEM)
        PRT = r.take(MT_, MH * P)
        r.at = at
        KT = [KT0, r.take(KC, MEM)]
        SS, SST = r.take(MEM), r.take(MT_, P)
        OA = XT
        r = Region()
        LG, OHG, GE = r.take(TT, GROUPS + NE), r.take(TT, GROUPS), r.take(TT, GROUPS)
        SEL, OH1, OH2, WE8, AS8 = (r.take(TT, EPG) for _ in range(5))
        EM, THR = r.take(TT, GROUPS, EPG), r.take((NT - 1) // CAP)
        ASG, CMB, KEY = r.take(TT, NE), r.take(TT, NE), r.take(TT, NE + 2)
        PG, PW, PWT = r.take(TT, 2, CAP), r.take(TT, 2, CAP), r.take(NT)
        XG, SG, HS, HT = r.take(KC, P), r.take(DE), r.take(DE), r.take(DE // P, P)
        Y, ACC = r.take(D), r.take(TT, D)

        def unit_cols(w, a):
            return w[:, a:a + HALF].rearrange("(k p) n -> p k n", p=P)

        wia, woa, wic, woc = I["w_in_a"][0], I["w_out_a"][0], I["w_in_c"][0], I["w_out_c"][0]
        F = HEADS * DK
        in_cols = [
            [("bg", 4 * F), ("cg", 5 * F), ("h", 6 * F), ("f", F), ("q", 0), ("g", 3 * F), ("v", 2 * F)],
            [("q", 0), ("k", F), ("g", 4 * F), ("g1", 5 * F), ("v", 2 * F), ("v1", 3 * F)],
        ]
        units = []
        for l in range(DEPTH):
            while len(units) % SLOTS:
                units.append(None)
            for name, a in in_cols[l]:
                units.append((l, name, unit_cols([wia, wic][l], a)))
            for j in range(2):
                units.append((l, f"out{j}", unit_cols([woa, woc][l], j * HALF)))
            for name in ("mk", "mv", "mq", "mo"):
                for j in range(2):
                    units.append((l, f"{name}{j}", unit_cols(I[f"w_{name}"][l], j * HALF)))
        UNIT = {u[:2]: n for n, u in enumerate(units) if u}

        def wslot(l, name):
            return W[:, UNIT[l, name] % SLOTS, :].rearrange("p (k n) -> p k n", k=KC)

        def loads_in(n):
            return sum(1 for m in range(n % SLOTS, n + 1, SLOTS) if units[m])

        def unit_landed(eng, l, name):
            n = UNIT[l, name]
            eng.wait_ge(S(f"w_in{n % SLOTS}"), 16 * loads_in(n))

        jobs = {}
        order = []

        def plan(stage, *names):
            jobs.setdefault(stage, [])
            for name in names:
                jobs[stage].append((len(order), name))
                order.append((stage, name))

        def plan_xt(inst):
            plan(("xt", inst), *[("xt", t, h) for t in range(TT) for h in range(2)])

        plan_xt(0)
        for l in range(DEPTH):
            for name, _ in in_cols[l]:
                if name[0] != "v":
                    plan(("in", l), *[("feat", name, c) for c in range(4)])
            if l == 1:
                plan(("in", l), ("gz", "gz", 0), *[("gk", "gk", c) for c in range(4)])
            for name, _ in in_cols[l]:
                if name[0] == "v":
                    plan(("in", l), *[("tok", name, t) for t in range(TT)])
            plan(("mem", l), *[("mt", i, h) for i in range(MT_) for h in range(2)])
            plan(("mem", l), *[("memtok", f"{w}{j}", i) for w in ("mk", "mv") for j in range(2) for i in range(MT_)])
            plan_xt(1 + 3 * l)
            plan(("mq", l), *[("feat", f"mq{j}", c) for j in range(2) for c in range(4)])
            plan_xt(2 + 3 * l)
            if l + 1 < DEPTH:
                plan_xt(3 + 3 * l)

        def number(stage, name=None):
            return max(n for n, j in jobs[stage] if name is None or j[1] == name) + 1

        def kv_loads(l, i):
            return l * len(range(i % 3, 2 * DB, 3)) + i // 3 + 1

        per_layer = dict(
            softplus=1, b_ready=HEADS, e_ready=HEADS, qd_exp=HEADS, qd_ready=HEADS, ex_ready=HEADS, ktok_ps=HEADS, ktok=HEADS, s_ps=HEADS,
            s1_ready=HEADS, o_ps=HEADS, sq_ready=HEADS, ms_ready=HEADS, root=HEADS, score_ps=TT * HEADS,
            kd_ready=HEADS, qk_ready=HEADS, st_ready=TT * HEADS, kexp=HEADS, ns_ps=HEADS, ss_ps=HEADS,
            rms=HEADS, state_new=HEADS, state_out=32 * HEADS, kt_full=4 * (DB + 1), kt_a=2 * (DB + 1), kt_d=2
            * (DB + 1), ssc=DB, ssel=DB, osel=DB, os_ps=1, smax=1, sexp=1, sp_ready=1, spt_ps=1, spt_sb=1, psc=PT_,
            pmax=PT_, pexp=PT_, pr_ready=PT_, prt_ps=PT_, prt_sb=PT_, po_ps=PT_, oa_ready=TT, pv_done=DB,
            memk_out=16, logits=1, assigned=1, ranks=1, rounds_known=1, gdiff=1, gexp=1)

        def count_at(name, l, n):
            return l * per_layer[name] + n

        LNS = 3 * DEPTH
        mem_src = I["mem_prompt"][0].rearrange("(i p) d -> p i d", p=P)
        EXPERT_UNITS = ("gate", "up", "down")
        gate_rows = I["w_gate"].rearrange("l g e (k p) f -> (l g e) p k f", p=P)
        up_rows = I["w_up"].rearrange("l g e (k p) f -> (l g e) p k f", p=P)
        down_rows = I["w_down"].rearrange("l g e (k p) d -> (l g e) p k d", p=P)

        block = ctx.enter_context(nc.Block())

        @block.sync
        def _(sp):
            for t in range(PT_):
                sp.dma_start(X[:, t, :], I["x_prompt"][0, t * P:(t + 1) * P, :]).then_inc(S("x_in"), 16)
            sp.dma_start(X[0:NS, PT_, :], I["x_sample"].rearrange("b t d -> (b t) d")).then_inc(S("x_in"), 16)

            def used(n):
                l, name = units[n][:2]
                if name.startswith("out") or name.startswith("mo"):
                    i = 2 * l + (name[:2] == "mo")
                    sp.wait_ge(S("mix_unit"), 2 * i + int(name[-1]) + 1)
                else:
                    stage = ("in", l) if name[:2] not in ("mk", "mv", "mq") else ("mq", l) if name[:2] == "mq" else ("mem", l)
                    sp.wait_ge(S("pipe_full"), number(stage, name))

            n = 0
            rm1 = None
            for l in range(DEPTH):
                end = max(UNIT[k] for k in UNIT if k[0] == l) + 1
                start = min(UNIT[k] for k in UNIT if k[0] == l)
                s_in = (I["state_hgrn"], I["state_gla"])[l][0].rearrange("b h k v -> h k b v")
                s_out = O[("hgrn_s", "gla_s")[l]][0].rearrange("b h k v -> h k b v")
                p_out = O[("hgrn_p", "gla_p")[l]][0, 0]
                for n in range(start, end):
                    if n == start + SLOTS:
                        if l:
                            sp.wait_ge(S("ln_done"), 9 * l)
                        sp.dma_start(MIX[l]["s0"], s_in[0]).then_inc(S(f"s0_in{l}"), 16)
                    if n == UNIT[l, "out0"] + SLOTS:
                        for h in range(HEADS):
                            sp.wait_ge(S("state_new"), count_at("state_new", l, h + 1))
                            sp.dma_start(s_out[h], MIX[l]["s0"]).then_inc(S("state_out"), 16)
                            sp.dma_start(p_out[h], MIX[l]["sf"]).then_inc(S("state_out"), 16)
                            if h + 1 < HEADS:
                                sp.wait_ge(S("state_out"), count_at("state_out", l, 32 * (h + 1)))
                                sp.dma_start(MIX[l]["s0"], s_in[h + 1]).then_inc(S(f"s0_in{l}"), 16)
                    if n - SLOTS >= start:
                        used(n - SLOTS)
                    elif l:
                        sp.wait_ge(S(f"{EXPERT_UNITS[n % SLOTS // 2]}_done{l - 1}"), rm1 * PAIRS + PAIRS)
                    sp.dma_start(W[:, n % SLOTS, :].rearrange("p (k n) -> p k n", k=KC), units[n][2]).then_inc(S(f"w_in{n % SLOTS}"), 16)

                def load_expert_unit(s, e):
                    base = (gate_rows, up_rows, down_rows)[s // 2]
                    sp.dma_start(W[:, s, :].rearrange("p (k n) -> p k n", k=(KC if s < 4 else DE // P)), base[e]).then_inc(S(f"e_in{l}_{s}"), 16)

                caches = [I[name][l, b].rearrange("(i p) h d -> p i (h d)", p=P) for name in ("cache_mem_k", "cache_mem_v") for b in range(DB)]
                for i in range(2 * DB):
                    if i == 0:
                        sp.wait_ge(S("pipe_full"), jobs[("mem", l)][2 * MT_ - 1][0] + 1)
                    elif i == 1:
                        sp.wait_ge(S("pipe_free"), number(("mem", l)))
                    elif i < DB + 3:
                        if i == 2:
                            sp.wait_ge(S("memk_out"), count_at("memk_out", l, 16))
                        sp.wait_ge(S("kt_full"), count_at("kt_full", l, 4 * (i - 1)))
                    else:
                        sp.wait_ge(S("pv_done"), count_at("pv_done", l, i - 3 - DB + 1))
                    sp.dma_start(KV[i % 3], caches[i]).then_inc(S(f"kv_in{i % 3}"), 16)

                for n in range(end - SLOTS, end):
                    used(n)
                    load_expert_unit(n % SLOTS, l * NE + n % SLOTS % 2)
                sp.wait_ge(S("rounds_known"), count_at("rounds_known", l, 1))
                rm1 = sp.value_load(rounds[0:1, 0:1], min_val=0, max_val=4)
                with sp.Fori(0, rm1 * PAIRS + (PAIRS - 1)) as i:
                    nxt = (i + 1) % PAIRS
                    for s in range(SLOTS):
                        if s % 2 == 0:
                            sp.wait_ge(S(f"{EXPERT_UNITS[s // 2]}_done{l}"), i + 1)
                        load_expert_unit(s, nxt * 2 + (l * NE + s % 2))

        @block.gpsimd
        def _(pool):
            st = Steps(pool, S("pool_step"))
            st.step(pool.memset(ones[:], 1.0))
            st.step(pool.affine_select(out=ident[:], in_=ones[:], compare_op=ALU.is_equal, fill=0.0, base=0,
                                       pattern=[[1, P]], channel_multiplier=-1))
            st.step(pool.affine_select(out=upper[:], in_=ones[:], compare_op=ALU.is_gt, fill=0.0, base=0,
                                       pattern=[[1, P]], channel_multiplier=-1))
            st.step(pool.memset(masks[:], 0.0))
            st.step(pool.tensor_copy(masks[:, 0, :], ident[:]))
            for lv in range(1, LEVELS):
                B = 1 << lv
                right = masks[:, lv, :].rearrange("p (n two h) -> p n two h", two=2, h=B // 2)[:, :, 1, :]
                one = ones[:].rearrange("p (n two h) -> p n two h", two=2, h=B // 2)[:, :, 1, :]
                st.step(pool.affine_select(out=right, in_=one, compare_op=ALU.is_ge, fill=0.0, base=0,
                                           pattern=[[-B, P // B], [0, B // 2]], channel_multiplier=1))
                st.step(pool.affine_select(out=right, in_=right, compare_op=ALU.is_ge, fill=0.0, base=B // 2 - 1,
                                           pattern=[[B, P // B], [0, B // 2]], channel_multiplier=-1))
            for j in range(MH):
                quarter = bmask[j * NS:(j + 1) * NS, :]
                st.step(pool.affine_select(out=quarter, in_=ones[j * NS:(j + 1) * NS, 0:DB], compare_op=ALU.is_ge, fill=0.0, base=0,
                                           pattern=[[-DS, DB]], channel_multiplier=1))
                st.step(pool.affine_select(out=quarter, in_=quarter, compare_op=ALU.is_ge, fill=0.0, base=DS - 1,
                                           pattern=[[DS, DB]], channel_multiplier=-1))
            st.step(pool.memset(carry[:], 1.0))
            st.step(pool.memset(carry[:, 0:SEQ].rearrange("p (t c) -> p t c", c=P)[:, :, 0], 0.0))
            st.step(pool.memset(carry[:, SEQ:NT].rearrange("p (b t) -> p b t", t=DS)[:, :, 0], 0.0))
            st.step(pool.memset(valid[:], 1.0))
            st.step(pool.memset(valid[:, TT - 1:TT], 0.0))
            pool.memset(valid[0:NS, TT - 1:TT], 1.0).then_inc(S("consts"), 1)

            def load(dst, src, sem):
                pool.dma_start(dst, src, allow_slow_non_contiguous=True).then_inc(S(sem), 16)

            load(convw[:], I["conv_w"][0].rearrange("(c p) j -> p c j", p=P), "small_in")
            for l in range(2):
                load(gnorm[l][:], I[("gnorm_a", "gnorm_c")[l]][0].rearrange("(c p) -> p c", p=P), "small_in")
            load(wgz[:], wic[:, 6 * F:6 * F + RANK].rearrange("(k p) n -> p k n", p=P), "small_in")
            load(wgk2[:], I["w_gk2"][0], "small_in")
            load(bgk2[:], I["b_gk2"][0].rearrange("(c p) -> p c", p=P), "small_in")

            for l in range(DEPTH):
                m = MIX[l]
                if l == 0:
                    load(conv_in, I["state_conv"][0].rearrange("b j w -> (b j) w"), "conv_in")
                    pool.wait_ge(S("conv_out"), 1)
                    pool.dma_start(O["conv_p"][0, 0], conv_tok[0:2, :]).then_inc(S("stores"), 16)
                    pool.dma_start(O["conv_s"][0].rearrange("b j w -> (b j) w"), conv_tok[2:2 + 2 * DB, :]).then_inc(S("stores"), 16)
                tt = pool.tensor_tensor

                def exponents(h):
                    b, qk, kd, dec = m["b"][:, h, :], m["qk"][h % 2], m["kd"][h % 2], m["dec"][h % 2]
                    pool.wait_ge(S("b_ready"), count_at("b_ready", l, h + 1))
                    if h >= 2:
                        pool.wait_ge(S("state_new"), count_at("state_new", l, h - 1))
                    for lv in range(1, LEVELS):
                        upto, half = (NT if lv < SL else SEQ), (1 << lv) // 2
                        (bl, br), (el, er) = halves(b, lv, upto), halves(qk[:, lv - 1, :], lv, upto)
                        mid = bl[:, :, half - 1:half].to_broadcast([P, upto // (2 * half), half])
                        tt(el, mid, bl, ALU.subtract)
                        tt(er, br, mid, ALU.subtract)
                    bp = b[:, 0:SEQ].rearrange("p (t c) -> p t c", t=PT_)
                    bs = b[:, SEQ:].rearrange("p (b t) -> p b t", b=DB)
                    tt(kd[:, 0:SEQ].rearrange("p (t c) -> p t c", t=PT_), bp[:, :, P - 1:P].to_broadcast([P, PT_, P]), bp, ALU.subtract)
                    tt(kd[:, SEQ:].rearrange("p (b t) -> p b t", b=DB), bs[:, :, DS - 1:DS].to_broadcast([P, DB, DS]), bs, ALU.subtract)
                    pool.tensor_copy(dec[:, 0:PT_], bp[:, :, P - 1])
                    st.tell(pool.tensor_copy(dec[:, PT_:], bs[:, :, DS - 1]), S("e_ready"))

                exponents(0)
                for h in range(HEADS):
                    if h + 1 < HEADS:
                        exponents(h + 1)
                    pool.wait_ge(S("ktok"), count_at("ktok", l, h + 1))
                    if h:
                        pool.wait_ge(S("ns_ps"), count_at("ns_ps", l, h))
                    elif l == 0:
                        pool.wait_ge(S("stores"), 32)
                    st.tell(tt(m["kexp"], m["ktok"][0:NS, PT_:PT_ + 1, :].to_broadcast([NS, DB, P]),
                               bmask[0:NS].unsqueeze(2).to_broadcast([NS, DB, P]), ALU.mult), S("kexp"))
                pool.wait_ge(S("state_out"), count_at("state_out", l, 32 * HEADS))

                pool.wait_ge(S("mix_unit"), 4 * l + 2)
                load(KV[0], mem_src, "mem_in")
                load(router_w[:, :, 0:GROUPS], I["w_grp"][l].rearrange("(k p) g -> p k g", p=P), "router_in")
                for g in range(GROUPS):
                    load(router_w[:, :, GROUPS + g * EPG:GROUPS + (g + 1) * EPG],
                         I["w_er"][l, g].rearrange("(k p) e -> p k e", p=P), "router_in")
                load(router_b[:, 0:GROUPS], I["b_grp"][l].partition_broadcast(P), "router_in")
                load(router_b[:, GROUPS:], I["b_er"][l].rearrange("g e -> (g e)").partition_broadcast(P), "router_in")
                pool.wait_ge(S("pipe_free"), number(("mem", l)))
                pool.dma_start(O["mem_k"][l, 0].rearrange("(i p) h d -> p i (h d)", p=P), KV[2]).then_inc(S("memk_out"), 16)
                pool.dma_start(O["mem_v"][l, 0].rearrange("(i p) h d -> p i (h d)", p=P), VP).then_inc(S("memv_out"), 16)

            for t in range(TT):
                pool.wait_ge(S("ln_done"), 3 * (LNS - 1) + t + 1)
                dst = O["y_prompt"][0, t * P:(t + 1) * P, :] if t < PT_ else O["y_sample"].rearrange("b t d -> (b t) d")
                pool.dma_start(dst, X[0:ROWS[t], t, :]).then_inc(S("stores"), 16)
            pool.wait_ge(S("memv_out"), 16 * DEPTH)
            pool.wait_ge(S("stores"), 16 * (2 + TT))

        @block.tensor
        def _(pe):
            mm, tr = pe.matmul, pe.transpose

            def run_jobs(stage):
                for n, (kind, name, c) in jobs[stage]:
                    if n >= 2:
                        pe.wait_ge(S("pipe_free"), n - 1)
                    bank = ps[:, 6 + n % 2, :]
                    l = stage[1]
                    if kind == "xt":
                        t, h = name, c
                        if h == 0 and stage[1] == 0:
                            pe.wait_ge(S("x_in"), 16 * TT)
                            pe.wait_ge(S("consts"), 1)
                        elif h == 0:
                            pe.wait_ge(S("ln_done"), 3 * (stage[1] - 1) + t + 1)
                        for k in range(4):
                            last = tr(bank[:, k * P:k * P + ROWS[t]], X[0:ROWS[t], t, (4 * h + k) * P:(4 * h + k + 1) * P],
                                      ident[0:ROWS[t], 0:ROWS[t]])
                    elif kind == "feat":
                        if c == 0:
                            unit_landed(pe, l, name)
                        w = wslot(l, name)
                        for k in range(KC):
                            last = mm(bank[:, 0:NT], w[:, k, c * P:(c + 1) * P], XT[:, k, :], start=(k == 0), stop=(k == KC - 1))
                    elif kind == "gz":
                        pe.wait_ge(S("small_in"), 16 * 6)
                        for k in range(KC):
                            last = mm(bank[0:RANK, 0:NT], wgz[:, k, :], XT[:, k, :], start=(k == 0), stop=(k == KC - 1))
                    elif kind == "gk":
                        if c == 0:
                            pe.wait_ge(S("pipe_free"), number(("in", 1), "gz"))
                        last = mm(bank[:, 0:NT], wgk2[:, c * P:(c + 1) * P], gz[:], start=True, stop=True)
                    elif kind == "tok":
                        if c == 0:
                            unit_landed(pe, l, name)
                        w = wslot(l, name)
                        for k in range(KC):
                            last = mm(bank[0:ROWS[c], :], XT[:, k, cols(c)], w[:, k, :], start=(k == 0), stop=(k == KC - 1))
                    elif kind == "mt":
                        i, h = name, c
                        if i == 0 and h == 0:
                            pe.wait_ge(S("mem_in"), 16 * (l + 1))
                        for k in range(4):
                            last = tr(bank[:, k * P:(k + 1) * P], KV[0][:, i, (4 * h + k) * P:(4 * h + k + 1) * P], ident[:])
                    elif kind == "memtok":
                        if c == 0:
                            unit_landed(pe, l, name)
                        if name == "mk0" and c == 0:
                            pe.wait_ge(S("pipe_free"), n)
                        w = wslot(l, name)
                        memT = KV[1].rearrange("p i d -> p (i d)").rearrange("p (k m) -> p k m", k=KC)
                        for k in range(KC):
                            last = mm(bank, memT[:, k, c * P:(c + 1) * P], w[:, k, :], start=(k == 0), stop=(k == KC - 1))
                    last.then_inc(S("pipe_full"), 1)
                pe.wait_ge(S("pipe_free"), number(stage))

            def project_out(l, src, which, inst):
                for j in range(2):
                    unit_landed(pe, l, f"{which}{j}")
                    w = wslot(l, f"{which}{j}")
                    for t in range(TT):
                        for k in range(KC):
                            last = mm(ps[0:ROWS[t], 2 * t + j, :], src[:, k, cols(t)], w[:, k, :], start=(k == 0), stop=(k == KC - 1))
                        if t < TT - 1:
                            last.then_inc(S("mix_done"), 1)
                    last.then_inc(S("mix_unit"), 1)

            def mixer(l):
                m, dvc = MIX[l], DVC[l]
                nv = dvc * P
                o_bank = [5, 6]
                if l == 0:
                    pe.wait_ge(S("iota_ready"), 1)
                    pe.wait_ge(S("conv_in"), 16)
                    for c in range(CW // P):
                        last = tr(ps[:, 0, c * 16:(c + 1) * 16], conv_in[:, c * P:(c + 1) * P], ident[0:2 * DB, 0:2 * DB])
                    last.then_inc(S("conv_ps"), 1)
                    pe.wait_ge(S("conv_u"), 1)
                    for c in range(CW // P):
                        last = tr(ps[0:2 + 2 * DB, 1, c * P:(c + 1) * P], conv_tail[:, c, :], ident[:])
                    last.then_inc(S("conv_ps"), 1)
                    pe.wait_ge(S("conv_out"), 1)
                ktok_bank = 6 - l
                for h in range(HEADS):
                    qk, kd = m["qk"][h % 2], m["kd"][h % 2]

                    def score(lv, t, out):
                        a, b = (m["k"][:, h, cols(t)], m["q"][:, h, cols(t)]) if lv == 0 else (qk[:, lv - 1, cols(t)],) * 2
                        return mm(out, a, b, start=True, stop=True)

                    pe.wait_ge(S("qk_ready"), count_at("qk_ready", l, h + 1))
                    if h:
                        pe.wait_ge(S("state_new"), count_at("state_new", l, h))
                    for t in range(PT_):
                        for lv in range(LEVELS):
                            last = score(lv, t, ps[:, 2 * t + lv // 4, (lv % 4) * P:(lv % 4 + 1) * P])
                        last.then_inc(S("score_ps"), 1)
                    if h:
                        pe.wait_ge(S("ms_ready"), count_at("ms_ready", l, h))
                    for lv in range(SL):
                        last = score(lv, PT_, ps[0:NS, 4, lv * NS:(lv + 1) * NS])
                    last.then_inc(S("score_ps"), 1)
                    pe.wait_ge(S("kd_ready"), count_at("kd_ready", l, h + 1))
                    if h:
                        pe.wait_ge(S("rms"), count_at("rms", l, h))
                    for t in range(TT):
                        last = tr(ps[0:ROWS[t], ktok_bank, t * P:(t + 1) * P], kd[:, cols(t)], ident[:])
                    last.then_inc(S("ktok_ps"), 1)
                    pe.wait_ge(S("ktok"), count_at("ktok", l, h + 1))
                    for t in range(PT_):
                        last = mm(ps[:, 7, t * nv:(t + 1) * nv], m["ktok"][:, t, :], m["v"][:, t, h * nv:(h + 1) * nv], start=True, stop=True)
                    last.then_inc(S("s_ps"), 1)
                    pe.wait_ge(S("kexp"), count_at("kexp", l, h + 1))
                    pe.wait_ge(S("st_ready"), count_at("st_ready", l, TT * h + PT_))
                    per = HALF // nv
                    for b in range(DB):
                        last = mm(ps[:, b // per, (b % per) * nv:(b % per + 1) * nv], m["kexp"][:, b, :],
                                  m["v"][0:NS, 2, h * nv:(h + 1) * nv], start=True, stop=True)
                    last.then_inc(S("ns_ps"), 1)
                    pe.wait_ge(S("st_ready"), count_at("st_ready", l, TT * (h + 1)))
                    pe.wait_ge(S("s1_ready"), count_at("s1_ready", l, h + 1))
                    pe.wait_ge(S("qd_ready"), count_at("qd_ready", l, h + 1))
                    pe.wait_ge(S(f"s0_in{l}"), 16 * (h + 1))
                    s0 = m["s0"]
                    for c in range(dvc):
                        o = ps[:, o_bank[c], :]
                        vc = slice(h * nv + c * P, h * nv + (c + 1) * P)
                        mm(o[:, cols(0)], m["v"][:, 0, vc], m["st"][:, 0, :], start=True, stop=True)
                        mm(o[:, cols(1)], m["v"][:, 1, vc], m["st"][:, 1, :], start=True, stop=False)
                        mm(o[:, cols(1)], m["s1"][:, c * P:(c + 1) * P], m["qd"][:, cols(1)], start=False, stop=True)
                        mm(o[:, cols(2)], m["v"][0:NS, 2, vc], m["st"][0:NS, 2, 0:NS], start=True, stop=False)
                        for b in range(DB):
                            sc = slice(SEQ + b * DS, SEQ + (b + 1) * DS)
                            last = mm(o[:, sc], s0[:, b, c * P:(c + 1) * P], m["qd"][:, sc], start=False, stop=(b == DB - 1))
                    last.then_inc(S("o_ps"), 1)
                    pe.wait_ge(S("sq_ready"), count_at("sq_ready", l, h + 1))
                    for c in range(dvc):
                        last = mm(ps[:, 4, 0:NT], ones[:], m["sq"][:, c, :], start=(c == 0), stop=(c == dvc - 1))
                    last.then_inc(S("ss_ps"), 1)
                pe.wait_ge(S("rms"), count_at("rms", l, HEADS))

            def attention(l):
                def turn_keys(n, src):
                    for j in range(4):
                        if n:
                            pe.wait_ge(S(("kt_a", "kt_d")[j // 2]), count_at("kt_a", l, 2 * (n - 1) + j % 2 + 1))
                        for c in range(2):
                            for i in range(MT_):
                                last = tr(ps[:, j, (2 * c + i) * P:(2 * c + i + 1) * P], src[:, i, (2 * j + c) * P:(2 * j + c + 1) * P], ident[:])
                        last.then_inc(S("kt_full"), 1)

                pe.wait_ge(S("ln_done"), 3 * (3 * l) + TT)
                turn_keys(0, KV[2])
                run_jobs(("xt", 1 + 3 * l))
                run_jobs(("mq", l))

                def sample_scores(b):
                    pe.wait_ge(S("kt_a"), count_at("kt_a", l, 2 * (b + 2)))
                    pe.wait_ge(S("kt_d"), count_at("kt_d", l, 2 * (b + 2)))
                    if b >= 2:
                        pe.wait_ge(S("ssel"), count_at("ssel", l, b - 1))
                    for c in range(2):
                        for h in range(MH):
                            last = mm(ps[h * NS:(h + 1) * NS, 4 + b % 2, 0:MEM], QT[:, 2 * h + c, SEQ:NT],
                                      KT[b % 2][:, 2 * h + c, :], start=(c == 0), stop=(c == 1))
                    last.then_inc(S("ssc"), 1)

                for b in range(DB):
                    pe.wait_ge(S(f"kv_in{b % 3}"), 16 * (kv_loads(l, b)))
                    turn_keys(b + 1, KV[b % 3])
                    if b:
                        sample_scores(b - 1)
                sample_scores(DB - 1)
                pe.wait_ge(S("kt_a"), count_at("kt_a", l, 2 * (DB + 1)))
                pe.wait_ge(S("kt_d"), count_at("kt_d", l, 2 * (DB + 1)))

                def prompt_scores(t):
                    for h in range(MH):
                        for c in range(2):
                            last = mm(ps[:, 2 * t + h // 2, (h % 2) * MEM:(h % 2 + 1) * MEM], QT[:, 2 * h + c, cols(t)],
                                      KTP[:, 2 * h + c, :], start=(c == 0), stop=(c == 1))
                    last.then_inc(S("psc"), 1)

                prompt_scores(0)
                prompt_scores(1)
                pe.wait_ge(S("sp_ready"), count_at("sp_ready", l, 1))
                for i in range(MT_):
                    last = tr(ps[:, 4, i * P:(i + 1) * P], SS[:, i * P:(i + 1) * P], ident[:])
                last.then_inc(S("spt_ps"), 1)
                pe.wait_ge(S("spt_sb"), count_at("spt_sb", l, 1))

                def sample_values(b):
                    i = DB + b
                    pe.wait_ge(S(f"kv_in{i % 3}"), 16 * kv_loads(l, i))
                    if b >= 2:
                        pe.wait_ge(S("osel"), count_at("osel", l, b - 1))
                    for i2 in range(MT_):
                        for h in range(MH):
                            last = mm(ps[h * NS:(h + 1) * NS, 5 - b % 2, 0:MHD], SST[:, i2, h * NS:(h + 1) * NS],
                                      KV[i % 3][:, i2, h * MHD:(h + 1) * MHD], start=(i2 == 0), stop=(i2 == MT_ - 1))
                    last.then_inc(S("pv_done"), 1)

                def prompt_values(t):
                    pe.wait_ge(S("pr_ready"), count_at("pr_ready", l, t + 1))
                    for i in range(MT_):
                        for h in range(MH):
                            last = tr(ps[:, 6 + i, h * P:(h + 1) * P], PR[:, h, i * P:(i + 1) * P], ident[:])
                    last.then_inc(S("prt_ps"), 1)
                    pe.wait_ge(S("prt_sb"), count_at("prt_sb", l, t + 1))
                    for k in range(KC):
                        for i in range(MT_):
                            last = mm(ps[:, 2 * t + k // 4, (k % 4) * P:(k % 4 + 1) * P], VP[:, i, k * P:(k + 1) * P],
                                      PRT[:, i, (k // 2) * P:(k // 2 + 1) * P], start=(i == 0), stop=(i == MT_ - 1))
                    last.then_inc(S("po_ps"), 1)

                prompt_values(0)
                for b in range(3):
                    sample_values(b)
                prompt_values(1)
                for b in range(3, DB):
                    sample_values(b)
                pe.wait_ge(S("osel"), count_at("osel", l, DB))
                for c in range(2):
                    last = tr(ps[:, 6, c * P:(c + 1) * P], SS[:, c * P:(c + 1) * P], ident[:])
                last.then_inc(S("os_ps"), 1)
                pe.wait_ge(S("oa_ready"), count_at("oa_ready", l, 3))

            def moe(l):
                pe.wait_ge(S("router_in"), 16 * (GROUPS + 3) * (l + 1))
                for t in range(TT):
                    for k in range(KC):
                        last = mm(ps[0:ROWS[t], 0, t * 64:t * 64 + GROUPS + NE], XT[:, k, cols(t)], router_w[:, k, :],
                                  start=(k == 0), stop=(k == KC - 1))
                last.then_inc(S("logits"), 1)
                pe.wait_ge(S("assigned"), count_at("assigned", l, 1))
                for t in range(TT):
                    for u in range(t + 1):
                        last = mm(ps[:, 1, t * NE:(t + 1) * NE], upper[:] if u == t else ones[:], ASG[:, u, :],
                                  start=(u == 0), stop=(u == t))
                for u in range(TT):
                    last = mm(ps[:, 1, TT * NE:(TT + 1) * NE], ones[:], ASG[:, u, :], start=(u == 0), stop=(u == TT - 1))
                last.then_inc(S("ranks"), 1)
                pe.wait_ge(S("rounds_known"), count_at("rounds_known", l, 1))
                rm1 = pe.value_load(rounds[0:1, 0:1], min_val=0, max_val=4)

                def scatter(it, part):
                    for n in part:
                        t, j = n // 2, n % 2
                        if n >= 2:
                            pe.wait_ge(S(f"acc{l}"), it * (2 * TT) + (n - 1))
                        last = mm(ps[0:ROWS[t], 7 - n % 2, :], PWT[:, cols(t)], Y[:, j * HALF:(j + 1) * HALF], start=True, stop=True)
                        last.then_inc(S(f"scat{l}"), 1)

                def gather(it):
                    pe.wait_ge(S(f"pg_part{l}"), it * TT + TT)
                    for k in range(KC):
                        for t in range(TT):
                            last = mm(ps[:, k // 4, (k % 4) * P:(k % 4 + 1) * P], X[0:ROWS[t], t, k * P:(k + 1) * P],
                                      PG[0:ROWS[t], t, :, :].rearrange("p j c -> p (j c)"), start=(t == 0), stop=(t == TT - 1))
                        if k == 3:
                            last.then_inc(S(f"xg_ps0{l}"), 1)
                    last.then_inc(S(f"xg_ps1{l}"), 1)

                gather(0)
                def both_experts(bank, s, x, n):
                    w = [W[:, s + j, :].rearrange("p (k n) -> p k n", k=x.shape[1]) for j in range(2)]
                    for k in range(x.shape[1]):
                        for j in range(2):
                            last = mm(ps[j * CAP:(j + 1) * CAP, bank, :], x[:, k, j * CAP:(j + 1) * CAP],
                                      w[j][:, k, n * HALF:(n + 1) * HALF], start=(k == 0), stop=(k == x.shape[1] - 1))
                    return last

                def landed(it, s):
                    pe.wait_ge(S(f"e_in{l}_{s}"), 16 * (it + 1))
                    pe.wait_ge(S(f"e_in{l}_{s + 1}"), 16 * (it + 1))

                with pe.Fori(0, rm1 + 1) as rd:
                    with pe.Fori(0, PAIRS) as p:
                        it = rd * PAIRS + p
                        pe.wait_ge(S(f"xg_a{l}"), it + 1)
                        pe.wait_ge(S(f"xg_d{l}"), it + 1)
                        pe.wait_ge(S(f"ht{l}"), it + 1)
                        landed(it, 0)
                        both_experts(2, 0, XG, 0).then_inc(S(f"gate_done{l}"), 1)
                        gather(it + 1)
                        pe.wait_ge(S(f"h_ready{l}"), it + 1)
                        landed(it, 2)
                        both_experts(3, 2, XG, 0).then_inc(S(f"up_done{l}"), 1)
                        pe.wait_ge(S(f"y_sb{l}"), it + 1)
                        pe.wait_ge(S(f"pwt_sb{l}"), it + 1)
                        scatter(it, range(0, 3))
                        pe.wait_ge(S(f"h_ready{l}"), it + 2)
                        for f in range(DE // P):
                            last = tr(ps[:, 2, f * P:(f + 1) * P], HS[:, f * P:(f + 1) * P], ident[:])
                        last.then_inc(S(f"ht_ps{l}"), 1)
                        scatter(it, range(3, 2 * TT))
                        pe.wait_ge(S(f"acc{l}"), it * (2 * TT) + 2 * TT)
                        pe.wait_ge(S(f"pw_part{l}"), it * TT + TT)
                        for t in range(TT):
                            last = tr(ps[:, 6, cols(t)], PW[0:ROWS[t], t, :, :].rearrange("p j c -> p (j c)"), ident[0:ROWS[t], 0:ROWS[t]])
                        last.then_inc(S(f"pwt_ps{l}"), 1)
                        pe.wait_ge(S(f"ht{l}"), it + 2)
                        landed(it, 4)
                        both_experts(4, 4, HT, 0)
                        both_experts(5, 4, HT, 1).then_inc(S(f"down_done{l}"), 1)
                pe.wait_ge(S(f"y_sb{l}"), rm1 * PAIRS + (PAIRS + 1))
                pe.wait_ge(S(f"pwt_sb{l}"), rm1 * PAIRS + (PAIRS + 1))
                scatter(rm1 * PAIRS + PAIRS, range(2 * TT))
                pe.wait_ge(S(f"acc{l}"), rm1 * (PAIRS * 2 * TT) + (PAIRS + 1) * 2 * TT)

            pe.wait_ge(S("consts"), 1)
            mm(ps[:, 0, 0:P], ones[:], upper[:], start=True, stop=True).then_inc(S("iota_ps"), 1)
            run_jobs(("xt", 0))
            for l in range(DEPTH):
                run_jobs(("in", l))
                mixer(l)
                project_out(l, MIX[l]["o"], "out", 1 + 3 * l)
                run_jobs(("mem", l))
                attention(l)
                project_out(l, OA, "mo", 2 + 3 * l)
                run_jobs(("xt", 2 + 3 * l))
                moe(l)
                if l + 1 < DEPTH:
                    run_jobs(("xt", 3 + 3 * l))

        @block.scalar
        def _(act):
            st = Steps(act, S("act_step"))
            fn = act.activation

            def load_gb(inst):
                l, n = (inst - 1) // 3, (inst - 1) % 3
                if inst > 1:
                    act.wait_ge(S("ln_done"), 3 * (inst - 1))
                act.dma_start(GB[:, 0, :], I["ln_g"][l, n].partition_broadcast(P)).then_inc(S("gb_in"), 16)
                act.dma_start(GB[:, 1, :], I["ln_b"][l, n].partition_broadcast(P)).then_inc(S("gb_in"), 16)

            def empty_jobs(stage, before=None):
                for n, (kind, name, c) in jobs[stage]:
                    act.wait_ge(S("pipe_full"), n + 1)
                    bank = ps[:, 6 + n % 2, :]
                    l = stage[1]
                    m = MIX[l] if l < 2 else None
                    full = bank[:, 0:NT]
                    if kind == "xt":
                        src = bank.rearrange("p (k t) -> p k t", k=4)[:, :, 0:ROWS[name]]
                        ins = fn(XT[:, 4 * c:4 * c + 4, cols(name)], src, ACT.Copy)
                    elif kind == "feat" and name[:2] == "mq":
                        ins = fn(QT[:, 4 * int(name[2]) + c, :], full, ACT.Copy, scale=float(MHD) ** -0.5)
                    elif kind == "feat" and name in ("bg", "cg", "h"):
                        ins = fn(m["conv"][("bg", "cg", "h").index(name)][:, c, :], full, ACT.Copy)
                    elif kind == "feat" and name == "f":
                        ins = fn(m["b"][:, c, :], full, ACT.Copy)
                    elif kind == "feat" and name == "q" and l == 0:
                        ins = fn(m["q"][:, c, :], full, ACT.Silu)
                    elif kind == "feat" and name == "q":
                        ins = fn(m["q"][:, c, :], full, ACT.Copy, scale=float(DK) ** -0.5)
                    elif kind == "feat" and name == "k":
                        ins = fn(m["k"][:, c, :], full, ACT.Copy)
                    elif kind == "feat":
                        ins = fn(m["g"][:, 4 * (name == "g1") + c, :], full, ACT.Silu)
                    elif kind == "gz":
                        ins = fn(gz[:], bank[0:RANK, 0:NT], ACT.Copy)
                    elif kind == "gk":
                        ins = fn(m["b"][:, c, :], full, ACT.Identity, bias=bgk2[:, c:c + 1])
                    elif kind == "tok":
                        at = HALF * (name == "v1")
                        ins = fn(m["v"][0:ROWS[c], c, at:at + HALF], bank[0:ROWS[c], :], ACT.Copy)
                    elif kind == "mt":
                        memT = KV[1].rearrange("p i d -> p (i d)").rearrange("p (k m) -> p k m", k=KC)
                        ins = fn(memT[:, 4 * c:4 * c + 4, name * P:(name + 1) * P], bank.rearrange("p (k t) -> p k t", k=4), ACT.Copy)
                    elif kind == "memtok":
                        at = HALF * int(name[2])
                        dst = KV[2] if name[:2] == "mk" else VP
                        ins = fn(dst[:, c, at:at + HALF], bank, ACT.Copy)
                    ins.then_inc(S("pipe_free"), 1)

            def mixer(l):
                m, dvc = MIX[l], DVC[l]
                z, tmp = m["b"], m["tmp"]
                act.wait_ge(S("pipe_free"), number(("in", l), "f" if l == 0 else "gk"))
                st.step(fn(tmp, z, ACT.Abs))
                st.step(fn(tmp, tmp, ACT.Exp, scale=-1.0))
                st.tell(fn(tmp, tmp, ACT.Ln, bias=1.0), S("softplus"))
                if l == 0:
                    act.wait_ge(S("amz_ready"), 1)
                    st.tell(fn(m["k"], m["k"], ACT.Exp), S("k_ready"))
                def decays(h):
                    qk, kd, dec = m["qk"][h % 2], m["kd"][h % 2], m["dec"][h % 2]
                    act.wait_ge(S("e_ready"), count_at("e_ready", l, h + 1))
                    fn(kd, kd, ACT.Exp)
                    fn(qk[:, 0:SL - 1, :], qk[:, 0:SL - 1, :], ACT.Exp)
                    fn(dec, dec, ACT.Exp)
                    st.tell(fn(qk[:, SL - 1:, 0:SEQ], qk[:, SL - 1:, 0:SEQ], ACT.Exp), S("ex_ready"))

                def query_decays(h):
                    st.tell(fn(m["qd"], m["b"][:, h, :], ACT.Exp), S("qd_exp"))

                decays(0)
                query_decays(0)
                for h in range(HEADS):
                    act.wait_ge(S("ktok_ps"), count_at("ktok_ps", l, h + 1))
                    fn(m["ktok"][:, 0:PT_, :], ps[:, 6 - l, 0:PT_ * P].rearrange("p (t c) -> p t c", t=PT_), ACT.Copy)
                    st.tell(fn(m["ktok"][0:NS, PT_, :], ps[0:NS, 6 - l, PT_ * P:(PT_ + 1) * P], ACT.Copy), S("ktok"))
                    act.wait_ge(S("s_ps"), count_at("s_ps", l, h + 1))
                    st.tell(fn(m["s1"], ps[:, 7, 0:dvc * P], ACT.Copy), S("s1_ready"))
                    if h + 1 < HEADS:
                        decays(h + 1)
                    act.wait_ge(S("o_ps"), count_at("o_ps", l, h + 1))
                    for c in range(dvc):
                        ins = fn(m["sq"][:, c, :], ps[:, 5 + c, 0:NT], ACT.Square)
                    st.tell(ins, S("sq_ready"))
                    if h + 1 < HEADS:
                        query_decays(h + 1)
                    else:
                        act.wait_ge(S("state_new"), count_at("state_new", l, HEADS))
                        load_gb(1 + 3 * l)
                    act.wait_ge(S("ms_ready"), count_at("ms_ready", l, h + 1))
                    st.tell(fn(m["rs"], m["rs"], ACT.Sqrt), S("root"))

            def norm(inst):
                for t in range(TT):
                    act.wait_ge(S("var_ready"), 3 * (inst - 1) + t + 1)
                    st.tell(fn(mv[0:ROWS[t], 2:3], mv[0:ROWS[t], 2:3], ACT.Sqrt), S("std_ready"))

            def attention(l):
                def keys(n, dst):
                    for j in range(2):
                        act.wait_ge(S("kt_full"), count_at("kt_full", l, 4 * n + j + 1))
                        st.tell(fn(dst[:, 2 * j:2 * j + 2, :].rearrange("p c m -> p (c m)"), ps[:, j, :], ACT.Copy), S("kt_a"))

                keys(0, KTP)
                empty_jobs(("xt", 1 + 3 * l))
                load_gb(2 + 3 * l)
                empty_jobs(("mq", l))
                for b in range(DB):
                    if b >= 2:
                        act.wait_ge(S("ssc"), count_at("ssc", l, b - 1))
                    keys(b + 1, KT[b % 2])
                act.wait_ge(S("smax"), count_at("smax", l, 1))
                st.tell(fn(SS, SS, ACT.Exp, bias=small[:, 0, 0:1], accum_out=small[:, 1, 0:1]), S("sexp"))
                act.wait_ge(S("spt_ps"), count_at("spt_ps", l, 1))
                st.tell(fn(SST.rearrange("p i c -> p (i c)"), ps[:, 4, 0:MEM], ACT.Copy), S("spt_sb"))
                for t in range(PT_):
                    act.wait_ge(S("pmax"), count_at("pmax", l, t + 1))
                    for h in range(MH):
                        ins = fn(PR[:, h, :], ps[:, 2 * t + h // 2, (h % 2) * MEM:(h % 2 + 1) * MEM], ACT.Exp,
                                 bias=small[:, 2, h:h + 1], accum_out=small[:, 3, h:h + 1])
                        if h < MH - 1:
                            st.step(ins)
                    st.tell(ins, S("pexp"))
                    act.wait_ge(S("prt_ps"), count_at("prt_ps", l, t + 1))
                    st.step(fn(PRT[:, 0, :], ps[:, 6, :], ACT.Copy))
                    st.tell(fn(PRT[:, 1, :], ps[:, 7, :], ACT.Copy), S("prt_sb"))
                    act.wait_ge(S("po_ps"), count_at("po_ps", l, t + 1))
                    st.step(fn(OA[:, 0:4, cols(t)], ps[:, 2 * t, :].rearrange("p (k t) -> p k t", k=4), ACT.Copy))
                    st.tell(fn(OA[:, 4:8, cols(t)], ps[:, 2 * t + 1, :].rearrange("p (k t) -> p k t", k=4), ACT.Copy), S("oa_ready"))
                act.wait_ge(S("os_ps"), count_at("os_ps", l, 1))
                for c in range(2):
                    dst = OA[:, :, SEQ:NT].rearrange("p (h c) n -> p h c n", c=2)[:, :, c, :]
                    ins = fn(dst, ps[:, 6, c * P:(c + 1) * P].rearrange("p (h n) -> p h n", h=MH), ACT.Copy)
                    if c == 0:
                        st.step(ins)
                st.tell(ins, S("oa_ready"))

            def moe(l):
                act.wait_ge(S("gdiff"), count_at("gdiff", l, 1))
                st.step(fn(GE, GE, ACT.Exp))
                st.tell(fn(small[:, 6, 0:TT], small[:, 6, 0:TT], ACT.Exp), S("gexp"))
                act.wait_ge(S("rounds_known"), count_at("rounds_known", l, 1))
                rm1 = act.value_load(rounds[0:1, 0:1], min_val=0, max_val=4)
                def move_gathered(it):
                    act.wait_ge(S(f"xg_ps0{l}"), it + 1)
                    fn(XG[:, 0:4, :].rearrange("p k c -> p (k c)"), ps[:, 0, :], ACT.Copy).then_inc(S(f"xg_a{l}"), 1)

                move_gathered(0)
                with act.Fori(0, rm1 + 1) as rd:
                    with act.Fori(0, PAIRS) as p:
                        it = rd * PAIRS + p
                        act.wait_ge(S(f"gate_done{l}"), it + 1)
                        act.wait_ge(S(f"h_ready{l}"), it + 1)
                        fn(SG, ps[:, 2, :], ACT.Silu).then_inc(S(f"sg{l}"), 1)
                        act.wait_ge(S(f"up_done{l}"), it + 1)
                        move_gathered(it + 1)
                        act.wait_ge(S(f"ht_ps{l}"), it + 1)
                        fn(HT.rearrange("p f c -> p (f c)"), ps[:, 2, :], ACT.Copy).then_inc(S(f"ht{l}"), 1)
                        act.wait_ge(S(f"pwt_ps{l}"), it + 2)
                        fn(PWT, ps[:, 6, 0:NT], ACT.Copy).then_inc(S(f"pwt_sb{l}"), 1)
                        act.wait_ge(S(f"down_done{l}"), it + 1)
                        fn(Y, ps[:, 4:6, :].rearrange("p j n -> p (j n)"), ACT.Copy).then_inc(S(f"y_sb{l}"), 1)

            empty_jobs(("xt", 0))
            for l in range(DEPTH):
                empty_jobs(("in", l))
                mixer(l)
                norm(1 + 3 * l)
                empty_jobs(("mem", l))
                attention(l)
                norm(2 + 3 * l)
                empty_jobs(("xt", 2 + 3 * l))
                load_gb(3 + 3 * l)
                moe(l)
                norm(3 + 3 * l)
                if l + 1 < DEPTH:
                    empty_jobs(("xt", 3 + 3 * l))

        @block.vector
        def _(dve):
            st = Steps(dve, S("dve_step"))
            step, tell = st.step, st.tell
            tt, ts, stt, cp, red = (dve.tensor_tensor, dve.tensor_scalar, dve.scalar_tensor_tensor,
                                    dve.tensor_copy, dve.tensor_reduce)

            def bc(ap, *shape):
                return ap.to_broadcast(list(shape))

            def conv(m):
                bg, cg, hh = m["conv"]
                up, us, C = m["up"], m["us"], CW // P
                dve.wait_ge(S("pipe_free"), number(("in", 0), "h"))
                step(dve.memset(up[:, :, 0:2], 0.0))
                dve.wait_ge(S("conv_ps"), 1)
                for c in range(C):
                    step(tt(up[:, c, 2:], cg[:, c, 0:SEQ], hh[:, c, 0:SEQ], ALU.mult))
                    step(tt(us[:, c, :, 2:], cg[:, c, SEQ:].rearrange("p (b t) -> p b t", b=DB),
                            hh[:, c, SEQ:].rearrange("p (b t) -> p b t", b=DB), ALU.mult))
                    step(cp(us[:, c, :, 0:2], ps[:, 0, c * 16:(c + 1) * 16].rearrange("p (b j) -> p b j", b=DB)))
                step(cp(conv_tail[:, :, 0:2], up[:, :, SEQ:SEQ + 2]))
                for c in range(C - 1):
                    step(cp(conv_tail[:, c, 2:].rearrange("p (b j) -> p b j", b=DB), us[:, c, :, DS:DS + 2]))
                tell(cp(conv_tail[:, C - 1, 2:].rearrange("p (b j) -> p b j", b=DB), us[:, C - 1, :, DS:DS + 2]), S("conv_u"))
                dve.wait_ge(S("small_in"), 16 * 6)
                for c in range(C):
                    for y, u, gate in ((m["o"][:, HEADS + c, 0:SEQ], lambda j: up[:, c, j:j + SEQ], bg[:, c, 0:SEQ]),
                                       (m["o"][:, HEADS + c, SEQ:].rearrange("p (b t) -> p b t", b=DB), lambda j: us[:, c, :, j:j + DS],
                                        bg[:, c, SEQ:].rearrange("p (b t) -> p b t", b=DB))):
                        step(ts(y, u(0), convw[:, c, 0:1], None, ALU.mult))
                        step(stt(y, u(1), convw[:, c, 1:2], y, ALU.mult, ALU.add))
                        step(stt(y, u(2), convw[:, c, 2:3], y, ALU.mult, ALU.add))
                        step(tt(y, y, gate, ALU.mult))
                dve.wait_ge(S("conv_ps"), 2)
                tell(cp(conv_tok, ps[0:2 + 2 * DB, 1, :]), S("conv_out"))

            def mixer(l):
                m, dvc = MIX[l], DVC[l]
                nv = dvc * P
                dv = nv
                if l == 0:
                    conv(m)
                z = m["b"]
                dve.wait_ge(S("pipe_free"), number(("in", l)))
                dve.wait_ge(S("softplus"), count_at("softplus", l, 1))
                zf, tf = (x.rearrange("p h t -> p (h t)") for x in (z, m["tmp"]))
                if l == 0:
                    step(stt(tf, zf, 0.0, tf, ALU.min, ALU.subtract))
                    tell(tt(m["k"].rearrange("p h t -> p (h t)"), tf, zf, ALU.subtract), S("amz_ready"))
                    a = m["tmp"]
                    dve.wait_ge(S("k_ready"), 1)
                else:
                    step(stt(tf, zf, 0.0, tf, ALU.min, ALU.subtract))
                    step(ts(tf, tf, 1.0 / 16.0, None, ALU.mult))
                    a = m["tmp"]
                for h in range(HEADS):
                    dve.tensor_tensor_scan(m["b"][:, h, :], carry[:], a[:, h, :], 0.0, ALU.mult, ALU.add).then_inc(S("b_ready"), 1)

                def decayed(h):
                    q, k, qk, kd = m["q"][:, h, :], m["k"][:, h, :], m["qk"][h % 2], m["kd"][h % 2]
                    dve.wait_ge(S("ex_ready"), count_at("ex_ready", l, h + 1))
                    tt(kd, kd, k, ALU.mult).then_inc(S("kd_ready"), 1)
                    for lv in range(1, LEVELS):
                        upto = NT if lv < SL else SEQ
                        (el, er), (kl, _), (_, qr) = halves(qk[:, lv - 1, :], lv, upto), halves(k, lv, upto), halves(q, lv, upto)
                        tt(el, el, kl, ALU.mult)
                        ins = tt(er, er, qr, ALU.mult)
                    tell(ins, S("qk_ready"))

                decayed(0)
                for h in range(HEADS):
                    dec, s0 = m["dec"][h % 2], m["s0"]
                    dve.wait_ge(S("qd_exp"), count_at("qd_exp", l, h + 1))
                    tell(tt(m["qd"], m["qd"], m["q"][:, h, :], ALU.mult), S("qd_ready"))
                    for t in range(TT):
                        R, L, C = ROWS[t], (LEVELS if t < PT_ else SL), ROWS[t]
                        dve.wait_ge(S("score_ps"), count_at("score_ps", l, TT * h + t + 1))
                        if t < PT_:
                            src = ps[:, 2 * t:2 * t + 2, :].rearrange("p a (b c) -> p (a b) c", c=P)
                        else:
                            src = ps[0:NS, 4, 0:SL * NS].rearrange("p (a c) -> p a c", a=SL)
                        ms = m["ms"][0:R, 0:L, 0:C]
                        step(tt(ms, src, masks[0:R, 0:L, 0:C], ALU.mult))
                        tell(red(m["st"][0:R, t, 0:C], ms.rearrange("p l t -> p t l"), AX.X, ALU.add), S("st_ready"))
                    if h + 1 < HEADS:
                        decayed(h + 1)
                    if h:
                        dve.wait_ge(S("state_out"), count_at("state_out", l, 32 * h))
                    dve.wait_ge(S("s_ps"), count_at("s_ps", l, h + 1))
                    dve.wait_ge(S("s1_ready"), count_at("s1_ready", l, h + 1))
                    step(stt(m["sf"], m["s1"], dec[:, 1:2], ps[:, 7, nv:2 * nv], ALU.mult, ALU.add))
                    dve.wait_ge(S("ns_ps"), count_at("ns_ps", l, h + 1))
                    dve.wait_ge(S("o_ps"), count_at("o_ps", l, h + 1))
                    new = ps[:, 0:DB * nv // HALF, :].rearrange("p a (b v) -> p (a b) v", v=nv)
                    for b in range(DB):
                        ins = stt(s0[:, b, :], s0[:, b, :], dec[:, PT_ + b:PT_ + b + 1], new[:, b, :], ALU.mult, ALU.add)
                    tell(ins, S("state_new"))
                    dve.wait_ge(S("ss_ps"), count_at("ss_ps", l, h + 1))
                    tell(ts(m["rs"], ps[:, 4, 0:NT], 1.0 / dv, RMS_EPS, ALU.mult, ALU.add), S("ms_ready"))
                    dve.wait_ge(S("root"), count_at("root", l, h + 1))
                    step(dve.reciprocal(m["rs"], m["rs"]))
                    for c in range(dvc):
                        o = m["o"][:, h * dvc + c, :]
                        step(stt(o, ps[:, 5 + c, 0:NT], gnorm[l][:, c:c + 1], m["rs"], ALU.mult, ALU.mult))
                        ins = tt(o, o, m["g"][:, h * dvc + c, :], ALU.mult)
                        if c < dvc - 1:
                            step(ins)
                    tell(ins, S("rms"))

            def norm(inst, src=None):
                dve.wait_ge(S("gb_in"), 32 * inst)
                i = 2 * ((inst - 1) // 3) + ((inst - 1) % 3)
                for t in range(TT):
                    R = ROWS[t]
                    x = X[0:R, t, :]
                    if src is None:
                        if t < TT - 1:
                            dve.wait_ge(S("mix_done"), 2 * (TT - 1) * i + (TT - 1) + t + 1)
                        else:
                            dve.wait_ge(S("mix_unit"), 2 * i + 2)
                        y = ps[0:R, 2 * t:2 * t + 2, :].rearrange("p a n -> p (a n)")
                    else:
                        y = src[0:R, t, :]
                    step(stt(x, x, ALPHA, y, ALU.mult, ALU.add))
                    for j in range(2):
                        step(dve.bn_stats(stat[0:R, j, :], x[:, j * HALF:(j + 1) * HALF]))
                    step(dve.bn_aggr(mv[0:R, 0:2], stat[0:R].rearrange("p a b -> p (a b)")))
                    tell(ts(mv[0:R, 2:3], mv[0:R, 1:2], LN_EPS, None, ALU.add), S("var_ready"))
                    dve.wait_ge(S("std_ready"), 3 * (inst - 1) + t + 1)
                    step(dve.reciprocal(mv[0:R, 3:4], mv[0:R, 2:3]))
                    step(ts(x, x, mv[0:R, 0:1], mv[0:R, 3:4], ALU.subtract, ALU.mult))
                    step(tt(x, x, GB[0:R, 0, :], ALU.mult))
                    tell(tt(x, x, GB[0:R, 1, :], ALU.add), S("ln_done"))

            def attention(l):
                def keys(n, dst):
                    for j in (2, 3):
                        dve.wait_ge(S("kt_full"), count_at("kt_full", l, 4 * n + j + 1))
                        tell(cp(dst[:, 2 * j:2 * j + 2, :].rearrange("p c m -> p (c m)"), ps[:, j, :]), S("kt_d"))

                def select(b, bank, sem):
                    x, mine = ps[:, bank, 0:MEM], bmask[:, b:b + 1]
                    tell(stt(SS, x, mine, SS, ALU.mult, ALU.add) if b else ts(SS, x, mine, None, ALU.mult), S(sem))

                keys(0, KTP)
                for b in range(DB):
                    if b >= 2:
                        dve.wait_ge(S("ssc"), count_at("ssc", l, b - 1))
                    keys(b + 1, KT[b % 2])
                    if b:
                        dve.wait_ge(S("ssc"), count_at("ssc", l, b))
                        select(b - 1, 4 + (b - 1) % 2, "ssel")
                dve.wait_ge(S("ssc"), count_at("ssc", l, DB))
                select(DB - 1, 4 + (DB - 1) % 2, "ssel")
                step(red(small[:, 0, 1:2], SS, AX.X, ALU.max))
                tell(ts(small[:, 0, 0:1], small[:, 0, 1:2], -1.0, None, ALU.mult), S("smax"))
                dve.wait_ge(S("sexp"), count_at("sexp", l, 1))
                step(dve.reciprocal(small[:, 1, 1:2], small[:, 1, 0:1]))
                tell(ts(SS, SS, small[:, 1, 1:2], None, ALU.mult), S("sp_ready"))
                for t in range(PT_):
                    dve.wait_ge(S("psc"), count_at("psc", l, t + 1))
                    step(red(small[:, 4, 0:MH], ps[:, 2 * t:2 * t + 2, :].rearrange("p a (b m) -> p (a b) m", m=MEM), AX.X, ALU.max))
                    tell(ts(small[:, 2, 0:MH], small[:, 4, 0:MH], -1.0, None, ALU.mult), S("pmax"))
                    dve.wait_ge(S("pexp"), count_at("pexp", l, t + 1))
                    step(dve.reciprocal(small[:, 5, 0:MH], small[:, 3, 0:MH]))
                    tell(tt(PR, PR, bc(small[:, 5, 0:MH].unsqueeze(2), P, MH, MEM), ALU.mult), S("pr_ready"))
                dve.wait_ge(S("spt_ps"), count_at("spt_ps", l, 1))
                for b in range(DB):
                    dve.wait_ge(S("pv_done"), count_at("pv_done", l, b + 1))
                    select(b, 5 - b % 2, "osel")

            def one_hot(dst, src, mx, n):
                step(red(mx, src, AX.X, ALU.max))
                step(tt(dst, src, bc(mx.unsqueeze(2), P, TT, n), ALU.is_equal))
                step(tt(dst, dst, bc(rev[:, 0:n].unsqueeze(1), P, TT, n), ALU.mult))
                step(red(small[:, 15, 0:TT], dst, AX.X, ALU.max))
                step(tt(dst, dst, bc(small[:, 15, 0:TT].unsqueeze(2), P, TT, n), ALU.is_equal))

            def moe(l):
                gm, m1, m2, dif, gw, w1, w2 = (small[:, n, 0:TT] for n in (4, 5, 7, 6, 8, 9, 10))
                dve.wait_ge(S("memv_out"), 16 * (l + 1))
                dve.wait_ge(S("router_in"), 16 * (GROUPS + 3) * (l + 1))
                step(dve.memset(LG, 0.0))
                dve.wait_ge(S("logits"), count_at("logits", l, 1))
                for t in range(TT):
                    R = ROWS[t]
                    step(tt(LG[0:R, t, :], ps[0:R, 0, t * 64:t * 64 + GROUPS + NE], router_b[0:R, :], ALU.add))
                one_hot(OHG, LG[:, :, 0:GROUPS], gm, GROUPS)
                step(tt(GE, LG[:, :, 0:GROUPS], bc(gm.unsqueeze(2), P, TT, GROUPS), ALU.subtract))
                for t in range(TT):
                    step(tt(EM[:, t, :, :], LG[:, t, GROUPS:].rearrange("p (g e) -> p g e", g=GROUPS),
                            bc(OHG[:, t, :].unsqueeze(2), P, GROUPS, EPG), ALU.mult))
                    step(red(SEL[:, t, :], EM[:, t, :, :].rearrange("p g e -> p e g"), AX.X, ALU.add))
                one_hot(OH1, SEL, m1, EPG)
                flat = [x.rearrange("p t e -> p (t e)") for x in (SEL, OH1)]
                step(stt(flat[0], flat[1], -3.0e38, flat[0], ALU.mult, ALU.add))
                one_hot(OH2, SEL, m2, EPG)
                tell(tt(dif, m2, m1, ALU.subtract), S("gdiff"))
                dve.wait_ge(S("gexp"), count_at("gexp", l, 1))
                step(red(gw, GE, AX.X, ALU.add))
                step(ts(w1, dif, 1.0, None, ALU.add))
                step(tt(w1, w1, gw, ALU.mult))
                step(dve.reciprocal(w1, w1))
                step(tt(w2, w1, dif, ALU.mult))
                step(tt(AS8, OH1, OH2, ALU.add))
                step(tt(OH1, OH1, bc(w1.unsqueeze(2), P, TT, EPG), ALU.mult))
                step(tt(OH2, OH2, bc(w2.unsqueeze(2), P, TT, EPG), ALU.mult))
                step(tt(WE8, OH1, OH2, ALU.add))
                step(tt(OHG, OHG, bc(valid[:].unsqueeze(2), P, TT, GROUPS), ALU.mult))
                for t in range(TT):
                    og = bc(OHG[:, t, :].unsqueeze(2), P, GROUPS, EPG)
                    for dst, src in ((ASG, AS8), (CMB, WE8)):
                        step(tt(dst[:, t, :].rearrange("p (g e) -> p g e", g=GROUPS), og, bc(src[:, t:t + 1, :], P, GROUPS, EPG), ALU.mult))
                step(dve.memset(ACC, 0.0))
                tell(dve.memset(small[:, 15, :], 0.0), S("assigned"))
                dve.wait_ge(S("ranks"), count_at("ranks", l, 1))
                step(red(small[:, 11, 0:1], ps[:, 1, TT * NE:(TT + 1) * NE], AX.X, ALU.max))
                step(ts(THR, iota[:, 1:1 + (NT - 1) // CAP], float(CAP), small[:, 11, 0:1], ALU.mult, ALU.is_lt))
                step(red(small[:, 12, 0:1], THR, AX.X, ALU.add))
                key = KEY.rearrange("p t e -> p (t e)")
                for t in range(TT):
                    step(stt(KEY[:, t, 0:NE], ps[:, 1, t * NE:(t + 1) * NE], 1.0, ASG[:, t, :], ALU.add, ALU.mult))
                step(ts(KEY[:, :, 0:NE], KEY[:, :, 0:NE], -1.0, None, ALU.add))
                step(ts(KEY[:, :, NE:], KEY[:, :, 0:2], -float(CAP), None, ALU.add))
                for n, free in enumerate(("xg_ps1", "pwt_ps", "ht", "h_ready")):
                    tell(dve.memset(small[:, 13, n:n + 1], 0.0), S(f"{free}{l}"))
                tell(dve.memset(PWT, 0.0), S(f"pwt_sb{l}"))
                tell(dve.memset(Y, 0.0), S(f"y_sb{l}"))
                tell(cp(rounds[:], small[0:1, 12, 0:1]), S("rounds_known"))
                rm1 = dve.value_load(rounds[0:1, 0:1], min_val=0, max_val=4)
                io = bc(iota[:, 0:CAP].unsqueeze(1), P, 2, CAP)

                def one_hots(e):
                    for t in range(TT):
                        k2 = KEY[:, t, e].unsqueeze(2)
                        tt(PG[:, t, :, :], io, bc(k2, P, 2, CAP), ALU.is_equal).then_inc(S(f"pg_part{l}"), 1)

                def move_gathered(it):
                    dve.wait_ge(S(f"xg_ps1{l}"), it + 2)
                    cp(XG[:, 4:8, :].rearrange("p k c -> p (k c)"), ps[:, 1, :]).then_inc(S(f"xg_d{l}"), 1)

                one_hots(slice(0, 2))
                move_gathered(0)
                with dve.Fori(0, rm1 + 1) as rd:
                    with dve.Fori(0, PAIRS) as p:
                        it = rd * PAIRS + p
                        dve.wait_ge(S(f"pg_part{l}"), it * TT + TT)
                        dve.wait_ge(S(f"pwt_ps{l}"), it + 1)
                        for t in range(TT):
                            w2e = CMB[:, t, bass.ds(p * 2, 2)].unsqueeze(2)
                            tt(PW[:, t, :, :], PG[:, t, :, :], bc(w2e, P, 2, CAP), ALU.mult).then_inc(S(f"pw_part{l}"), 1)
                        dve.wait_ge(S(f"pw_part{l}"), it * TT + TT)
                        dve.wait_ge(S(f"xg_ps1{l}"), it + 2)
                        one_hots(bass.ds(p * 2 + 2, 2))
                        dve.wait_ge(S(f"sg{l}"), it + 1)
                        dve.wait_ge(S(f"up_done{l}"), it + 1)
                        tt(HS, SG, ps[:, 3, :], ALU.mult).then_inc(S(f"h_ready{l}"), 1)
                        move_gathered(it + 1)
                        for n in range(2 * TT):
                            t, j = n // 2, n % 2
                            dve.wait_ge(S(f"scat{l}"), it * (2 * TT) + (n + 1))
                            a = ACC[0:ROWS[t], t, j * HALF:(j + 1) * HALF]
                            tt(a, a, ps[0:ROWS[t], 7 - n % 2, :], ALU.add).then_inc(S(f"acc{l}"), 1)
                    dve.wait_ge(S(f"pg_part{l}"), rd * (PAIRS * TT) + (PAIRS + 1) * TT)
                    ts(key, key, -float(CAP), None, ALU.add).then_inc(S(f"round_end{l}"), 1)
                    dve.wait_ge(S(f"round_end{l}"), rd + 1)
                for n in range(2 * TT):
                    t, j = n // 2, n % 2
                    dve.wait_ge(S(f"scat{l}"), rm1 * (PAIRS * 2 * TT) + (PAIRS * 2 * TT + n + 1))
                    a = ACC[0:ROWS[t], t, j * HALF:(j + 1) * HALF]
                    tt(a, a, ps[0:ROWS[t], 7 - n % 2, :], ALU.add).then_inc(S(f"acc{l}"), 1)
                dve.wait_ge(S(f"acc{l}"), rm1 * (PAIRS * 2 * TT) + (PAIRS + 1) * 2 * TT)

            dve.wait_ge(S("iota_ps"), 1)
            step(cp(iota[:], ps[:, 0, 0:P]))
            tell(ts(rev[:], iota[:, 0:EPG], -1.0, float(EPG), ALU.mult, ALU.add), S("iota_ready"))
            for l in range(DEPTH):
                mixer(l)
                norm(1 + 3 * l)
                attention(l)
                norm(2 + 3 * l)
                moe(l)
                norm(3 + 3 * l, ACC)


_INS = ["x_prompt", "x_sample", "state_hgrn", "state_conv", "state_gla", "cache_mem_k", "cache_mem_v", "mem_prompt",
        "w_in_a", "lb_a", "conv_w", "gnorm_a", "w_out_a", "w_in_c", "w_gk2", "b_gk2", "gnorm_c", "w_out_c",
        "w_mq", "w_mk", "w_mv", "w_mo", "ln_g", "ln_b", "w_grp", "b_grp", "w_er", "b_er", "w_gate", "w_up", "w_down"]


def kernel(**inputs):
    import numpy as _np
    import concourse.bacc as _bacc
    from concourse.bass_utils import run_bass_kernel_spmd as _run

    nc = _bacc.Bacc("TRN2", target_bir_lowering=False, num_devices=1)
    arrays, I, O = {}, {}, {}
    for name in _INS:
        a = _np.ascontiguousarray(inputs[name])
        arrays[f"in_{name}"] = a
        I[name] = nc.dram_tensor(f"in_{name}", a.shape, mybir.dt.from_np(a.dtype), kind="ExternalInput").ap()
    like = {k: inputs[k].shape for k in _INS}
    depth, _, mem, mh, mhd = like["cache_mem_k"]
    outs = [
        ("y_prompt", like["x_prompt"]), ("y_sample", like["x_sample"]),
        ("hgrn_p", (like["state_hgrn"][0], 1) + tuple(like["state_hgrn"][2:])),
        ("conv_p", (like["state_conv"][0], 1) + tuple(like["state_conv"][2:])),
        ("gla_p", (like["state_gla"][0], 1) + tuple(like["state_gla"][2:])),
        ("mem_k", (depth, 1, mem, mh, mhd)), ("mem_v", (depth, 1, mem, mh, mhd)),
        ("hgrn_s", like["state_hgrn"]), ("conv_s", like["state_conv"]), ("gla_s", like["state_gla"]),
    ]
    for name, shape in outs:
        O[name] = nc.dram_tensor(f"out_{name}", tuple(shape), F32, kind="ExternalOutput").ap()
    build(nc, I, O)
    r = _run(nc, [arrays], core_ids=[0])
    return tuple(r.results[0][f"out_{name}"] for name, _ in outs)
```

```python
from contextlib import ExitStack

import concourse.bass as bass
from concourse import mybir

ALU = mybir.AluOpType
ACT = mybir.ActivationFunctionType
AX = mybir.AxisListType
F32 = mybir.dt.float32
I32 = mybir.dt.int32
P = 128


class Steps:

    def __init__(self, eng, own, base=0):
        self.eng, self.own, self.base, self.n, self.told = eng, own, base, 0, {}

    def step(self, ins):
        self.n += 1
        ins.then_inc(self.own, 1)
        self.eng.wait_ge(self.own, self.base + self.n)

    def tell(self, ins, sem, base=0):
        self.told[sem.name] = self.told.get(sem.name, 0) + 1
        ins.then_inc(sem, 1)
        self.eng.wait_ge(sem, base + self.told[sem.name])


def build(nc, I, O):
    _, SEQ, D = I["x_prompt"].shape
    DB, DS, _ = I["x_sample"].shape
    NA, _, HEADS, DK, HDV = I["state_hgrn"].shape
    NC_, GDV = I["state_gla"].shape[0], I["state_gla"].shape[4]
    DEPTH, _, MEM, MH, MHD = I["cache_mem_k"].shape
    GROUPS, EPG, _, DE = I["w_gate"].shape[1:]
    CW = I["conv_w"].shape[1]
    NE = GROUPS * EPG
    KC = D // P
    NS = DB * DS
    NT = SEQ + NS
    PT_ = SEQ // P
    ROWS = [P] * PT_ + [NS]
    TT = len(ROWS)
    ORDER = [PT_] + list(range(PT_))
    HALF = 512
    SLOTS = 6
    CAP = 64
    PAIRS = NE // 2
    SCATTERS = 2 * PT_ + 1
    LEVELS = 8
    SL = 3
    MT_ = MEM // P
    RANK = I["w_gk2"].shape[1]
    ALPHA = (2.0 * DEPTH) ** 0.25
    LN_EPS, RMS_EPS = 1e-5, 1e-6
    assert NA == 1 and NC_ == 1 and DEPTH == 2 and PT_ == 2 and DK == P and DS == 4 and D == 1024
    DVC = [HDV // P, GDV // P]

    def cols(t):
        return slice(t * P, t * P + ROWS[t])

    ctx = ExitStack()
    with ctx:
        sems = {}

        def S(name):
            if name not in sems:
                sems[name] = ctx.enter_context(nc.semaphore(name))
            return sems[name]

        def sb(name, shape, dt=F32):
            return ctx.enter_context(nc.sbuf_tensor(name, shape, dt))

        ones = sb("ones", [P, P])
        masks = sb("masks", [P, LEVELS, P])
        ident = masks[:, 0, :]
        fold = sb("fold", [P, NS])
        own = sb("own", [P, 2])
        upper = sb("upper", [P, P])
        iota = sb("iota", [P, P])
        bmask = sb("bmask", [P, DB])
        carry = sb("carry", [P, NT])
        valid = sb("valid", [P, TT])
        W = sb("W", [P, SLOTS, KC * HALF])
        X = sb("X", [P, TT, D])
        XT = sb("XT", [P, KC, NT])
        GB = sb("GB", [P, 2, D])
        convw = sb("convw", [P, CW // P, 3])
        gnorm = [sb(f"gnorm{l}", [P, DVC[l]]) for l in range(2)]
        wgz = sb("wgz", [P, KC, RANK])
        wgk2 = sb("wgk2", [RANK, HEADS * DK])
        bgk2 = sb("bgk2", [P, HEADS])
        gz = sb("gz", [RANK, NT])
        router_w = sb("router_w", [P, KC, GROUPS + NE])
        router_b = sb("router_b", [P, GROUPS + NE])
        stat = sb("stat", [P, 2, 6])
        mv = sb("mv", [P, 4])
        small = sb("small", [P, 16, 4])
        rev = sb("rev", [P, EPG])
        rounds = sb("rounds", [1, 1], I32)
        SCR_WORDS = nc.sbuf_bytes_remaining // 4 - 8
        scr = sb("scr", [P, SCR_WORDS])
        ps = ctx.enter_context(nc.psum_tensor("ps", [P, 8, HALF], F32))

        class Region:

            def __init__(self):
                self.at = 0

            def take(self, *shape, rows=P):
                n = 1
                for x in shape:
                    n *= x
                assert self.at + n <= SCR_WORDS, (self.at + n, SCR_WORDS)
                v = scr[0:rows, self.at:self.at + n]
                self.at += n
                if len(shape) == 2:
                    v = v.rearrange("p (a b) -> p a b", a=shape[0])
                if len(shape) == 3:
                    v = v.rearrange("p (a b c) -> p a b c", a=shape[0], b=shape[1])
                return v

        MIX = []
        for l in range(2):
            r, nv = Region(), DVC[l] * P
            m = dict(q=r.take(HEADS, NT), k=r.take(HEADS, NT), b=r.take(HEADS, NT),
                     g=r.take(HEADS * DVC[l], NT), v=r.take(TT, HEADS * nv),
                     qkd=r.take(2 * NT), kexp_all=r.take(DB * P),
                     o=r.take(KC, NT), ktok=r.take(TT, P), sq=r.take(DVC[l], NT), rs=r.take(NT),
                     s1=r.take(nv), sf=r.take(nv), dec=[r.take(DB + PT_), small[:, :, :].rearrange("p a b -> p (a b)")[:, 0:DB + PT_]],
                     s0=r.take(DB, nv))
            m["qd"] = m["qkd"][:, 0:NT]
            m["conv_rows"] = m["qkd"][:, 0:CW]
            m["kexp"] = m["kexp_all"][0:NS, :].rearrange("p (b d) -> p b d", b=DB)
            mark = r.at
            m["ms"], m["st"] = r.take(LEVELS, P), r.take(TT, P)
            spare = GB[:, :, :].rearrange("p a d -> p (a d)")
            m["qk"] = [spare[:, 0:(LEVELS - 1) * NT].rearrange("p (v t) -> p v t", v=LEVELS - 1), XT[:, 0:LEVELS - 1, :]]
            m["kd"] = [m["qkd"][:, NT:2 * NT], XT[:, LEVELS - 1, :]]
            m["tmp"] = m["o"][:, 0:HEADS, :]
            m["so"] = m["sq"].rearrange("p c t -> p (c t)")[:, 0:2 * nv].rearrange("p (r v) -> p r v", r=2)
            if l == 0:
                m["conv"] = [r.take(CW // P, NT) for _ in range(3)]
                r.at = mark
                m["up"], m["us"] = r.take(CW // P, SEQ + 2), r.take(CW // P, DB, 6)
            MIX.append(m)

        def halves(x, lv, upto):
            v = x[:, 0:upto].rearrange("p (n two h) -> p n two h", two=2, h=(1 << lv) // 2)
            return v[:, :, 0, :], v[:, :, 1, :]

        conv_in = MIX[0]["conv_rows"][0:2 * DB, :]
        conv_tok = MIX[0]["kexp_all"][0:2 + 2 * DB, 0:CW]
        conv_tail = MIX[0]["s1"][:, 0:(CW // P) * (2 + 2 * DB)].rearrange("p (c n) -> p c n", c=CW // P)
        r = Region()
        QT, KTP, VP = r.take(KC, NT), r.take(KC, MEM), r.take(MT_, D)
        KV = [r.take(MT_, D) for _ in range(3)]
        KT0 = r.take(KC, MEM)
        at = r.at
        PR = r.take(MH, MEM)
        PRT = r.take(MT_, MH * P)
        r.at = at
        KT = [KT0, r.take(KC, MEM)]
        SS, SST = r.take(MEM), r.take(MT_, P)
        OA = XT
        r = Region()
        LG, OHG, GE = r.take(TT, GROUPS + NE), r.take(TT, GROUPS), r.take(TT, GROUPS)
        SEL, OH1, OH2, WE8, AS8 = (r.take(TT, EPG) for _ in range(5))
        EM, THR = r.take(TT, GROUPS, EPG), r.take((NT - 1) // CAP)
        ASG, CMB, KEY = r.take(TT, NE), r.take(TT, NE), r.take(TT, NE + 2)
        PG, PW, PWT = r.take(TT, 2, CAP), r.take(TT, 2, CAP), r.take(NT)
        XG, SG, HS, HT = r.take(KC, P), r.take(DE), r.take(DE), r.take(DE // P, P)
        Y, ACC = r.take(D), r.take(TT, D)
        GATE_ODD = r.take(2, KC * HALF)
        EXPERT = {("gate", 0): W[:, 0:2, :], ("gate", 1): GATE_ODD, ("up", 0): W[:, 2:4, :], ("down", 0): W[:, 4:6, :]}

        def unit_cols(w, a):
            return w[:, a:a + HALF].rearrange("(k p) n -> p k n", p=P)

        wia, woa, wic, woc = I["w_in_a"][0], I["w_out_a"][0], I["w_in_c"][0], I["w_out_c"][0]
        F = HEADS * DK
        in_cols = [
            [("bg", 4 * F), ("cg", 5 * F), ("h", 6 * F), ("f", F), ("q", 0), ("g", 3 * F), ("v", 2 * F)],
            [("q", 0), ("k", F), ("g", 4 * F), ("g1", 5 * F), ("v", 2 * F), ("v1", 3 * F)],
        ]
        units = []
        for l in range(DEPTH):
            while len(units) % SLOTS:
                units.append(None)
            for name, a in in_cols[l]:
                units.append((l, name, unit_cols([wia, wic][l], a)))
            for j in range(2):
                units.append((l, f"out{j}", unit_cols([woa, woc][l], j * HALF)))
            for name in ("mk", "mv", "mq", "mo"):
                for j in range(2):
                    units.append((l, f"{name}{j}", unit_cols(I[f"w_{name}"][l], j * HALF)))
        UNIT = {u[:2]: n for n, u in enumerate(units) if u}

        def wslot(l, name):
            return W[:, UNIT[l, name] % SLOTS, :].rearrange("p (k n) -> p k n", k=KC)

        def loads_in(n):
            return sum(1 for m in range(n % SLOTS, n + 1, SLOTS) if units[m])

        def unit_landed(eng, l, name):
            n = UNIT[l, name]
            eng.wait_ge(S(f"w_in{n % SLOTS}"), 16 * loads_in(n))

        jobs = {}
        order = []

        def plan(stage, *names):
            jobs.setdefault(stage, [])
            for name in names:
                jobs[stage].append((len(order), name))
                order.append((stage, name))

        def plan_xt(inst):
            plan(("xt", inst), *[("xt", t, h) for t in (0, PT_, 1) for h in range(2)])

        plan_xt(0)
        for l in range(DEPTH):
            for name, _ in in_cols[l]:
                if name[0] != "v":
                    plan(("in", l), *[("feat", name, c) for c in range(4)])
                else:
                    plan(("in", l), *[("tok", name, t) for t in range(TT)])
                if l == 1 and name == "k":
                    plan(("in", l), ("gz", "gz", 0), *[("gk", "gk", c) for c in range(4)])
            plan(("mem", l), *[("mt", i, h) for i in range(MT_) for h in range(2)])
            plan(("mem", l), *[("memtok", f"{w}{j}", i) for w in ("mk", "mv") for j in range(2) for i in range(MT_)])
            plan_xt(1 + 3 * l)
            plan(("mq", l), *[("feat", f"mq{j}", c) for j in range(2) for c in range(4)])
            plan_xt(2 + 3 * l)
            if l + 1 < DEPTH:
                plan_xt(3 + 3 * l)

        def number(stage, name=None):
            return max(n for n, j in jobs[stage] if name is None or j[1] == name) + 1

        def part(stage, after=None, upto=None):
            lo = number(stage, after) if after else 0
            hi = number(stage, upto) if upto else number(stage)
            return [j for j in jobs[stage] if lo <= j[0] < hi]

        GATES, QUERIES = ("f", "gk"), ("q", "gk")

        def kv_loads(l, i):
            return l * len(range(i % 3, 2 * DB, 3)) + i // 3 + 1

        per_layer = dict(
            softplus=1, b_ready=HEADS, e_ready=HEADS, qd_exp=HEADS, qd_ready=HEADS, ex_ready=HEADS, ktok_ps=HEADS, ktok=HEADS, s_ps=HEADS,
            s1_ready=HEADS, o_ps=HEADS, sq_ready=HEADS, ms_ready=HEADS, root=HEADS, score_ps=TT * HEADS,
            kd_ready=HEADS, qk_ready=HEADS, st_ready=TT * HEADS, kexp=HEADS, ns_ps=2 * HEADS, so_ps=HEADS, so_ready=HEADS, state_half=HEADS, ss_ps=HEADS,
            rms=HEADS, state_new=HEADS, state_out=32 * HEADS, early_out=16 * HEADS, kt_full=4 * (DB + 1), kt_a=2 * (DB + 1), kt_d=2
            * (DB + 1), ssc=DB, ssel=DB, osel=DB, os_ps=1, smax=1, sexp=1, sp_ready=1, spt_ps=1, spt_sb=1, psc=PT_,
            pmax=PT_, pexp=PT_, pr_ready=PT_, prt_ps=PT_, prt_sb=PT_, po_ps=PT_, oa_ready=TT, pv_done=DB,
            memk_out=16, logits=1, assigned=1, ranks=1, rounds_known=1, gdiff=1, gexp=1)

        def count_at(name, l, n):
            return l * per_layer[name] + n

        LNS = 3 * DEPTH
        mem_src = I["mem_prompt"][0].rearrange("(i p) d -> p i d", p=P)
        EXPERT_UNITS = ("gate", "up", "down")
        gate_rows = I["w_gate"].rearrange("l g e (k p) f -> (l g e) p k f", p=P)
        up_rows = I["w_up"].rearrange("l g e (k p) f -> (l g e) p k f", p=P)
        down_rows = I["w_down"].rearrange("l g e (k p) d -> (l g e) p k d", p=P)

        block = ctx.enter_context(nc.Block())

        @block.sync
        def _(sp):
            for t in range(PT_):
                sp.dma_start(X[:, t, :], I["x_prompt"][0, t * P:(t + 1) * P, :]).then_inc(S("x_in"), 16)
            sp.dma_start(X[0:NS, PT_, :], I["x_sample"].rearrange("b t d -> (b t) d")).then_inc(S("x_in"), 16)

            def used(n):
                l, name = units[n][:2]
                if name.startswith("out") or name.startswith("mo"):
                    i = 2 * l + (name[:2] == "mo")
                    sp.wait_ge(S("mix_unit"), 2 * i + int(name[-1]) + 1)
                else:
                    stage = ("in", l) if name[:2] not in ("mk", "mv", "mq") else ("mq", l) if name[:2] == "mq" else ("mem", l)
                    sp.wait_ge(S("pipe_full"), number(stage, name))

            n = 0
            rm1 = None
            for l in range(DEPTH):
                end = max(UNIT[k] for k in UNIT if k[0] == l) + 1
                start = min(UNIT[k] for k in UNIT if k[0] == l)
                s_in = (I["state_hgrn"], I["state_gla"])[l][0].rearrange("b h k v -> h k b v")
                s_out = O[("hgrn_s", "gla_s")[l]][0].rearrange("b h k v -> h k b v")
                p_out = O[("hgrn_p", "gla_p")[l]][0, 0]
                for n in range(start, end):
                    if n == start + SLOTS:
                        if l:
                            sp.wait_ge(S("ln_done"), 9 * l)
                        sp.dma_start(MIX[l]["s0"], s_in[0]).then_inc(S(f"s0_in{l}"), 16)
                    if n == UNIT[l, "out0"] + SLOTS:
                        for h in range(HEADS):
                            early, late = (slice(0, DB // 2), slice(DB // 2, DB))
                            s0 = MIX[l]["s0"]
                            sp.wait_ge(S("state_half"), count_at("state_half", l, h + 1))
                            sp.dma_start(s_out[h][:, early], s0[:, early]).then_inc(S("early_out"), 16)
                            sp.wait_ge(S("state_new"), count_at("state_new", l, h + 1))
                            sp.dma_start(s_out[h][:, late], s0[:, late]).then_inc(S("state_out"), 16)
                            sp.dma_start(p_out[h], MIX[l]["sf"]).then_inc(S("state_out"), 16)
                            sp.wait_ge(S("early_out"), count_at("early_out", l, 16 * (h + 1)))
                            if h + 1 < HEADS:
                                sp.dma_start(s0[:, early], s_in[h + 1][:, early]).then_inc(S(f"s0_in{l}"), 16)
                                sp.wait_ge(S("state_out"), count_at("state_out", l, 32 * (h + 1)))
                                sp.dma_start(s0[:, late], s_in[h + 1][:, late]).then_inc(S(f"s0_in{l}"), 16)
                    if n - SLOTS >= start:
                        used(n - SLOTS)
                    elif l:
                        sp.wait_ge(S(f"{EXPERT_UNITS[n % SLOTS // 2]}_done{l - 1}"), rm1 * PAIRS + PAIRS)
                    sp.dma_start(W[:, n % SLOTS, :].rearrange("p (k n) -> p k n", k=KC), units[n][2]).then_inc(S(f"w_in{n % SLOTS}"), 16)

                def load_expert_half(which, odd, j, pair):
                    base, k = {"gate": (gate_rows, KC), "up": (up_rows, KC), "down": (down_rows, DE // P)}[which]
                    dst = EXPERT[which, odd][:, j, :].rearrange("p (k n) -> p k n", k=k)
                    sp.dma_start(dst, base[pair * 2 + (l * NE + j)]).then_inc(S(f"{which}{odd}_in{l}"), 16)

                def load_expert_pair(which, odd, pair):
                    for j in range(2):
                        load_expert_half(which, odd, j, pair)

                caches = [I[name][l, b].rearrange("(i p) h d -> p i (h d)", p=P) for name in ("cache_mem_k", "cache_mem_v") for b in range(DB)]
                for i in range(2 * DB):
                    if i == 0:
                        sp.wait_ge(S("pipe_full"), jobs[("mem", l)][2 * MT_ - 1][0] + 1)
                    elif i == 1:
                        sp.wait_ge(S("pipe_free"), number(("mem", l)))
                    elif i < DB + 3:
                        if i == 2:
                            sp.wait_ge(S("memk_out"), count_at("memk_out", l, 16))
                        sp.wait_ge(S("kt_full"), count_at("kt_full", l, 4 * (i - 1)))
                    else:
                        sp.wait_ge(S("pv_done"), count_at("pv_done", l, i - 3 - DB + 1))
                    sp.dma_start(KV[i % 3], caches[i]).then_inc(S(f"kv_in{i % 3}"), 16)

                for n in range(end - SLOTS, end):
                    if n == UNIT[l, "mo0"]:
                        sp.wait_ge(S("memv_out"), 16 * (l + 1))
                        sp.wait_ge(S("oa_ready"), count_at("oa_ready", l, TT))
                        load_expert_pair("gate", 1, 1)
                    used(n)
                    s = n % SLOTS
                    load_expert_half(EXPERT_UNITS[s // 2], 0, s % 2, 0)
                sp.wait_ge(S("rounds_known"), count_at("rounds_known", l, 1))
                rm1 = sp.value_load(rounds[0:1, 0:1], min_val=0, max_val=4)
                with sp.Fori(0, rm1 * (PAIRS // 2) + (PAIRS // 2 - 1)) as ii:
                    for odd in range(2):
                        i = ii * 2 + odd
                        sp.wait_ge(S(f"gate_done{l}"), i + 1)
                        load_expert_pair("gate", odd, (i + 2) % PAIRS)
                        for which in ("up", "down"):
                            sp.wait_ge(S(f"{which}_done{l}"), i + 1)
                            load_expert_pair(which, 0, (i + 1) % PAIRS)
                for which in ("up", "down"):
                    sp.wait_ge(S(f"{which}_done{l}"), rm1 * PAIRS + (PAIRS - 1))
                    load_expert_pair(which, 0, PAIRS - 1)

        @block.gpsimd
        def _(pool):
            st = Steps(pool, S("pool_step"))
            pool.dma_start(conv_in, I["state_conv"][0].rearrange("b j w -> (b j) w")).then_inc(S("conv_in"), 16)
            st.step(pool.memset(ones[:], 1.0))
            st.step(pool.memset(masks[:], 0.0))
            st.step(pool.affine_select(out=ident, in_=ones[:], compare_op=ALU.is_equal, fill=0.0, base=0,
                                       pattern=[[1, P]], channel_multiplier=-1))
            st.tell(pool.affine_select(out=upper[:], in_=ones[:], compare_op=ALU.is_gt, fill=0.0, base=0,
                                       pattern=[[1, P]], channel_multiplier=-1), S("consts"))
            for lv in range(1, LEVELS):
                B = 1 << lv
                right = masks[:, lv, :].rearrange("p (n two h) -> p n two h", two=2, h=B // 2)[:, :, 1, :]
                one = ones[:].rearrange("p (n two h) -> p n two h", two=2, h=B // 2)[:, :, 1, :]
                st.step(pool.affine_select(out=right, in_=one, compare_op=ALU.is_ge, fill=0.0, base=0,
                                           pattern=[[-B, P // B], [0, B // 2]], channel_multiplier=1))
                st.step(pool.affine_select(out=right, in_=right, compare_op=ALU.is_ge, fill=0.0, base=B // 2 - 1,
                                           pattern=[[B, P // B], [0, B // 2]], channel_multiplier=-1))
            for j in range(MH):
                quarter = bmask[j * NS:(j + 1) * NS, :]
                st.step(pool.affine_select(out=quarter, in_=ones[j * NS:(j + 1) * NS, 0:DB], compare_op=ALU.is_ge, fill=0.0, base=0,
                                           pattern=[[-DS, DB]], channel_multiplier=1))
                st.step(pool.affine_select(out=quarter, in_=quarter, compare_op=ALU.is_ge, fill=0.0, base=DS - 1,
                                           pattern=[[DS, DB]], channel_multiplier=-1))
            for j in range(MH):
                rows = slice(j * NS, (j + 1) * NS)
                st.step(pool.tensor_copy(fold[rows, :], ident[rows, rows]))
                st.step(pool.tensor_copy(own[rows, :], bmask[rows, :].rearrange("p (r j) -> p r j", r=2)[:, :, j]))
            st.step(pool.memset(carry[:], 1.0))
            st.step(pool.memset(carry[:, 0:SEQ].rearrange("p (t c) -> p t c", c=P)[:, :, 0], 0.0))
            st.step(pool.memset(carry[:, SEQ:NT].rearrange("p (b t) -> p b t", t=DS)[:, :, 0], 0.0))
            st.step(pool.memset(valid[:], 1.0))
            st.step(pool.memset(valid[:, TT - 1:TT], 0.0))
            st.tell(pool.memset(valid[0:NS, TT - 1:TT], 1.0), S("tables"))

            def load(dst, src, sem):
                pool.dma_start(dst, src, allow_slow_non_contiguous=True).then_inc(S(sem), 16)

            load(convw[:], I["conv_w"][0].rearrange("(c p) j -> p c j", p=P), "small_in")
            for l in range(2):
                load(gnorm[l][:], I[("gnorm_a", "gnorm_c")[l]][0].rearrange("(c p) -> p c", p=P), "small_in")
            load(wgz[:], wic[:, 6 * F:6 * F + RANK].rearrange("(k p) n -> p k n", p=P), "small_in")
            load(wgk2[:], I["w_gk2"][0], "small_in")
            load(bgk2[:], I["b_gk2"][0].rearrange("(c p) -> p c", p=P), "small_in")

            for l in range(DEPTH):
                m = MIX[l]
                if l == 0:
                    pool.wait_ge(S("conv_out"), 1)
                    pool.dma_start(O["conv_p"][0, 0], conv_tok[0:2, :]).then_inc(S("stores"), 16)
                    pool.dma_start(O["conv_s"][0].rearrange("b j w -> (b j) w"), conv_tok[2:2 + 2 * DB, :]).then_inc(S("stores"), 16)
                tt = pool.tensor_tensor

                def exponents(h):
                    b, qk, kd, dec = m["b"][:, h, :], m["qk"][h % 2], m["kd"][h % 2], m["dec"][h % 2]
                    pool.wait_ge(S("b_ready"), count_at("b_ready", l, h + 1))
                    if h == 1:
                        pool.wait_ge(S("pipe_full"), number(("in", l)))
                    if h >= 2:
                        pool.wait_ge(S("state_new"), count_at("state_new", l, h - 1))
                    for lv in range(1, LEVELS):
                        upto, half = (NT if lv < SL else SEQ), (1 << lv) // 2
                        (bl, br), (el, er) = halves(b, lv, upto), halves(qk[:, lv - 1, :], lv, upto)
                        mid = bl[:, :, half - 1:half].to_broadcast([P, upto // (2 * half), half])
                        tt(el, mid, bl, ALU.subtract)
                        tt(er, br, mid, ALU.subtract)
                    bp = b[:, 0:SEQ].rearrange("p (t c) -> p t c", t=PT_)
                    bs = b[:, SEQ:].rearrange("p (b t) -> p b t", b=DB)
                    tt(kd[:, 0:SEQ].rearrange("p (t c) -> p t c", t=PT_), bp[:, :, P - 1:P].to_broadcast([P, PT_, P]), bp, ALU.subtract)
                    tt(kd[:, SEQ:].rearrange("p (b t) -> p b t", b=DB), bs[:, :, DS - 1:DS].to_broadcast([P, DB, DS]), bs, ALU.subtract)
                    pool.tensor_copy(dec[:, 0:PT_], bp[:, :, P - 1])
                    st.tell(pool.tensor_copy(dec[:, PT_:], bs[:, :, DS - 1]), S("e_ready"))

                exponents(0)
                for h in range(HEADS):
                    if h + 1 < HEADS:
                        exponents(h + 1)
                    pool.wait_ge(S("ktok"), count_at("ktok", l, h + 1))
                    if h:
                        pool.wait_ge(S("ns_ps"), count_at("ns_ps", l, 2 * h))
                    elif l == 0:
                        pool.wait_ge(S("stores"), 32)
                    st.tell(tt(m["kexp"], m["ktok"][0:NS, PT_:PT_ + 1, :].to_broadcast([NS, DB, P]),
                               bmask[0:NS].unsqueeze(2).to_broadcast([NS, DB, P]), ALU.mult), S("kexp"))
                pool.wait_ge(S("state_out"), count_at("state_out", l, 32 * HEADS))
                pool.wait_ge(S("early_out"), count_at("early_out", l, 16 * HEADS))

                pool.wait_ge(S("rms"), count_at("rms", l, HEADS))
                load(VP, mem_src, "mem_in")
                load(router_w[:, :, 0:GROUPS], I["w_grp"][l].rearrange("(k p) g -> p k g", p=P), "router_in")
                for g in range(GROUPS):
                    load(router_w[:, :, GROUPS + g * EPG:GROUPS + (g + 1) * EPG],
                         I["w_er"][l, g].rearrange("(k p) e -> p k e", p=P), "router_in")
                load(router_b[:, 0:GROUPS], I["b_grp"][l].partition_broadcast(P), "router_in")
                load(router_b[:, GROUPS:], I["b_er"][l].rearrange("g e -> (g e)").partition_broadcast(P), "router_in")
                pool.wait_ge(S("pipe_free"), number(("mem", l)))
                pool.dma_start(O["mem_k"][l, 0].rearrange("(i p) h d -> p i (h d)", p=P), KV[2]).then_inc(S("memk_out"), 16)
                pool.dma_start(O["mem_v"][l, 0].rearrange("(i p) h d -> p i (h d)", p=P), VP).then_inc(S("memv_out"), 16)

                pool.wait_ge(S("memv_out"), 16 * (l + 1))
                pool.wait_ge(S("oa_ready"), count_at("oa_ready", l, TT))
                pool.memset(ACC, 0.0)
                pool.memset(PWT, 0.0)
                st.tell(pool.memset(Y, 0.0), S("zeros"))

            for n, t in enumerate(ORDER):
                pool.wait_ge(S("ln_done"), 3 * (LNS - 1) + n + 1)
                dst = O["y_prompt"][0, t * P:(t + 1) * P, :] if t < PT_ else O["y_sample"].rearrange("b t d -> (b t) d")
                pool.dma_start(dst, X[0:ROWS[t], t, :]).then_inc(S("stores"), 16)
            pool.wait_ge(S("memv_out"), 16 * DEPTH)
            pool.wait_ge(S("stores"), 16 * (2 + TT))

        @block.tensor
        def _(pe):
            mm, tr = pe.matmul, pe.transpose

            def run_jobs(stage, some=None):
                for n, (kind, name, c) in some or jobs[stage]:
                    if n >= 2:
                        pe.wait_ge(S("pipe_free"), n - 1)
                    bank = ps[:, 6 + n % 2, :]
                    l = stage[1]
                    if kind == "xt":
                        t, h = name, c
                        if h == 0 and stage[1] == 0:
                            pe.wait_ge(S("x_in"), 16 * TT)
                            pe.wait_ge(S("consts"), 1)
                        elif h == 0:
                            pe.wait_ge(S("ln_done"), 3 * (stage[1] - 1) + ORDER.index(t) + 1)
                        for k in range(4):
                            last = tr(bank[:, k * P:k * P + ROWS[t]], X[0:ROWS[t], t, (4 * h + k) * P:(4 * h + k + 1) * P],
                                      ident[0:ROWS[t], 0:ROWS[t]])
                    elif kind == "feat":
                        if c == 0:
                            unit_landed(pe, l, name)
                        w = wslot(l, name)
                        for k in range(KC):
                            last = mm(bank[:, 0:NT], w[:, k, c * P:(c + 1) * P], XT[:, k, :], start=(k == 0), stop=(k == KC - 1))
                    elif kind == "gz":
                        pe.wait_ge(S("small_in"), 16 * 6)
                        for k in range(KC):
                            last = mm(bank[0:RANK, 0:NT], wgz[:, k, :], XT[:, k, :], start=(k == 0), stop=(k == KC - 1))
                    elif kind == "gk":
                        if c == 0:
                            pe.wait_ge(S("pipe_free"), number(("in", 1), "gz"))
                        last = mm(bank[:, 0:NT], wgk2[:, c * P:(c + 1) * P], gz[:], start=True, stop=True)
                    elif kind == "tok":
                        if c == 0:
                            unit_landed(pe, l, name)
                        w = wslot(l, name)
                        for k in range(KC):
                            if c < PT_:
                                last = mm(bank[:, :], XT[:, k, cols(c)], w[:, k, :], start=(k == 0), stop=(k == KC - 1))
                                continue
                            for q in range(4):
                                last = mm(bank[q * NS:(q + 1) * NS, 0:P], XT[:, k, SEQ:NT], w[:, k, q * P:(q + 1) * P],
                                          start=(k == 0), stop=(k == KC - 1))
                    elif kind == "mt":
                        i, h = name, c
                        if i == 0 and h == 0:
                            pe.wait_ge(S("mem_in"), 16 * (l + 1))
                        for k in range(4):
                            last = tr(bank[:, k * P:(k + 1) * P], VP[:, i, (4 * h + k) * P:(4 * h + k + 1) * P], ident)
                    elif kind == "memtok":
                        if c == 0:
                            unit_landed(pe, l, name)
                        if name == "mk0" and c == 0:
                            pe.wait_ge(S("pipe_free"), n)
                        w = wslot(l, name)
                        memT = KV[1].rearrange("p i d -> p (i d)").rearrange("p (k m) -> p k m", k=KC)
                        for k in range(KC):
                            last = mm(bank, memT[:, k, c * P:(c + 1) * P], w[:, k, :], start=(k == 0), stop=(k == KC - 1))
                    last.then_inc(S("pipe_full"), 1)
                if some is None or some[-1][0] + 1 == number(stage):
                    pe.wait_ge(S("pipe_free"), number(stage))

            def project_out(l, src, which, inst):
                w = [wslot(l, f"{which}{j}") for j in range(2)]
                def prompt(j, t):
                    for k in range(KC):
                        last = mm(ps[:, 2 * t + j, :], src[:, k, cols(t)], w[j][:, k, :], start=(k == 0), stop=(k == KC - 1))
                    return last

                unit_landed(pe, l, f"{which}0")
                for t in range(PT_):
                    prompt(0, t)
                unit_landed(pe, l, f"{which}1")
                for k in range(KC):
                    for q in range(4):
                        last = mm(ps[q * NS:(q + 1) * NS, 4, 0:D // 4], src[:, k, SEQ:NT],
                                  w[q // 2][:, k, q % 2 * (D // 4):(q % 2 + 1) * (D // 4)], start=(k == 0), stop=(k == KC - 1))
                last.then_inc(S("mix_unit"), 1)
                prompt(1, 0).then_inc(S("mix_done"), 1)
                prompt(1, 1).then_inc(S("mix_unit"), 1)

            def mixer(l):
                m, dvc = MIX[l], DVC[l]
                nv = dvc * P
                o_bank = [5, 6]
                ktok_bank = 6 - l
                for h in range(HEADS):
                    qk, kd = m["qk"][h % 2], m["kd"][h % 2]

                    def score(lv, t, out):
                        a, b = (m["k"][:, h, cols(t)], m["q"][:, h, cols(t)]) if lv == 0 else (qk[:, lv - 1, cols(t)],) * 2
                        return mm(out, a, b, start=True, stop=True)

                    pe.wait_ge(S("qk_ready"), count_at("qk_ready", l, h + 1))
                    for t in range(PT_):
                        if h and t == 0 and l:
                            pe.wait_ge(S("state_half"), count_at("state_half", l, h))
                        elif h:
                            pe.wait_ge(S("state_new"), count_at("state_new", l, h))
                        for lv in range(LEVELS):
                            last = score(lv, t, ps[:, 2 * t + lv // 4, (lv % 4) * P:(lv % 4 + 1) * P])
                        last.then_inc(S("score_ps"), 1)
                    if h:
                        pe.wait_ge(S("ms_ready"), count_at("ms_ready", l, h))
                    for lv in range(SL):
                        last = score(lv, PT_, ps[0:NS, 4, lv * NS:(lv + 1) * NS])
                    last.then_inc(S("score_ps"), 1)
                    pe.wait_ge(S("kd_ready"), count_at("kd_ready", l, h + 1))
                    if h:
                        pe.wait_ge(S("rms"), count_at("rms", l, h))
                    for t in range(TT):
                        last = tr(ps[0:ROWS[t], ktok_bank, t * P:(t + 1) * P], kd[:, cols(t)], ident)
                    last.then_inc(S("ktok_ps"), 1)
                    pe.wait_ge(S("ktok"), count_at("ktok", l, h + 1))
                    for t in range(PT_):
                        last = mm(ps[:, 7, t * nv:(t + 1) * nv], m["ktok"][:, t, :], m["v"][:, t, h * nv:(h + 1) * nv], start=True, stop=True)
                    last.then_inc(S("s_ps"), 1)
                    pe.wait_ge(S("qd_ready"), count_at("qd_ready", l, h + 1))
                    pe.wait_ge(S(f"s0_in{l}"), 16 + 32 * h)
                    for b in range(DB):
                        j, r = b % 4, b // 4
                        last = mm(ps[j * NS:(j + 1) * NS, 5 + l, r * nv:(r + 1) * nv], m["qd"][:, SEQ:NT], m["s0"][:, b, :], start=True, stop=True)
                    last.then_inc(S("so_ps"), 1)
                    pe.wait_ge(S("st_ready"), count_at("st_ready", l, TT * (h + 1)))
                    pe.wait_ge(S("s1_ready"), count_at("s1_ready", l, h + 1))
                    pe.wait_ge(S("so_ready"), count_at("so_ready", l, h + 1))
                    for c in range(dvc):
                        o = ps[:, o_bank[c], :]
                        vc = slice(h * nv + c * P, h * nv + (c + 1) * P)
                        mm(o[:, cols(0)], m["v"][:, 0, vc], m["st"][:, 0, :], start=True, stop=True)
                        mm(o[:, cols(1)], m["v"][:, 1, vc], m["st"][:, 1, :], start=True, stop=False)
                        mm(o[:, cols(1)], m["s1"][:, c * P:(c + 1) * P], m["qd"][:, cols(1)], start=False, stop=True)
                        mm(o[:, cols(2)], m["v"][0:NS, 2, vc], m["st"][0:NS, 2, 0:NS], start=True, stop=False)
                        for r in range(2):
                            last = mm(o[:, cols(2)], m["so"][:, r, c * P:(c + 1) * P], fold[:], start=False, stop=(r == 1))
                    last.then_inc(S("o_ps"), 1)
                    pe.wait_ge(S("kexp"), count_at("kexp", l, h + 1))
                    per = HALF // nv
                    for b in range(DB):
                        last = mm(ps[:, b // per, (b % per) * nv:(b % per + 1) * nv], m["kexp"][:, b, :],
                                  m["v"][0:NS, 2, h * nv:(h + 1) * nv], start=True, stop=True)
                        if b % 4 == 3:
                            last.then_inc(S("ns_ps"), 1)
                    pe.wait_ge(S("sq_ready"), count_at("sq_ready", l, h + 1))
                    for c in range(dvc):
                        last = mm(ps[:, 4, 0:NT], ones[:], m["sq"][:, c, :], start=(c == 0), stop=(c == dvc - 1))
                    last.then_inc(S("ss_ps"), 1)
                pe.wait_ge(S("rms"), count_at("rms", l, HEADS))

            def attention(l):
                def turn_keys(n, src):
                    for j in range(4):
                        if n:
                            pe.wait_ge(S(("kt_a", "kt_d")[j // 2]), count_at("kt_a", l, 2 * (n - 1) + j % 2 + 1))
                        for c in range(2):
                            for i in range(MT_):
                                last = tr(ps[:, j, (2 * c + i) * P:(2 * c + i + 1) * P], src[:, i, (2 * j + c) * P:(2 * j + c + 1) * P], ident)
                        last.then_inc(S("kt_full"), 1)

                pe.wait_ge(S("ln_done"), 3 * (3 * l) + TT)
                turn_keys(0, KV[2])
                run_jobs(("xt", 1 + 3 * l))
                run_jobs(("mq", l))

                def sample_scores(b):
                    pe.wait_ge(S("kt_a"), count_at("kt_a", l, 2 * (b + 2)))
                    pe.wait_ge(S("kt_d"), count_at("kt_d", l, 2 * (b + 2)))
                    if b >= 2:
                        pe.wait_ge(S("ssel"), count_at("ssel", l, b - 1))
                    for c in range(2):
                        for h in range(MH):
                            last = mm(ps[h * NS:(h + 1) * NS, 4 + b % 2, 0:MEM], QT[:, 2 * h + c, SEQ:NT],
                                      KT[b % 2][:, 2 * h + c, :], start=(c == 0), stop=(c == 1))
                    last.then_inc(S("ssc"), 1)

                for b in range(DB):
                    pe.wait_ge(S(f"kv_in{b % 3}"), 16 * (kv_loads(l, b)))
                    turn_keys(b + 1, KV[b % 3])
                    if b:
                        sample_scores(b - 1)
                sample_scores(DB - 1)
                pe.wait_ge(S("kt_a"), count_at("kt_a", l, 2 * (DB + 1)))
                pe.wait_ge(S("kt_d"), count_at("kt_d", l, 2 * (DB + 1)))

                def prompt_scores(t):
                    for h in range(MH):
                        for c in range(2):
                            last = mm(ps[:, 2 * t + h // 2, (h % 2) * MEM:(h % 2 + 1) * MEM], QT[:, 2 * h + c, cols(t)],
                                      KTP[:, 2 * h + c, :], start=(c == 0), stop=(c == 1))
                    last.then_inc(S("psc"), 1)

                prompt_scores(0)
                prompt_scores(1)
                pe.wait_ge(S("sp_ready"), count_at("sp_ready", l, 1))
                for i in range(MT_):
                    last = tr(ps[:, 4, i * P:(i + 1) * P], SS[:, i * P:(i + 1) * P], ident)
                last.then_inc(S("spt_ps"), 1)
                pe.wait_ge(S("spt_sb"), count_at("spt_sb", l, 1))

                def sample_values(b):
                    i = DB + b
                    pe.wait_ge(S(f"kv_in{i % 3}"), 16 * kv_loads(l, i))
                    if b >= 2:
                        pe.wait_ge(S("osel"), count_at("osel", l, b - 1))
                    for i2 in range(MT_):
                        for h in range(MH):
                            last = mm(ps[h * NS:(h + 1) * NS, 5 - b % 2, 0:MHD], SST[:, i2, h * NS:(h + 1) * NS],
                                      KV[i % 3][:, i2, h * MHD:(h + 1) * MHD], start=(i2 == 0), stop=(i2 == MT_ - 1))
                    last.then_inc(S("pv_done"), 1)

                def prompt_values(t):
                    pe.wait_ge(S("pr_ready"), count_at("pr_ready", l, t + 1))
                    for i in range(MT_):
                        for h in range(MH):
                            last = tr(ps[:, 6 + i, h * P:(h + 1) * P], PR[:, h, i * P:(i + 1) * P], ident)
                    last.then_inc(S("prt_ps"), 1)
                    pe.wait_ge(S("prt_sb"), count_at("prt_sb", l, t + 1))
                    for k in range(KC):
                        for i in range(MT_):
                            last = mm(ps[:, 2 * t + k // 4, (k % 4) * P:(k % 4 + 1) * P], VP[:, i, k * P:(k + 1) * P],
                                      PRT[:, i, (k // 2) * P:(k // 2 + 1) * P], start=(i == 0), stop=(i == MT_ - 1))
                    last.then_inc(S("po_ps"), 1)

                prompt_values(0)
                for b in range(3):
                    sample_values(b)
                prompt_values(1)
                for b in range(3, DB):
                    sample_values(b)
                pe.wait_ge(S("osel"), count_at("osel", l, DB))
                for c in range(2):
                    last = tr(ps[:, 6, c * P:(c + 1) * P], SS[:, c * P:(c + 1) * P], ident)
                last.then_inc(S("os_ps"), 1)
                pe.wait_ge(S("oa_ready"), count_at("oa_ready", l, 3))

            def moe(l):
                pe.wait_ge(S("router_in"), 16 * (GROUPS + 3) * (l + 1))
                for t in range(TT):
                    for k in range(KC):
                        last = mm(ps[0:ROWS[t], 0, t * 64:t * 64 + GROUPS + NE], XT[:, k, cols(t)], router_w[:, k, :],
                                  start=(k == 0), stop=(k == KC - 1))
                last.then_inc(S("logits"), 1)
                pe.wait_ge(S("assigned"), count_at("assigned", l, 1))
                for t in range(TT):
                    for u in range(t + 1):
                        last = mm(ps[:, 1, t * NE:(t + 1) * NE], upper[:] if u == t else ones[:], ASG[:, u, :],
                                  start=(u == 0), stop=(u == t))
                for u in range(TT):
                    last = mm(ps[:, 1, TT * NE:(TT + 1) * NE], ones[:], ASG[:, u, :], start=(u == 0), stop=(u == TT - 1))
                last.then_inc(S("ranks"), 1)
                pe.wait_ge(S("rounds_known"), count_at("rounds_known", l, 1))
                rm1 = pe.value_load(rounds[0:1, 0:1], min_val=0, max_val=4)

                def scatter(it, part):
                    for n in part:
                        t, j = n // 2, n % 2
                        if n >= 2:
                            pe.wait_ge(S(f"acc{l}"), it * SCATTERS + (n - 1))
                        if t < PT_:
                            last = mm(ps[:, 7 - n % 2, :], PWT[:, cols(t)], Y[:, j * HALF:(j + 1) * HALF], start=True, stop=True)
                        else:
                            for q in range(4):
                                last = mm(ps[q * NS:(q + 1) * NS, 7 - n % 2, 0:D // 4], PWT[:, cols(t)],
                                          Y[:, q * (D // 4):(q + 1) * (D // 4)], start=True, stop=True)
                        last.then_inc(S(f"scat{l}"), 1)

                def gather(it):
                    pe.wait_ge(S(f"pg_part{l}"), it * TT + TT)
                    for k in range(KC):
                        for t in range(TT):
                            last = mm(ps[:, k // 4, (k % 4) * P:(k % 4 + 1) * P], X[0:ROWS[t], t, k * P:(k + 1) * P],
                                      PG[0:ROWS[t], t, :, :].rearrange("p j c -> p (j c)"), start=(t == 0), stop=(t == TT - 1))
                        if k == 3:
                            last.then_inc(S(f"xg_ps0{l}"), 1)
                    last.then_inc(S(f"xg_ps1{l}"), 1)

                gather(0)
                def both_experts(bank, weights, x, n):
                    w = [weights[:, j, :].rearrange("p (k n) -> p k n", k=x.shape[1]) for j in range(2)]
                    for k in range(x.shape[1]):
                        for j in range(2):
                            last = mm(ps[j * CAP:(j + 1) * CAP, bank, :], x[:, k, j * CAP:(j + 1) * CAP],
                                      w[j][:, k, n * HALF:(n + 1) * HALF], start=(k == 0), stop=(k == x.shape[1] - 1))
                    return last

                with pe.Fori(0, rm1 + 1) as rd:
                    with pe.Fori(0, PAIRS // 2) as pp:
                        for odd in range(2):
                            it = rd * PAIRS + (pp * 2 + odd)
                            pe.wait_ge(S(f"xg_a{l}"), it + 1)
                            pe.wait_ge(S(f"xg_d{l}"), it + 1)
                            pe.wait_ge(S(f"ht{l}"), it + 1)
                            pe.wait_ge(S(f"gate{odd}_in{l}"), (rd * (PAIRS // 2) + pp) * 32 + 32)
                            both_experts(2, EXPERT["gate", odd], XG, 0).then_inc(S(f"gate_done{l}"), 1)
                            gather(it + 1)
                            pe.wait_ge(S(f"h_ready{l}"), it + 1)
                            pe.wait_ge(S(f"up0_in{l}"), it * 32 + 32)
                            both_experts(3, EXPERT["up", 0], XG, 0).then_inc(S(f"up_done{l}"), 1)
                            pe.wait_ge(S(f"y_sb{l}"), it + 1)
                            pe.wait_ge(S(f"pwt_sb{l}"), it + 1)
                            scatter(it, range(0, 3))
                            pe.wait_ge(S(f"h_ready{l}"), it + 2)
                            for f in range(DE // P):
                                last = tr(ps[:, 2, f * P:(f + 1) * P], HS[:, f * P:(f + 1) * P], ident)
                            last.then_inc(S(f"ht_ps{l}"), 1)
                            scatter(it, range(3, SCATTERS))
                            pe.wait_ge(S(f"acc{l}"), it * SCATTERS + SCATTERS)
                            pe.wait_ge(S(f"pw_part{l}"), it * TT + TT)
                            for t in range(TT):
                                last = tr(ps[:, 6, cols(t)], PW[0:ROWS[t], t, :, :].rearrange("p j c -> p (j c)"), ident[0:ROWS[t], 0:ROWS[t]])
                            last.then_inc(S(f"pwt_ps{l}"), 1)
                            pe.wait_ge(S(f"ht{l}"), it + 2)
                            pe.wait_ge(S(f"down0_in{l}"), it * 32 + 32)
                            both_experts(4, EXPERT["down", 0], HT, 0)
                            both_experts(5, EXPERT["down", 0], HT, 1).then_inc(S(f"down_done{l}"), 1)
                pe.wait_ge(S(f"y_sb{l}"), rm1 * PAIRS + (PAIRS + 1))
                pe.wait_ge(S(f"pwt_sb{l}"), rm1 * PAIRS + (PAIRS + 1))
                scatter(rm1 * PAIRS + PAIRS, range(SCATTERS))
                pe.wait_ge(S(f"acc{l}"), rm1 * (PAIRS * SCATTERS) + (PAIRS + 1) * SCATTERS)

            pe.wait_ge(S("consts"), 1)
            mm(ps[:, 0, 0:P], ones[:], upper[:], start=True, stop=True).then_inc(S("iota_ps"), 1)
            run_jobs(("xt", 0))
            for l in range(DEPTH):
                if l == 0:
                    run_jobs(("in", l), part(("in", l), upto="bg"))
                    pe.wait_ge(S("iota_ready"), 1)
                    pe.wait_ge(S("conv_in"), 16)
                    for c in range(CW // P):
                        last = tr(ps[:, 0, c * 16:(c + 1) * 16], conv_in[:, c * P:(c + 1) * P], ident[0:2 * DB, 0:2 * DB])
                    last.then_inc(S("conv_ps"), 1)
                    run_jobs(("in", l), part(("in", l), after="bg", upto="f"))
                    pe.wait_ge(S("conv_u"), 1)
                    for c in range(CW // P):
                        last = tr(ps[0:2 + 2 * DB, 1, c * P:(c + 1) * P], conv_tail[:, c, :], ident)
                    last.then_inc(S("conv_ps"), 1)
                    run_jobs(("in", l), part(("in", l), after="f"))
                    pe.wait_ge(S("conv_out"), 1)
                else:
                    run_jobs(("in", l))
                mixer(l)
                project_out(l, MIX[l]["o"], "out", 1 + 3 * l)
                run_jobs(("mem", l))
                attention(l)
                project_out(l, OA, "mo", 2 + 3 * l)
                run_jobs(("xt", 2 + 3 * l))
                moe(l)
                if l + 1 < DEPTH:
                    run_jobs(("xt", 3 + 3 * l))

        @block.scalar
        def _(act):
            st = Steps(act, S("act_step"))
            fn = act.activation

            def fetch_table(function):
                st.step(fn(small[0:1, 15, 3:4], ones[0:1, 0:1], function))

            def load_gb(inst):
                l, n = (inst - 1) // 3, (inst - 1) % 3
                if inst > 1:
                    act.wait_ge(S("ln_done"), 3 * (inst - 1))
                act.dma_start(GB[:, 0, :], I["ln_g"][l, n].partition_broadcast(P)).then_inc(S("gb_in"), 16)
                act.dma_start(GB[:, 1, :], I["ln_b"][l, n].partition_broadcast(P)).then_inc(S("gb_in"), 16)

            def empty_jobs(stage, some=None):
                for n, (kind, name, c) in some or jobs[stage]:
                    act.wait_ge(S("pipe_full"), n + 1)
                    bank = ps[:, 6 + n % 2, :]
                    l = stage[1]
                    m = MIX[l] if l < 2 else None
                    full = bank[:, 0:NT]
                    if kind == "xt":
                        src = bank.rearrange("p (k t) -> p k t", k=4)[:, :, 0:ROWS[name]]
                        ins = fn(XT[:, 4 * c:4 * c + 4, cols(name)], src, ACT.Copy)
                    elif kind == "feat" and name[:2] == "mq":
                        ins = fn(QT[:, 4 * int(name[2]) + c, :], full, ACT.Copy, scale=float(MHD) ** -0.5)
                    elif kind == "feat" and name in ("bg", "cg", "h"):
                        ins = fn(m["conv"][("bg", "cg", "h").index(name)][:, c, :], full, ACT.Copy)
                    elif kind == "feat" and name == "f":
                        ins = fn(m["b"][:, c, :], full, ACT.Copy)
                    elif kind == "feat" and name == "q" and l == 0:
                        ins = fn(m["q"][:, c, :], full, ACT.Silu)
                    elif kind == "feat" and name == "q":
                        ins = fn(m["q"][:, c, :], full, ACT.Copy, scale=float(DK) ** -0.5)
                    elif kind == "feat" and name == "k":
                        ins = fn(m["k"][:, c, :], full, ACT.Copy)
                    elif kind == "feat":
                        ins = fn(m["g"][:, 4 * (name == "g1") + c, :], full, ACT.Silu)
                    elif kind == "gz":
                        ins = fn(gz[:], bank[0:RANK, 0:NT], ACT.Copy)
                    elif kind == "gk":
                        ins = fn(m["b"][:, c, :], full, ACT.Identity, bias=bgk2[:, c:c + 1])
                    elif kind == "tok":
                        at = HALF * (name == "v1")
                        if c < PT_:
                            ins = fn(m["v"][:, c, at:at + HALF], bank, ACT.Copy)
                        else:
                            for q in range(4):
                                ins = fn(m["v"][0:NS, c, at + q * P:at + (q + 1) * P], bank[q * NS:(q + 1) * NS, 0:P], ACT.Copy)
                    elif kind == "mt":
                        memT = KV[1].rearrange("p i d -> p (i d)").rearrange("p (k m) -> p k m", k=KC)
                        ins = fn(memT[:, 4 * c:4 * c + 4, name * P:(name + 1) * P], bank.rearrange("p (k t) -> p k t", k=4), ACT.Copy)
                    elif kind == "memtok":
                        at = HALF * int(name[2])
                        dst = KV[2] if name[:2] == "mk" else VP
                        ins = fn(dst[:, c, at:at + HALF], bank, ACT.Copy)
                    ins.then_inc(S("pipe_free"), 1)

            def mixer(l):
                m, dvc = MIX[l], DVC[l]
                z, tmp = m["b"], m["tmp"]
                stage = ("in", l)
                empty_jobs(stage, part(stage, upto=GATES[l]))
                act.wait_ge(S("pipe_free"), number(stage, GATES[l]))
                st.step(fn(tmp, z, ACT.Abs))
                st.step(fn(tmp, tmp, ACT.Exp, scale=-1.0))
                st.tell(fn(tmp, tmp, ACT.Ln, bias=1.0), S("softplus"))
                if l == 0:
                    empty_jobs(stage, part(stage, after="f", upto="q"))
                    act.wait_ge(S("amz_ready"), 1)
                    st.tell(fn(m["k"], m["k"], ACT.Exp), S("k_ready"))
                def decays(h):
                    qk, kd, dec = m["qk"][h % 2], m["kd"][h % 2], m["dec"][h % 2]
                    act.wait_ge(S("e_ready"), count_at("e_ready", l, h + 1))
                    fn(kd, kd, ACT.Exp)
                    fn(qk[:, 0:SL - 1, :], qk[:, 0:SL - 1, :], ACT.Exp)
                    fn(dec, dec, ACT.Exp)
                    st.tell(fn(qk[:, SL - 1:, 0:SEQ], qk[:, SL - 1:, 0:SEQ], ACT.Exp), S("ex_ready"))

                def query_decays(h):
                    st.tell(fn(m["qd"], m["b"][:, h, :], ACT.Exp), S("qd_exp"))

                empty_jobs(stage, part(stage, after=QUERIES[l], upto="g"))
                decays(0)
                query_decays(0)
                empty_jobs(stage, part(stage, after="g"))
                for h in range(HEADS):
                    act.wait_ge(S("ktok_ps"), count_at("ktok_ps", l, h + 1))
                    fn(m["ktok"][:, 0:PT_, :], ps[:, 6 - l, 0:PT_ * P].rearrange("p (t c) -> p t c", t=PT_), ACT.Copy)
                    st.tell(fn(m["ktok"][0:NS, PT_, :], ps[0:NS, 6 - l, PT_ * P:(PT_ + 1) * P], ACT.Copy), S("ktok"))
                    act.wait_ge(S("s_ps"), count_at("s_ps", l, h + 1))
                    st.tell(fn(m["s1"], ps[:, 7, 0:dvc * P], ACT.Copy), S("s1_ready"))
                    act.wait_ge(S("so_ps"), count_at("so_ps", l, h + 1))
                    for r in range(2):
                        ins = fn(m["so"][:, r, :], ps[:, 5 + l, r * dvc * P:(r + 1) * dvc * P], ACT.Copy, scale=own[:, r:r + 1])
                    st.tell(ins, S("so_ready"))
                    if h + 1 < HEADS:
                        decays(h + 1)
                    act.wait_ge(S("o_ps"), count_at("o_ps", l, h + 1))
                    for c in range(dvc):
                        ins = fn(m["sq"][:, c, :], ps[:, 5 + c, 0:NT], ACT.Square)
                    st.tell(ins, S("sq_ready"))
                    if h + 1 < HEADS:
                        query_decays(h + 1)
                    else:
                        act.wait_ge(S("state_new"), count_at("state_new", l, HEADS - 1))
                        load_gb(1 + 3 * l)
                    fetch_table(ACT.Sqrt)
                    act.wait_ge(S("ms_ready"), count_at("ms_ready", l, h + 1))
                    st.tell(fn(m["rs"], m["rs"], ACT.Sqrt), S("root"))
                    fetch_table(ACT.Exp)

            def norm(inst, tiles=range(TT)):
                fetch_table(ACT.Sqrt)
                for n in tiles:
                    t = ORDER[n]
                    act.wait_ge(S("var_ready"), 3 * (inst - 1) + n + 1)
                    st.tell(fn(mv[0:ROWS[t], 2:3], mv[0:ROWS[t], 2:3], ACT.Sqrt), S("std_ready"))

            def attention(l):
                def keys(n, dst):
                    for j in range(2):
                        act.wait_ge(S("kt_full"), count_at("kt_full", l, 4 * n + j + 1))
                        st.tell(fn(dst[:, 2 * j:2 * j + 2, :].rearrange("p c m -> p (c m)"), ps[:, j, :], ACT.Copy), S("kt_a"))

                keys(0, KTP)
                empty_jobs(("xt", 1 + 3 * l))
                load_gb(2 + 3 * l)
                empty_jobs(("mq", l))
                for b in range(DB):
                    if b >= 2:
                        act.wait_ge(S("ssc"), count_at("ssc", l, b - 1))
                    keys(b + 1, KT[b % 2])
                act.wait_ge(S("smax"), count_at("smax", l, 1))
                st.tell(fn(SS, SS, ACT.Exp, bias=small[:, 0, 0:1], accum_out=small[:, 1, 0:1]), S("sexp"))
                act.wait_ge(S("spt_ps"), count_at("spt_ps", l, 1))
                st.tell(fn(SST.rearrange("p i c -> p (i c)"), ps[:, 4, 0:MEM], ACT.Copy), S("spt_sb"))
                for t in range(PT_):
                    act.wait_ge(S("pmax"), count_at("pmax", l, t + 1))
                    for h in range(MH):
                        ins = fn(PR[:, h, :], ps[:, 2 * t + h // 2, (h % 2) * MEM:(h % 2 + 1) * MEM], ACT.Exp,
                                 bias=small[:, 2, h:h + 1], accum_out=small[:, 3, h:h + 1])
                        if h < MH - 1:
                            st.step(ins)
                    st.tell(ins, S("pexp"))
                    act.wait_ge(S("prt_ps"), count_at("prt_ps", l, t + 1))
                    st.step(fn(PRT[:, 0, :], ps[:, 6, :], ACT.Copy))
                    st.tell(fn(PRT[:, 1, :], ps[:, 7, :], ACT.Copy), S("prt_sb"))
                    act.wait_ge(S("po_ps"), count_at("po_ps", l, t + 1))
                    st.step(fn(OA[:, 0:4, cols(t)], ps[:, 2 * t, :].rearrange("p (k t) -> p k t", k=4), ACT.Copy))
                    st.tell(fn(OA[:, 4:8, cols(t)], ps[:, 2 * t + 1, :].rearrange("p (k t) -> p k t", k=4), ACT.Copy), S("oa_ready"))
                act.wait_ge(S("os_ps"), count_at("os_ps", l, 1))
                for c in range(2):
                    dst = OA[:, :, SEQ:NT].rearrange("p (h c) n -> p h c n", c=2)[:, :, c, :]
                    ins = fn(dst, ps[:, 6, c * P:(c + 1) * P].rearrange("p (h n) -> p h n", h=MH), ACT.Copy)
                    if c == 0:
                        st.step(ins)
                st.tell(ins, S("oa_ready"))

            def moe(l):
                act.wait_ge(S("gdiff"), count_at("gdiff", l, 1))
                st.step(fn(GE, GE, ACT.Exp))
                st.tell(fn(small[:, 6, 0:TT], small[:, 6, 0:TT], ACT.Exp), S("gexp"))
                act.wait_ge(S("rounds_known"), count_at("rounds_known", l, 1))
                rm1 = act.value_load(rounds[0:1, 0:1], min_val=0, max_val=4)
                def move_gathered(it):
                    act.wait_ge(S(f"xg_ps0{l}"), it + 1)
                    fn(XG[:, 0:4, :].rearrange("p k c -> p (k c)"), ps[:, 0, :], ACT.Copy).then_inc(S(f"xg_a{l}"), 1)

                move_gathered(0)
                with act.Fori(0, rm1 + 1) as rd:
                    with act.Fori(0, PAIRS) as p:
                        it = rd * PAIRS + p
                        act.wait_ge(S(f"gate_done{l}"), it + 1)
                        act.wait_ge(S(f"h_ready{l}"), it + 1)
                        fn(SG, ps[:, 2, :], ACT.Silu).then_inc(S(f"sg{l}"), 1)
                        act.wait_ge(S(f"up_done{l}"), it + 1)
                        move_gathered(it + 1)
                        act.wait_ge(S(f"ht_ps{l}"), it + 1)
                        fn(HT.rearrange("p f c -> p (f c)"), ps[:, 2, :], ACT.Copy).then_inc(S(f"ht{l}"), 1)
                        act.wait_ge(S(f"pwt_ps{l}"), it + 2)
                        fn(PWT, ps[:, 6, 0:NT], ACT.Copy).then_inc(S(f"pwt_sb{l}"), 1)
                        act.wait_ge(S(f"down_done{l}"), it + 1)
                        fn(Y, ps[:, 4:6, :].rearrange("p j n -> p (j n)"), ACT.Copy).then_inc(S(f"y_sb{l}"), 1)

            empty_jobs(("xt", 0))
            for l in range(DEPTH):
                mixer(l)
                norm(1 + 3 * l, range(PT_))
                empty_jobs(("mem", l), part(("mem", l), upto="mk0"))
                norm(1 + 3 * l, range(PT_, TT))
                empty_jobs(("mem", l), part(("mem", l), after="mk0"))
                attention(l)
                norm(2 + 3 * l)
                empty_jobs(("xt", 2 + 3 * l))
                load_gb(3 + 3 * l)
                moe(l)
                norm(3 + 3 * l)
                if l + 1 < DEPTH:
                    empty_jobs(("xt", 3 + 3 * l))

        @block.vector
        def _(dve):
            st = Steps(dve, S("dve_step"))
            step, tell = st.step, st.tell
            tt, ts, stt, cp, red = (dve.tensor_tensor, dve.tensor_scalar, dve.scalar_tensor_tensor,
                                    dve.tensor_copy, dve.tensor_reduce)

            def bc(ap, *shape):
                return ap.to_broadcast(list(shape))

            def conv(m):
                bg, cg, hh = m["conv"]
                up, us, C = m["up"], m["us"], CW // P
                dve.wait_ge(S("pipe_free"), number(("in", 0), "h"))
                sample = lambda x: x[:, :, SEQ:].rearrange("p c (b t) -> p c b t", b=DB)
                dve.memset(up[:, :, 0:2], 0.0)
                dve.wait_ge(S("conv_ps"), 1)
                step(tt(up[:, :, 2:], cg[:, :, 0:SEQ], hh[:, :, 0:SEQ], ALU.mult))
                for c in range(C):
                    tt(us[:, c, :, 2:], sample(cg)[:, c], sample(hh)[:, c], ALU.mult)
                    ins = cp(us[:, c, :, 0:2], ps[:, 0, c * 16:(c + 1) * 16].rearrange("p (b j) -> p b j", b=DB))
                step(ins)
                cp(conv_tail[:, :, 0:2], up[:, :, SEQ:SEQ + 2])
                for c in range(C):
                    ins = cp(conv_tail[:, c, 2:].rearrange("p (b j) -> p b j", b=DB), us[:, c, :, DS:DS + 2])
                tell(ins, S("conv_u"))
                dve.wait_ge(S("small_in"), 16 * 6)
                outs = m["o"][:, HEADS:HEADS + C, :]
                for j in range(3):
                    for c in range(C):
                        w = convw[:, c, j:j + 1]
                        for y, u in ((outs[:, c, 0:SEQ], up[:, c, j:j + SEQ]), (sample(outs)[:, c], us[:, c, :, j:j + DS])):
                            ins = stt(y, u, w, y, ALU.mult, ALU.add) if j else ts(y, u, w, None, ALU.mult)
                    step(ins)
                step(tt(outs, outs, bg, ALU.mult))
                dve.wait_ge(S("conv_ps"), 2)
                tell(cp(conv_tok, ps[0:2 + 2 * DB, 1, :]), S("conv_out"))

            def mixer(l):
                m, dvc = MIX[l], DVC[l]
                nv = dvc * P
                dv = nv
                if l == 0:
                    conv(m)
                z = m["b"]
                dve.wait_ge(S("softplus"), count_at("softplus", l, 1))
                zf, tf = (x.rearrange("p h t -> p (h t)") for x in (z, m["tmp"]))
                a = m["tmp"]
                step(stt(tf, zf, 0.0, tf, ALU.min, ALU.subtract))
                if l == 0:
                    tell(tt(m["k"].rearrange("p h t -> p (h t)"), tf, zf, ALU.subtract), S("amz_ready"))
                else:
                    step(ts(tf, tf, 1.0 / 16.0, None, ALU.mult))
                for h in range(HEADS):
                    dve.tensor_tensor_scan(m["b"][:, h, :], carry[:], a[:, h, :], 0.0, ALU.mult, ALU.add).then_inc(S("b_ready"), 1)

                def decayed(h):
                    q, k, qk, kd = m["q"][:, h, :], m["k"][:, h, :], m["qk"][h % 2], m["kd"][h % 2]
                    dve.wait_ge(S("ex_ready"), count_at("ex_ready", l, h + 1))
                    tt(kd, kd, k, ALU.mult).then_inc(S("kd_ready"), 1)
                    for lv in range(1, LEVELS):
                        upto = NT if lv < SL else SEQ
                        (el, er), (kl, _), (_, qr) = halves(qk[:, lv - 1, :], lv, upto), halves(k, lv, upto), halves(q, lv, upto)
                        tt(el, el, kl, ALU.mult)
                        ins = tt(er, er, qr, ALU.mult)
                    tell(ins, S("qk_ready"))

                if l == 0:
                    dve.wait_ge(S("k_ready"), 1)
                decayed(0)
                dve.wait_ge(S("pipe_free"), number(("in", l)))
                for h in range(HEADS):
                    dec, s0 = m["dec"][h % 2], m["s0"]
                    dve.wait_ge(S("qd_exp"), count_at("qd_exp", l, h + 1))
                    tell(tt(m["qd"], m["qd"], m["q"][:, h, :], ALU.mult), S("qd_ready"))
                    for t in range(TT):
                        R, L, C = ROWS[t], (LEVELS if t < PT_ else SL), ROWS[t]
                        dve.wait_ge(S("score_ps"), count_at("score_ps", l, TT * h + t + 1))
                        if t < PT_:
                            src = ps[:, 2 * t:2 * t + 2, :].rearrange("p a (b c) -> p (a b) c", c=P)
                        else:
                            src = ps[0:NS, 4, 0:SL * NS].rearrange("p (a c) -> p a c", a=SL)
                        ms = m["ms"][0:R, 0:L, 0:C]
                        step(tt(ms, src, masks[0:R, 0:L, 0:C], ALU.mult))
                        tell(red(m["st"][0:R, t, 0:C], ms.rearrange("p l t -> p t l"), AX.X, ALU.add), S("st_ready"))
                    if h + 1 < HEADS:
                        decayed(h + 1)
                    if h:
                        dve.wait_ge(S("state_out"), count_at("state_out", l, 32 * h))
                    dve.wait_ge(S("s_ps"), count_at("s_ps", l, h + 1))
                    dve.wait_ge(S("s1_ready"), count_at("s1_ready", l, h + 1))
                    step(stt(m["sf"], m["s1"], dec[:, 1:2], ps[:, 7, nv:2 * nv], ALU.mult, ALU.add))
                    dve.wait_ge(S("o_ps"), count_at("o_ps", l, h + 1))
                    new = ps[:, 0:DB * nv // HALF, :].rearrange("p a (b v) -> p (a b) v", v=nv)
                    for b in range(DB):
                        if b % 4 == 0:
                            dve.wait_ge(S("ns_ps"), count_at("ns_ps", l, 2 * h + b // 4 + 1))
                        ins = stt(s0[:, b, :], s0[:, b, :], dec[:, PT_ + b:PT_ + b + 1], new[:, b, :], ALU.mult, ALU.add)
                        if b == 3:
                            ins.then_inc(S("state_half"), 1)
                    tell(ins, S("state_new"))
                    dve.wait_ge(S("ss_ps"), count_at("ss_ps", l, h + 1))
                    tell(ts(m["rs"], ps[:, 4, 0:NT], 1.0 / dv, RMS_EPS, ALU.mult, ALU.add), S("ms_ready"))
                    dve.wait_ge(S("root"), count_at("root", l, h + 1))
                    step(dve.reciprocal(m["rs"], m["rs"]))
                    for c in range(dvc):
                        o = m["o"][:, h * dvc + c, :]
                        step(stt(o, ps[:, 5 + c, 0:NT], gnorm[l][:, c:c + 1], m["rs"], ALU.mult, ALU.mult))
                        ins = tt(o, o, m["g"][:, h * dvc + c, :], ALU.mult)
                        if c < dvc - 1:
                            step(ins)
                    tell(ins, S("rms"))

            def norm(inst, src=None):
                dve.wait_ge(S("gb_in"), 32 * inst)
                i = 2 * ((inst - 1) // 3) + ((inst - 1) % 3)
                for n, t in enumerate(ORDER):
                    R = ROWS[t]
                    x = X[0:R, t, :]
                    if src is not None:
                        step(stt(x, x, ALPHA, src[0:R, t, :], ALU.mult, ALU.add))
                    elif t < PT_:
                        if t == 0:
                            dve.wait_ge(S("mix_done"), i + 1)
                        else:
                            dve.wait_ge(S("mix_unit"), 2 * i + 2)
                        step(stt(x, x, ALPHA, ps[:, 2 * t:2 * t + 2, :].rearrange("p a n -> p (a n)"), ALU.mult, ALU.add))
                    else:
                        dve.wait_ge(S("mix_unit"), 2 * i + 1)
                        for q in range(4):
                            xq = x[:, q * (D // 4):(q + 1) * (D // 4)]
                            ins = stt(xq, xq, ALPHA, ps[q * NS:(q + 1) * NS, 4, 0:D // 4], ALU.mult, ALU.add)
                        step(ins)
                    for j in range(2):
                        ins = dve.bn_stats(stat[0:R, j, :], x[:, j * HALF:(j + 1) * HALF])
                    step(ins)
                    step(dve.bn_aggr(mv[0:R, 0:2], stat[0:R].rearrange("p a b -> p (a b)")))
                    ts(mv[0:R, 2:3], mv[0:R, 1:2], LN_EPS, None, ALU.add).then_inc(S("var_ready"), 1)
                    step(stt(x, x, mv[0:R, 0:1], GB[0:R, 0, :], ALU.subtract, ALU.mult))
                    dve.wait_ge(S("std_ready"), 3 * (inst - 1) + n + 1)
                    step(dve.reciprocal(mv[0:R, 3:4], mv[0:R, 2:3]))
                    tell(stt(x, x, mv[0:R, 3:4], GB[0:R, 1, :], ALU.mult, ALU.add), S("ln_done"))

            def attention(l):
                def keys(n, dst):
                    for j in (2, 3):
                        dve.wait_ge(S("kt_full"), count_at("kt_full", l, 4 * n + j + 1))
                        tell(cp(dst[:, 2 * j:2 * j + 2, :].rearrange("p c m -> p (c m)"), ps[:, j, :]), S("kt_d"))

                def select(b, bank, sem):
                    x, mine = ps[:, bank, 0:MEM], bmask[:, b:b + 1]
                    tell(stt(SS, x, mine, SS, ALU.mult, ALU.add) if b else ts(SS, x, mine, None, ALU.mult), S(sem))

                keys(0, KTP)
                for b in range(DB):
                    if b >= 2:
                        dve.wait_ge(S("ssc"), count_at("ssc", l, b - 1))
                    keys(b + 1, KT[b % 2])
                    if b:
                        dve.wait_ge(S("ssc"), count_at("ssc", l, b))
                        select(b - 1, 4 + (b - 1) % 2, "ssel")
                dve.wait_ge(S("ssc"), count_at("ssc", l, DB))
                select(DB - 1, 4 + (DB - 1) % 2, "ssel")
                step(red(small[:, 0, 1:2], SS, AX.X, ALU.max))
                tell(ts(small[:, 0, 0:1], small[:, 0, 1:2], -1.0, None, ALU.mult), S("smax"))
                dve.wait_ge(S("sexp"), count_at("sexp", l, 1))
                step(dve.reciprocal(small[:, 1, 1:2], small[:, 1, 0:1]))
                tell(ts(SS, SS, small[:, 1, 1:2], None, ALU.mult), S("sp_ready"))
                for t in range(PT_):
                    dve.wait_ge(S("psc"), count_at("psc", l, t + 1))
                    step(red(small[:, 4, 0:MH], ps[:, 2 * t:2 * t + 2, :].rearrange("p a (b m) -> p (a b) m", m=MEM), AX.X, ALU.max))
                    tell(ts(small[:, 2, 0:MH], small[:, 4, 0:MH], -1.0, None, ALU.mult), S("pmax"))
                    dve.wait_ge(S("pexp"), count_at("pexp", l, t + 1))
                    step(dve.reciprocal(small[:, 5, 0:MH], small[:, 3, 0:MH]))
                    tell(tt(PR, PR, bc(small[:, 5, 0:MH].unsqueeze(2), P, MH, MEM), ALU.mult), S("pr_ready"))
                dve.wait_ge(S("spt_ps"), count_at("spt_ps", l, 1))
                for b in range(DB):
                    dve.wait_ge(S("pv_done"), count_at("pv_done", l, b + 1))
                    select(b, 5 - b % 2, "osel")

            def one_hot(dst, src, mx, n):
                step(red(mx, src, AX.X, ALU.max))
                step(tt(dst, src, bc(mx.unsqueeze(2), P, TT, n), ALU.is_equal))
                step(tt(dst, dst, bc(rev[:, 0:n].unsqueeze(1), P, TT, n), ALU.mult))
                step(red(small[:, 15, 0:TT], dst, AX.X, ALU.max))
                step(tt(dst, dst, bc(small[:, 15, 0:TT].unsqueeze(2), P, TT, n), ALU.is_equal))

            def moe(l):
                gm, m1, m2, dif, gw, w1, w2 = (small[:, n, 0:TT] for n in (4, 5, 7, 6, 8, 9, 10))
                dve.wait_ge(S("memv_out"), 16 * (l + 1))
                dve.wait_ge(S("router_in"), 16 * (GROUPS + 3) * (l + 1))
                step(dve.memset(LG, 0.0))
                dve.wait_ge(S("logits"), count_at("logits", l, 1))
                for t in range(TT):
                    R = ROWS[t]
                    step(tt(LG[0:R, t, :], ps[0:R, 0, t * 64:t * 64 + GROUPS + NE], router_b[0:R, :], ALU.add))
                one_hot(OHG, LG[:, :, 0:GROUPS], gm, GROUPS)
                step(tt(GE, LG[:, :, 0:GROUPS], bc(gm.unsqueeze(2), P, TT, GROUPS), ALU.subtract))
                for t in range(TT):
                    step(tt(EM[:, t, :, :], LG[:, t, GROUPS:].rearrange("p (g e) -> p g e", g=GROUPS),
                            bc(OHG[:, t, :].unsqueeze(2), P, GROUPS, EPG), ALU.mult))
                    step(red(SEL[:, t, :], EM[:, t, :, :].rearrange("p g e -> p e g"), AX.X, ALU.add))
                one_hot(OH1, SEL, m1, EPG)
                flat = [x.rearrange("p t e -> p (t e)") for x in (SEL, OH1)]
                step(stt(flat[0], flat[1], -3.0e38, flat[0], ALU.mult, ALU.add))
                one_hot(OH2, SEL, m2, EPG)
                tell(tt(dif, m2, m1, ALU.subtract), S("gdiff"))
                dve.wait_ge(S("gexp"), count_at("gexp", l, 1))
                step(red(gw, GE, AX.X, ALU.add))
                step(ts(w1, dif, 1.0, None, ALU.add))
                step(tt(w1, w1, gw, ALU.mult))
                step(dve.reciprocal(w1, w1))
                step(tt(w2, w1, dif, ALU.mult))
                step(tt(AS8, OH1, OH2, ALU.add))
                step(tt(OH1, OH1, bc(w1.unsqueeze(2), P, TT, EPG), ALU.mult))
                step(tt(OH2, OH2, bc(w2.unsqueeze(2), P, TT, EPG), ALU.mult))
                step(tt(WE8, OH1, OH2, ALU.add))
                step(tt(OHG, OHG, bc(valid[:].unsqueeze(2), P, TT, GROUPS), ALU.mult))
                for t in range(TT):
                    og = bc(OHG[:, t, :].unsqueeze(2), P, GROUPS, EPG)
                    for dst, src in ((ASG, AS8), (CMB, WE8)):
                        step(tt(dst[:, t, :].rearrange("p (g e) -> p g e", g=GROUPS), og, bc(src[:, t:t + 1, :], P, GROUPS, EPG), ALU.mult))
                tell(dve.memset(small[:, 15, :], 0.0), S("assigned"))
                dve.wait_ge(S("ranks"), count_at("ranks", l, 1))
                step(red(small[:, 11, 0:1], ps[:, 1, TT * NE:(TT + 1) * NE], AX.X, ALU.max))
                step(ts(THR, iota[:, 1:1 + (NT - 1) // CAP], float(CAP), small[:, 11, 0:1], ALU.mult, ALU.is_lt))
                step(red(small[:, 12, 0:1], THR, AX.X, ALU.add))
                key = KEY.rearrange("p t e -> p (t e)")
                for t in range(TT):
                    step(stt(KEY[:, t, 0:NE], ps[:, 1, t * NE:(t + 1) * NE], 1.0, ASG[:, t, :], ALU.add, ALU.mult))
                step(ts(KEY[:, :, 0:NE], KEY[:, :, 0:NE], -1.0, None, ALU.add))
                step(ts(KEY[:, :, NE:], KEY[:, :, 0:2], -float(CAP), None, ALU.add))
                for n, free in enumerate(("xg_ps1", "pwt_ps", "ht", "h_ready")):
                    tell(dve.memset(small[:, 13, n:n + 1], 0.0), S(f"{free}{l}"))
                dve.wait_ge(S("zeros"), l + 1)
                tell(dve.memset(small[:, 13, 0:1], 0.0), S(f"pwt_sb{l}"))
                tell(dve.memset(small[:, 13, 1:2], 0.0), S(f"y_sb{l}"))
                tell(cp(rounds[:], small[0:1, 12, 0:1]), S("rounds_known"))
                rm1 = dve.value_load(rounds[0:1, 0:1], min_val=0, max_val=4)
                io = bc(iota[:, 0:CAP].unsqueeze(1), P, 2, CAP)

                def one_hots(e):
                    for t in range(TT):
                        k2 = KEY[:, t, e].unsqueeze(2)
                        tt(PG[:, t, :, :], io, bc(k2, P, 2, CAP), ALU.is_equal).then_inc(S(f"pg_part{l}"), 1)

                def move_gathered(it):
                    dve.wait_ge(S(f"xg_ps1{l}"), it + 2)
                    cp(XG[:, 4:8, :].rearrange("p k c -> p (k c)"), ps[:, 1, :]).then_inc(S(f"xg_d{l}"), 1)

                def add_scattered(n):
                    t, j, bank = n // 2, n % 2, 7 - n % 2
                    if t < PT_:
                        a = ACC[:, t, j * HALF:(j + 1) * HALF]
                        ins = tt(a, a, ps[:, bank, :], ALU.add)
                    else:
                        for q in range(4):
                            a = ACC[0:NS, t, q * (D // 4):(q + 1) * (D // 4)]
                            ins = tt(a, a, ps[q * NS:(q + 1) * NS, bank, 0:D // 4], ALU.add)
                    ins.then_inc(S(f"acc{l}"), 1)

                one_hots(slice(0, 2))
                move_gathered(0)
                with dve.Fori(0, rm1 + 1) as rd:
                    with dve.Fori(0, PAIRS) as p:
                        it = rd * PAIRS + p
                        dve.wait_ge(S(f"pg_part{l}"), it * TT + TT)
                        dve.wait_ge(S(f"pwt_ps{l}"), it + 1)
                        for t in range(TT):
                            w2e = CMB[:, t, bass.ds(p * 2, 2)].unsqueeze(2)
                            tt(PW[:, t, :, :], PG[:, t, :, :], bc(w2e, P, 2, CAP), ALU.mult).then_inc(S(f"pw_part{l}"), 1)
                        dve.wait_ge(S(f"pw_part{l}"), it * TT + TT)
                        dve.wait_ge(S(f"xg_ps1{l}"), it + 2)
                        one_hots(bass.ds(p * 2 + 2, 2))
                        dve.wait_ge(S(f"sg{l}"), it + 1)
                        dve.wait_ge(S(f"up_done{l}"), it + 1)
                        tt(HS, SG, ps[:, 3, :], ALU.mult).then_inc(S(f"h_ready{l}"), 1)
                        move_gathered(it + 1)
                        for n in range(SCATTERS):
                            dve.wait_ge(S(f"scat{l}"), it * SCATTERS + (n + 1))
                            add_scattered(n)
                    dve.wait_ge(S(f"pg_part{l}"), rd * (PAIRS * TT) + (PAIRS + 1) * TT)
                    ts(key, key, -float(CAP), None, ALU.add).then_inc(S(f"round_end{l}"), 1)
                    dve.wait_ge(S(f"round_end{l}"), rd + 1)
                for n in range(SCATTERS):
                    dve.wait_ge(S(f"scat{l}"), rm1 * (PAIRS * SCATTERS) + (PAIRS * SCATTERS + n + 1))
                    add_scattered(n)
                dve.wait_ge(S(f"acc{l}"), rm1 * (PAIRS * SCATTERS) + (PAIRS + 1) * SCATTERS)

            dve.wait_ge(S("iota_ps"), 1)
            step(cp(iota[:], ps[:, 0, 0:P]))
            tell(ts(rev[:], iota[:, 0:EPG], -1.0, float(EPG), ALU.mult, ALU.add), S("iota_ready"))
            dve.wait_ge(S("tables"), 1)
            for l in range(DEPTH):
                mixer(l)
                norm(1 + 3 * l)
                attention(l)
                norm(2 + 3 * l)
                moe(l)
                norm(3 + 3 * l, ACC)


_INS = ["x_prompt", "x_sample", "state_hgrn", "state_conv", "state_gla", "cache_mem_k", "cache_mem_v", "mem_prompt",
        "w_in_a", "lb_a", "conv_w", "gnorm_a", "w_out_a", "w_in_c", "w_gk2", "b_gk2", "gnorm_c", "w_out_c",
        "w_mq", "w_mk", "w_mv", "w_mo", "ln_g", "ln_b", "w_grp", "b_grp", "w_er", "b_er", "w_gate", "w_up", "w_down"]


def kernel(**inputs):
    import numpy as _np
    import concourse.bacc as _bacc
    from concourse.bass_utils import run_bass_kernel_spmd as _run

    nc = _bacc.Bacc("TRN2", target_bir_lowering=False, num_devices=1)
    arrays, I, O = {}, {}, {}
    for name in _INS:
        a = _np.ascontiguousarray(inputs[name])
        arrays[f"in_{name}"] = a
        I[name] = nc.dram_tensor(f"in_{name}", a.shape, mybir.dt.from_np(a.dtype), kind="ExternalInput").ap()
    like = {k: inputs[k].shape for k in _INS}
    depth, _, mem, mh, mhd = like["cache_mem_k"]
    outs = [
        ("y_prompt", like["x_prompt"]), ("y_sample", like["x_sample"]),
        ("hgrn_p", (like["state_hgrn"][0], 1) + tuple(like["state_hgrn"][2:])),
        ("conv_p", (like["state_conv"][0], 1) + tuple(like["state_conv"][2:])),
        ("gla_p", (like["state_gla"][0], 1) + tuple(like["state_gla"][2:])),
        ("mem_k", (depth, 1, mem, mh, mhd)), ("mem_v", (depth, 1, mem, mh, mhd)),
        ("hgrn_s", like["state_hgrn"]), ("conv_s", like["state_conv"]), ("gla_s", like["state_gla"]),
    ]
    for name, shape in outs:
        O[name] = nc.dram_tensor(f"out_{name}", tuple(shape), F32, kind="ExternalOutput").ap()
    build(nc, I, O)
    r = _run(nc, [arrays], core_ids=[0])
    return tuple(r.results[0][f"out_{name}"] for name, _ in outs)
```
